# Optimizing a Trainium2 kernel written in Bass

```python
import math
import jax, jax.numpy as jnp
from jax import lax
import numpy as np

D_MODEL = 1024
BATCH = 1
SEQ = 1024
DEPTH = 1

GLA_HEADS = 4
GLA_DK = 64
GLA_DV = 128
GLA_RANK = 16
GLA_TAU = 16.0
GLA_CHUNK = 16
DIFF_HEADS = 4
DIFF_DH = 64
DIFF_DV = 2 * DIFF_DH
Q_BLOCK = 128
ALIBI_MAX_BIAS = 8.0
D_FF = 2816
EPS = 1e-6
N_BRANCH = 2
N_MOD = 9

GLA_KW = GLA_HEADS * GLA_DK
GLA_VW = GLA_HEADS * GLA_DV
DIFF_QW = DIFF_HEADS * 2 * DIFF_DH
DIFF_VW = DIFF_HEADS * DIFF_DV
IN_SIZES = (GLA_KW, GLA_KW, GLA_VW, GLA_VW, GLA_RANK, DIFF_QW, DIFF_QW, DIFF_VW, N_BRANCH * D_MODEL)
IN_COLS = GLA_KW * 2 + GLA_VW * 2 + GLA_RANK + DIFF_QW * 2 + DIFF_VW + N_BRANCH * D_MODEL

kernel_name = "hybrid_gla_diffattn_macaron_adaln"

def split_points(sizes):
    pts, acc = [], 0
    for s in sizes[:-1]:
        acc += s
        pts.append(acc)
    return pts

def rmsnorm(x, g):
    xf = x.astype(jnp.float32)
    y = xf * lax.rsqrt(jnp.mean(xf * xf, axis=-1, keepdims=True) + EPS)
    return (y * g.astype(jnp.float32)).astype(x.dtype)

def modulate(xn, shift, scale):
    return xn * (1.0 + scale[:, None, :]) + shift[:, None, :]

def swiglu(x, w_in, w_out):
    g, u = jnp.split(x @ w_in, 2, axis=-1)
    return (jax.nn.silu(g) * u) @ w_out

def gla(q, k, v, a_low, w2, b2):
    B, S, _ = q.shape
    C = GLA_CHUNK
    N = S // C
    f32 = jnp.float32
    log_a = jax.nn.log_sigmoid((a_low @ w2 + b2).astype(f32)) / GLA_TAU

    def chunks(t, d):
        return t.reshape(B, N, C, GLA_HEADS, d).transpose(0, 3, 1, 2, 4).astype(f32)

    qc = chunks(q, GLA_DK) * (GLA_DK ** -0.5)
    kc = chunks(k, GLA_DK)
    vc = chunks(v, GLA_DV)
    b = jnp.cumsum(chunks(log_a, GLA_DK), axis=3)
    b_last = b[:, :, :, -1:, :]

    causal = jnp.tril(jnp.ones((C, C), dtype=bool))
    diff = b[:, :, :, :, None, :] - b[:, :, :, None, :, :]
    decay = jnp.exp(jnp.where(causal[:, :, None], diff, -jnp.inf))
    scores = jnp.einsum('bhntk,bhnsk,bhntsk->bhnts', qc, kc, decay)
    o_intra = jnp.einsum('bhnts,bhnsv->bhntv', scores, vc)

    kv = jnp.einsum('bhnck,bhncv->nbhkv', kc * jnp.exp(b_last - b), vc)
    chunk_decay = jnp.exp(b_last[:, :, :, 0, :]).transpose(2, 0, 1, 3)

    def step(state, inp):
        dec, kvn = inp
        return dec[..., None] * state + kvn, state

    s0 = jnp.zeros((B, GLA_HEADS, GLA_DK, GLA_DV), f32)
    _, s_prev = lax.scan(step, s0, (chunk_decay, kv))
    o_inter = jnp.einsum('bhnck,nbhkv->bhncv', qc * jnp.exp(b), s_prev)
    o = o_intra + o_inter
    return o.transpose(0, 2, 3, 1, 4).reshape(B, S, GLA_HEADS, GLA_DV).astype(v.dtype)

def diff_attention(q, k, v, lq1, lk1, lq2, lk2, lam_init):
    B, S, _ = q.shape
    H = DIFF_HEADS
    f32 = jnp.float32
    q = q.reshape(B, S, H, 2, DIFF_DH).transpose(0, 2, 3, 1, 4) * (DIFF_DH ** -0.5)
    k = k.reshape(B, S, H, 2, DIFF_DH).transpose(0, 2, 3, 1, 4)
    v = v.reshape(B, S, H, DIFF_DV).transpose(0, 2, 1, 3)
    lam = (jnp.exp(jnp.sum(lq1.astype(f32) * lk1.astype(f32)))
           - jnp.exp(jnp.sum(lq2.astype(f32) * lk2.astype(f32))) + lam_init)
    slopes = jnp.exp2(-ALIBI_MAX_BIAS * jnp.arange(1, H + 1, dtype=f32) / H)
    NB = S // Q_BLOCK
    qb = q.reshape(B, H, 2, NB, Q_BLOCK, DIFF_DH).transpose(3, 0, 1, 2, 4, 5)
    kpos = jnp.arange(S)

    def block(args):
        qi, i = args
        qpos = i * Q_BLOCK + jnp.arange(Q_BLOCK)
        rel = (qpos[:, None] - kpos[None, :]).astype(f32)
        s = jnp.einsum('bhiqd,bhikd->bhiqk', qi, k).astype(f32)
        s = s - slopes[None, :, None, None, None] * rel
        s = jnp.where(rel >= 0, s, -jnp.inf)
        p = jax.nn.softmax(s, axis=-1)
        a = p[:, :, 0] - lam * p[:, :, 1]
        return jnp.einsum('bhqk,bhkv->bhqv', a.astype(v.dtype), v)

    o = lax.map(block, (qb, jnp.arange(NB)))
    return o.transpose(1, 0, 3, 2, 4).reshape(B, S, H, DIFF_DV)

def token_mixer(u, w_in, gla_alpha_w2, gla_alpha_b, gla_head_norm,
                diff_lq1, diff_lk1, diff_lq2, diff_lk2, diff_head_norm,
                w_branch_a, w_branch_b, w_out, lam_init):
    B, S, _ = u.shape
    proj = u @ w_in
    gq, gk, gv, gr, ga, dq, dk, dv, gates = jnp.split(proj, split_points(IN_SIZES), axis=-1)
    ya = gla(gq, gk, gv, ga, gla_alpha_w2, gla_alpha_b)
    ya = rmsnorm(ya, gla_head_norm) * jax.nn.silu(gr).reshape(B, S, GLA_HEADS, GLA_DV)
    ya = ya.reshape(B, S, GLA_VW) @ w_branch_a
    yb = diff_attention(dq, dk, dv, diff_lq1, diff_lk1, diff_lq2, diff_lk2, lam_init)
    yb = rmsnorm(yb, diff_head_norm) * (1.0 - lam_init)
    yb = yb.reshape(B, S, DIFF_VW) @ w_branch_b
    g_a, g_b = jnp.split(jax.nn.sigmoid(gates), N_BRANCH, axis=-1)
    return (g_a * ya + g_b * yb) @ w_out

def setup_inputs(seed: int = 0) -> dict:
    key = jax.random.key(seed)
    ks = jax.random.split(key, 24)
    L, D = DEPTH, D_MODEL
    nrm = jax.random.normal

    def gain(k, n):
        return 1.0 + 0.02 * nrm(k, (L, n), jnp.float32)

    return {
        "x": nrm(ks[0], (BATCH, SEQ, D), jnp.float32),
        "c": nrm(ks[1], (BATCH, D), jnp.float32),
        "w_ada": nrm(ks[2], (L, D, N_MOD * D), jnp.float32) * (0.5 * D ** -0.5),
        "b_ada": 0.02 * nrm(ks[3], (L, N_MOD * D), jnp.float32),
        "ffn1_norm": gain(ks[4], D),
        "ffn1_w_in": nrm(ks[5], (L, D, 2 * D_FF), jnp.float32) * D ** -0.5,
        "ffn1_w_out": nrm(ks[6], (L, D_FF, D), jnp.float32) * D_FF ** -0.5,
        "mix_norm": gain(ks[7], D),
        "w_in": nrm(ks[8], (L, D, IN_COLS), jnp.float32) * D ** -0.5,
        "gla_alpha_w2": nrm(ks[9], (L, GLA_RANK, GLA_KW), jnp.float32) * GLA_RANK ** -0.5,
        "gla_alpha_b": 0.1 * nrm(ks[10], (L, GLA_KW), jnp.float32),
        "gla_head_norm": gain(ks[11], GLA_DV),
        "diff_lq1": 0.1 * nrm(ks[12], (L, DIFF_DH), jnp.float32),
        "diff_lk1": 0.1 * nrm(ks[13], (L, DIFF_DH), jnp.float32),
        "diff_lq2": 0.1 * nrm(ks[14], (L, DIFF_DH), jnp.float32),
        "diff_lk2": 0.1 * nrm(ks[15], (L, DIFF_DH), jnp.float32),
        "diff_head_norm": gain(ks[16], DIFF_DV),
        "w_branch_a": nrm(ks[17], (L, GLA_VW, D), jnp.float32) * GLA_VW ** -0.5,
        "w_branch_b": nrm(ks[18], (L, DIFF_VW, D), jnp.float32) * DIFF_VW ** -0.5,
        "w_out": nrm(ks[19], (L, D, D), jnp.float32) * D ** -0.5,
        "ffn2_norm": gain(ks[20], D),
        "ffn2_w_in": nrm(ks[21], (L, D, 2 * D_FF), jnp.float32) * D ** -0.5,
        "ffn2_w_out": nrm(ks[22], (L, D_FF, D), jnp.float32) * D_FF ** -0.5,
        "final_norm": 1.0 + 0.02 * nrm(ks[23], (D,), jnp.float32),
    }

def reference(x, c, w_ada, b_ada, ffn1_norm, ffn1_w_in, ffn1_w_out, mix_norm, w_in,
              gla_alpha_w2, gla_alpha_b, gla_head_norm, diff_lq1, diff_lk1, diff_lq2,
              diff_lk2, diff_head_norm, w_branch_a, w_branch_b, w_out, ffn2_norm,
              ffn2_w_in, ffn2_w_out, final_norm):
    h = x
    c_act = jax.nn.silu(c)
    for l in range(DEPTH):
        lam_init = 0.8 - 0.6 * math.exp(-0.3 * l)
        mod = c_act @ w_ada[l] + b_ada[l]
        (sh1, sc1, gt1, sh2, sc2, gt2, sh3, sc3, gt3) = jnp.split(mod, N_MOD, axis=-1)
        u = modulate(rmsnorm(h, ffn1_norm[l]), sh1, sc1)
        h = h + 0.5 * gt1[:, None, :] * swiglu(u, ffn1_w_in[l], ffn1_w_out[l])
        u = modulate(rmsnorm(h, mix_norm[l]), sh2, sc2)
        m = token_mixer(u, w_in[l], gla_alpha_w2[l], gla_alpha_b[l], gla_head_norm[l],
                        diff_lq1[l], diff_lk1[l], diff_lq2[l], diff_lk2[l], diff_head_norm[l],
                        w_branch_a[l], w_branch_b[l], w_out[l], lam_init)
        h = h + gt2[:, None, :] * m
        u = modulate(rmsnorm(h, ffn2_norm[l]), sh3, sc3)
        h = h + 0.5 * gt3[:, None, :] * swiglu(u, ffn2_w_in[l], ffn2_w_out[l])
    return rmsnorm(h, final_norm)


_drawn_inputs = setup_inputs


def setup_inputs(seed=0):
    import zlib

    import numpy as np

    out = dict(_drawn_inputs(seed))
    spreads = {}
    factors = {'b_ada': 2.951,
     'ffn1_norm': 8.0,
     'mix_norm': 8.0,
     'gla_alpha_b': 8.0,
     'gla_head_norm': 23.342,
     'diff_lq1': 7.387,
     'diff_lk1': 3.125,
     'diff_lq2': 64.0,
     'diff_lk2': 6.233,
     'diff_head_norm': 64.0,
     'ffn2_norm': 30.442,
     'final_norm': 8.42}
    for name, (base, spread) in spreads.items():
        noise = np.random.default_rng([zlib.crc32(name.encode()), seed]).standard_normal(out[name].shape)
        drawn = base * np.exp(spread * noise) if base else spread * noise
        out[name] = __import__('jax').numpy.asarray(drawn.astype(out[name].dtype))
    for name, factor in factors.items():
        out[name] = (out[name] * factor).astype(out[name].dtype)
    return out
```

```python
import numpy as np
import concourse.bass as bass
from concourse import mybir
from contextlib import ExitStack

F32 = mybir.dt.float32
F32R = mybir.dt.float32r
I32 = mybir.dt.int32
ALU = mybir.AluOpType
ACT = mybir.ActivationFunctionType
AX = mybir.AxisListType

P = 128
D = 1024
S = 1024
KT = D // P
TT = S // P
HALF = S // 2
D_FF = 2816
FT = D_FF // P
GROUPS = FT // 2
DOWN = 2 * KT
EPS = 1e-6
N_MOD = 9
ADA_FIRST = 3
SLOTS = 3
ADA_SLOTS = 4
FFN_UNITS = 3 * FT
GLA_H, GLA_DK, GLA_DV, GLA_RANK, GLA_TAU = 4, 64, 128, 16, 16.0
DIFF_H, DIFF_DH, DIFF_DV, ALIBI = 4, 64, 128, 8.0
LAM_INIT = 0.2
KW, VW = GLA_H * GLA_DK, GLA_H * GLA_DV
QW, DVW = DIFF_H * 2 * DIFF_DH, DIFF_H * DIFF_DV
C_GQ, C_GK, C_GV, C_GR = 0, KW, 2 * KW, 2 * KW + VW
C_GA = C_GR + VW
C_DQ = C_GA + GLA_RANK
C_DK, C_DV = C_DQ + QW, C_DQ + 2 * QW
C_GATE = C_DV + DVW
CT = KW // P
LEVELS = 7
EC = (LEVELS + 2) * P
U_GA, U_GQ, U_GK, U_GV = 0, 1, 3, 5
U_HEAD, U_BRANCH = 9, 25
U_OUT = U_BRANCH + 24
MIX_UNITS = U_OUT + KT
MB = FFN_UNITS
BASE = [0, FFN_UNITS + MIX_UNITS]
ROWS = {}
_n = 0
for _name, _rows in (("b_ada", N_MOD * KT), ("ffn1_norm", KT), ("mix_norm", KT), ("ffn2_norm", KT),
                     ("final_norm", KT), ("c", KT), ("gla_head_norm", 1), ("diff_head_norm", 1)):
    ROWS[_name] = (_n, _n + _rows)
    _n += _rows
N_ROWS = _n


def build_program(nc, a, out):
    ctx = ExitStack()
    with ctx:
        def sb(name, shape, dt=F32):
            return ctx.enter_context(nc.sbuf_tensor(name, shape, dt))

        def sem(name):
            return ctx.enter_context(nc.semaphore(name))

        h = sb("h", [P, KT, S])
        u_hi = sb("u_hi", [P, KT, S], F32R)
        u_lo = sb("u_lo", [P, KT, S], F32R)
        w_raw = sb("w_raw", [P, SLOTS, D])
        w_hi = sb("w_hi", [P, SLOTS, D], F32R)
        w_lo = sb("w_lo", [P, SLOTS, D], F32R)
        ident = sb("ident", [P, P])
        ones = sb("ones", [P, P])
        vec = sb("vec", [P, P])
        vecT = sb("vecT", [P, P])
        mod = sb("mod", [P, N_MOD * KT])
        scale_c = sb("scale_c", [P, 3, KT])
        gate_c = sb("gate_c", [P, 2, KT])
        c_act = sb("c_act", [P, KT])
        eps_c = sb("eps_c", [P, 1])
        rar = sb("rar", [P, 8 * S], F32R)
        far = sb("far", [P, 9 * S])

        hid_hi = rar[:, 0:2 * S].rearrange("p (j s) -> p j s", j=2)
        hid_lo = rar[:, 2 * S:4 * S].rearrange("p (j s) -> p j s", j=2)
        silu_b = far[:, 0:S]
        prod_b = far[:, S:2 * S]
        ada_raw = far[:, 2 * S:6 * S].rearrange("p (j s) -> p j s", j=ADA_SLOTS)
        ada_acc = far[:, 6 * S:7 * S]
        x_tile = [far[:, j * S:(j + 1) * S] for j in (0, 1, 7, 8)]
        sq_b = [far[:, j * HALF:(j + 1) * HALF] for j in (0, 1)]
        rstd = [far[:, j * HALF:(j + 1) * HALF] for j in (2, 3)]
        xn_b = [far[:, j * HALF:(j + 1) * HALF] for j in (14, 15)]
        un_b = [far[:, j * HALF:(j + 1) * HALF] for j in (16, 17)]

        gq = [h[:, j, :] for j in (0, 1)]
        gk = [h[:, j, :] for j in (2, 3)]
        gv = h[:, 4:8, :].rearrange("p a (b c) -> p (a b) c", b=2)
        ya = far[:, 0:4 * S].rearrange("p (j s) -> p j s", j=4)
        v_t = [far[:, 4 * S:5 * S], far[:, 6 * S:7 * S]]
        low = far[0:GLA_RANK + 1, 5 * S:6 * S]
        la_b = [far[:, 6 * S + j * HALF:6 * S + (j + 1) * HALF] for j in range(4)]
        la_hi = rar[:, 0:2 * S].rearrange("p (t c) -> p t c", t=TT)
        la_lo = rar[:, 2 * S:4 * S].rearrange("p (t c) -> p t c", t=TT)
        cum = rar[:, 4 * S:4 * S + EC]
        ed = [far[:, 6 * S + c * EC:6 * S + (c + 1) * EC] for c in range(CT)]
        st = far[:, 6 * S + 2 * EC:6 * S + 2 * EC + HALF]
        og = far[:, 4 * S:4 * S + HALF]
        og_sq = far[:, 4 * S + HALF:5 * S]
        og_rs = far[:, 5 * S:5 * S + HALF]
        kd = far[:, 5 * S + HALF:5 * S + HALF + 2 * P]
        qk = [far[:, 5 * S + HALF + (2 + c) * P:5 * S + HALF + (3 + c) * P] for c in range(CT)]
        state = sb("state", [P, CT, GLA_DV])
        dec = sb("dec", [P, 2, CT])
        w2b = sb("w2b", [GLA_RANK + 1, KW])
        mask = sb("mask", [P, LEVELS * (P // 2)], mybir.dt.int8)
        heads2 = sb("heads2", [P, 2])
        dq_hi, dq_lo, dk_hi, dk_lo = [rar[:, j * S:(j + 1) * S] for j in range(4)]
        dv_hi, dv_lo = [rar[:, (4 + j) * S:(5 + j) * S] for j in range(2)]
        at_hi = [rar[:, 6 * S + j * HALF:6 * S + (j + 1) * HALF] for j in range(2)]
        at_lo = [rar[:, 7 * S + j * HALF:7 * S + (j + 1) * HALF] for j in range(2)]
        sc_b = [[h[:, 2 * j + m, :] for m in range(2)] for j in range(2)]
        yb = h[:, 4:8, :]
        r_b = far[:, 5 * S + HALF:6 * S]
        rel = far[:, 7 * S:8 * S]
        bias_b = far[:, 8 * S:9 * S]
        mx = sb("mx", [P, 2, 2, 2])
        nmx = sb("nmx", [P, 2, 2])
        lsum = sb("lsum", [P, 2, 2])
        rec = sb("rec", [P, 2, 2])
        ratio = sb("ratio", [P, 2])
        lamv = sb("lamv", [1, 4, DIFF_DH])
        lams = sb("lams", [P, 6])
        lamj = sb("lamj", [1, DIFF_DH])
        gains = sb("gains", [P, 2])
        y_hi = rar[:, 0:4 * S].rearrange("p (j s) -> p j s", j=4)
        y_lo = rar[:, 4 * S:8 * S].rearrange("p (j s) -> p j s", j=4)
        z = [far[:, j * S:(j + 1) * S] for j in (5, 6, 7, 8, 0, 1, 2, 3)]
        sig_b = [far[:, 4 * S + j * HALF:4 * S + (j + 1) * HALF] for j in range(2)]
        h_dram = nc.dram_tensor("h_dram", (P, KT * S), F32).ap()
        o_tile = [far[:, j * S:(j + 1) * S] for j in (7, 8)]

        ps = [ctx.enter_context(nc.psum_tensor(f"ps{i}", [P, HALF], F32)) for i in range(8)]

        def fm(name):
            return vecT[:, ROWS[name][0]:ROWS[name][1]]

        vec_in = sem("vec_in")
        const_ready = sem("const_ready")
        vec_t = sem("vec_t")
        vecT_ready = sem("vecT_ready")
        c_ready = sem("c_ready")
        x_in = [sem(f"x_in{j}") for j in range(4)]
        x_t = sem("x_t")
        h_act = sem("h_act")
        h_dve = sem("h_dve")
        ada_in = [sem(f"ada_in{j}") for j in range(ADA_SLOTS)]
        ada_used = sem("ada_used")
        ada_sum = sem("ada_sum")
        mod_ready = sem("mod_ready")
        scale_ready = sem("scale_ready")
        w_in_sem = [sem(f"w_loaded{j}") for j in range(SLOTS)]
        w_go = sem("w_go")
        w_high = sem("w_high")
        w_split = sem("w_split")
        unit_done = sem("unit_done")
        sq_ready = sem("sq_ready")
        sq_used = sem("sq_used")
        ln_ready = sem("ln_ready")
        rstd_ready = sem("rstd_ready")
        xn_ready = sem("xn_ready")
        un_ready = sem("un_ready")
        uhi_ready = sem("uhi_ready")
        ulo_ready = sem("ulo_ready")
        silu_ready = sem("silu_ready")
        prod_ready = sem("prod_ready")
        hhi_ready = sem("hhi_ready")
        hlo_ready = sem("hlo_ready")
        out_done = sem("out_done")
        acc_done = sem("acc_done")
        y_ready = sem("y_ready")
        low_init = sem("low_init")
        w2_in = sem("w2_in")
        lam_in = sem("lam_in")
        spill = sem("spill")
        low_ready = sem("low_ready")
        z_done = sem("z_done")
        abs_ready = sem("abs_ready")
        ez_ready = sem("ez_ready")
        lz_ready = sem("lz_ready")
        la_ready = sem("la_ready")
        lahi_ready = sem("lahi_ready")
        lalo_ready = sem("lalo_ready")
        gqk_act = sem("gqk_act")
        gqk_dve = sem("gqk_dve")
        vt_act = sem("vt_act")
        vt_dve = sem("vt_dve")
        v_tr = sem("v_tr")
        gv_act = sem("gv_act")
        gv_dve = sem("gv_dve")
        piece_ready = sem("piece_ready")
        piece_used = sem("piece_used")
        mult_dve = sem("mult_dve")
        mult_pool = sem("mult_pool")
        qk_ready = sem("qk_ready")
        score_done = sem("score_done")
        pred_ready = sem("pred_ready")
        kv_done = sem("kv_done")
        state_ready = sem("state_ready")
        o_done = sem("o_done")
        og_ready = sem("og_ready")
        ogsq_ready = sem("ogsq_ready")
        gln_ready = sem("gln_ready")
        grs_ready = sem("grs_ready")
        ya_ready = sem("ya_ready")
        rel_ready = sem("rel_ready")
        bias_ready = sem("bias_ready")
        s_done = sem("s_done")
        max_ready = sem("max_ready")
        nmx_ready = sem("nmx_ready")
        exp_ready = sem("exp_ready")
        ratio_ready = sem("ratio_ready")
        comb_ready = sem("comb_ready")
        a_ready = sem("a_ready")
        at_done = sem("at_done")
        athi_ready = sem("athi_ready")
        atlo_ready = sem("atlo_ready")
        pv_done = sem("pv_done")
        dqhi = sem("dqhi")
        dqlo = sem("dqlo")
        dvhi = sem("dvhi")
        dvlo = sem("dvlo")
        ob_ready = sem("ob_ready")
        obsq_ready = sem("obsq_ready")
        bms_done = sem("bms_done")
        bln_ready = sem("bln_ready")
        brs_ready = sem("brs_ready")
        yb_ready = sem("yb_ready")
        r_done = sem("r_done")
        r_ready = sem("r_ready")
        rt_ready = sem("rt_ready")
        lam_s = sem("lam_s")
        lam_ps = sem("lam_ps")
        lam_e = sem("lam_e")
        lam_ready = sem("lam_ready")
        yhi_ready = sem("yhi_ready")
        ylo_ready = sem("ylo_ready")
        sig_ready = sem("sig_ready")
        zz_ready = sem("zz_ready")
        zhi_ready = sem("zhi_ready")
        zlo_ready = sem("zlo_ready")
        res_ready = sem("res_ready")
        h_back = sem("h_back")
        chain = sem("chain")
        r_half = sem("r_half")
        pa_done = sem("pa_done")
        gz_ready = sem("gz_ready")
        gains_ready = sem("gains_ready")
        y_t = sem("y_t")
        o_act = sem("o_act")
        o_dve = sem("o_dve")
        o_stored = [sem(f"o_stored{j}") for j in range(2)]

        block = ctx.enter_context(nc.Block())

        W_IN = [a["ffn1_w_in"][0], a["ffn2_w_in"][0]]
        W_OUT = [a["ffn1_w_out"][0], a["ffn2_w_out"][0]]

        pieces = [("E", 0, c, p) for c in range(CT) for p in range(3)]
        for t in range(TT):
            for c in range(CT):
                if t < TT - 1:
                    pieces += [("T", t, c)] + [("E", t + 1, c, p) for p in range(3)]
            if t > 0:
                pieces.append(("ms", t - 1))
        pieces.append(("ms", TT - 1))
        piece_at = {what: n for n, what in enumerate(pieces)}
        ring = []
        for hd in range(DIFF_H):
            for i in range(TT):
                ring += [("T", hd, i, cc) for cc in range(i // 4 + 1)]
                if i in (4, 7):
                    ring.append(("ms", hd, i // 5))
        ring_at = {what: n for n, what in enumerate(ring)}
        chunk_at = {what: n for n, what in enumerate(w for w in ring if w[0] == "T")}
        ms_at = {what: n for n, what in enumerate(w for w in ring if w[0] == "ms")}
        pairs = [(hd, i, cc) for hd in range(DIFF_H) for i in range(TT) for cc in range(i // 4 + 1)]
        pair_at = {what: n for n, what in enumerate(pairs)}

        def width(i, cc):
            return min(HALF, (i + 1) * P - cc * HALF)

        def half(hf):
            return slice(hf * HALF, (hf + 1) * HALF)

        def tile(t):
            return slice(t * P, (t + 1) * P)

        def first_halves(x, l):
            return x.rearrange("p (j two r) -> p j two r", two=2, r=P >> (l + 1))[:, :, 0, :]

        def second_halves(x, l):
            return x.rearrange("p (j two r) -> p j two r", two=2, r=P >> (l + 1))[:, :, 1, :]

        def blocks(x, l):
            return x.rearrange("p (j r) -> p j r", r=P >> (l + 1))

        def decay_products(eng, t, c, done):
            eng.wait_ge(piece_used, piece_at["E", t, c, 2] + 1)
            q, k = gq[c][:, tile(t)], gk[c][:, tile(t)]
            for l in range(LEVELS):
                e = ed[c][:, l * P:(l + 1) * P]
                eng.tensor_tensor(first_halves(e, l), first_halves(e, l), first_halves(k, l), ALU.mult)
                eng.tensor_tensor(second_halves(e, l), second_halves(e, l), second_halves(q, l), ALU.mult)
            e = ed[c][:, LEVELS * P:(LEVELS + 1) * P]
            eng.tensor_tensor(e, e, q, ALU.mult)
            e = ed[c][:, (LEVELS + 1) * P:EC]
            eng.tensor_tensor(e, e, k, ALU.mult).then_inc(done, 1)

        def unit0(f, g):
            return BASE[f] + 4 + 6 * (g - 1)

        def gate_unit(f, j, jj):
            if isinstance(j, int) and j < 2:
                return BASE[f] + 2 * j
            return unit0(f, 0) + 3 * (j - jj) + 4 * jj

        @block.sync
        def _(sp):
            def columns(n, slot, w, c):
                if not (isinstance(n, int) and n < SLOTS):
                    sp.wait_ge(w_split, n - SLOTS + 1)
                sp.dma_start(w_raw[:, slot, :].rearrange("p (k m) -> p k m", k=KT),
                             w[:, c].rearrange("(k p) m -> p k m", p=P)).then_inc(w_in_sem[slot], 16)

            def rows(n, slot, w, r):
                sp.wait_ge(w_split, n - SLOTS + 1)
                sp.dma_start(w_raw[:, slot, :], w[r, :]).then_inc(w_in_sem[slot], 16)

            def ada(m, k):
                i = m * KT + k
                if not (isinstance(i, int) and i < ADA_SLOTS):
                    sp.wait_ge(ada_used, i - ADA_SLOTS + 1)
                sp.dma_start(ada_raw[:, k % ADA_SLOTS, :],
                             a["w_ada"][0][k * P:(k + 1) * P, bass.ds(m * D, D)]).then_inc(ada_in[k % ADA_SLOTS], 16)

            def pair(f, n, slot, j):
                columns(n, slot % SLOTS, W_IN[f], bass.ds(j * P, P))
                columns(n + 1, (slot + 1) % SLOTS, W_IN[f], bass.ds(D_FF + j * P, P))

            def outs(f, n, slot, g):
                rows(n, slot % SLOTS, W_OUT[f], bass.ds(g * 2 * P, P))
                rows(n + 1, (slot + 1) % SLOTS, W_OUT[f], bass.ds(g * 2 * P + P, P))

            def ffn(f):
                pair(f, BASE[f], 0, 0)
                if f == 0:
                    for k in range(KT):
                        ada(2, k)
                pair(f, BASE[f] + 2, 2, 1)

                def body(g, with_ada):
                    n = unit0(f, g)
                    pair(f, n, 1, 2 * g)
                    if with_ada:
                        for k in range(KT):
                            ada(g + ADA_FIRST - 1, k)
                    outs(f, n + 2, 0, g - 1)
                    pair(f, n + 4, 2, 2 * g + 1)
                first = 1
                if f == 0:
                    first = 1 + N_MOD - ADA_FIRST
                    with sp.Fori(1, first) as g:
                        body(g, True)
                with sp.Fori(first, GROUPS) as g:
                    body(g, False)
                outs(f, unit0(f, GROUPS), 1, GROUPS - 1)

            for name, (r0, r1) in ROWS.items():
                src = a[name] if name in ("final_norm",) else a[name][0]
                sp.dma_start(vec[r0:r1, :], src.rearrange("(r c) -> r c", c=P)).then_inc(vec_in, 16)
            sp.dma_start(w2b[0:GLA_RANK, :], a["gla_alpha_w2"][0]).then_inc(w2_in, 16)
            sp.dma_start(w2b[GLA_RANK:GLA_RANK + 1, :], a["gla_alpha_b"]).then_inc(w2_in, 16)
            for j, name in enumerate(("diff_lq1", "diff_lk1", "diff_lq2", "diff_lk2")):
                sp.dma_start(lamv[0:1, j, :], a[name]).then_inc(lam_in, 16)
            for t in range(TT):
                if t >= 4:
                    sp.wait_ge(x_t, 2 * (t - 4) + 2)
                sp.dma_start(x_tile[t % 4], a["x"][0][t * P:(t + 1) * P, :]).then_inc(x_in[t % 4], 16)
                if t == 3:
                    for k in range(ADA_SLOTS):
                        ada(0, k)
            for k in range(ADA_SLOTS, KT):
                ada(0, k)
            for k in range(KT):
                ada(1, k)
            ffn(0)
            W = a["w_in"][0]

            def mix_columns(u, w, c):
                columns(MB + u, u % SLOTS, w, slice(c, c + P))
            starts = [C_GA, C_GQ, C_GQ + P, C_GK, C_GK + P] + [C_GV + P * hd for hd in range(GLA_H)]
            for hd in range(DIFF_H):
                starts += [C_DQ + P * hd, C_DK + P * hd, C_DV + P * hd, C_GR + P * hd]
            for u, c in enumerate(starts):
                mix_columns(u, W, c)
                if u == SLOTS - 1:
                    sp.wait_ge(acc_done, DOWN * GROUPS)
                    sp.dma_start(h_dram, h[:].rearrange("p k s -> p (k s)")).then_inc(spill, 16)
            for br, wb in enumerate((a["w_branch_a"][0], a["w_branch_b"][0])):
                for i in range(4):
                    u = U_BRANCH + 12 * br + 3 * i
                    mix_columns(u, W, C_GATE + D * br + 2 * P * i)
                    mix_columns(u + 1, W, C_GATE + D * br + 2 * P * i + P)
                    n = MB + u + 2
                    sp.wait_ge(w_split, n - SLOTS + 1)
                    sp.dma_start(w_raw[:, (u + 2) % SLOTS, :].rearrange("p (k m) -> p k m", k=4),
                                 wb[:, 2 * P * i:2 * P * (i + 1)].rearrange("(k p) m -> p k m", p=P)
                                 ).then_inc(w_in_sem[(u + 2) % SLOTS], 16)
                    if br == 1 and i == 1:
                        sp.wait_ge(yhi_ready, 8)
                        sp.wait_ge(ylo_ready, 8)
                        sp.dma_start(h[:].rearrange("p k s -> p (k s)"), h_dram).then_inc(h_back, 16)
            for m in range(KT):
                mix_columns(U_OUT + m, a["w_out"][0], m * P)
            ffn(1)
            for t in range(TT):
                sp.wait_ge(o_act, t + 1)
                sp.wait_ge(o_dve, t + 1)
                sp.dma_start(out[0][t * P:(t + 1) * P, :], o_tile[t % 2]).then_inc(o_stored[t % 2], 16)
            for j in range(2):
                sp.wait_ge(o_stored[j], 16 * TT // 2)

        @block.gpsimd
        def _(pool):
            nc.gpsimd.memset(ident[:], 0.0).then_inc(const_ready, 1)
            nc.gpsimd.memset(ones[:], 1.0).then_inc(const_ready, 1)
            nc.gpsimd.memset(eps_c[:], EPS).then_inc(const_ready, 1)
            pool.wait_ge(const_ready, 3)
            nc.gpsimd.affine_select(out=ident[:], in_=ident[:], compare_op=ALU.not_equal, fill=1.0, base=0,
                                    pattern=[[-1, P]], channel_multiplier=1).then_inc(const_ready, 1)

            def select(out_, in_, pattern, base, step, op):
                nc.gpsimd.affine_select(out=out_, in_=in_, compare_op=op, fill=0.0, base=base, pattern=pattern,
                                        channel_multiplier=step).then_inc(const_ready, 1)

            nc.gpsimd.memset(mask[:], 1).then_inc(const_ready, 1)
            nc.gpsimd.memset(heads2[:], 1.0).then_inc(const_ready, 1)
            pool.wait_ge(const_ready, 6)
            for l in range(LEVELS):
                hb, nb = P >> (l + 1), 1 << l
                e = cum[:, l * P:(l + 1) * P]
                one = blocks(ones[:, 0:P // 2], l)
                select(second_halves(e, l), one, [[2 * hb, nb], [1, hb]], hb, -1, ALU.is_ge)
                select(first_halves(e, l), one, [[-2 * hb, nb], [-1, hb]], 0, 1, ALU.is_gt)
                m = blocks(mask[:, l * P // 2:(l + 1) * P // 2], l)
                select(m, m, [[-2 * hb, nb], [0, hb]], 0, 1, ALU.is_ge)
            select(cum[:, LEVELS * P:(LEVELS + 1) * P], ones[:], [[1, P]], 0, -1, ALU.is_ge)
            select(cum[:, (LEVELS + 1) * P:EC], ones[:], [[-1, P]], 0, 1, ALU.is_gt)
            select(heads2[:, 0:1], heads2[:, 0:1], [[0, 1]], P // 2 - 1, -1, ALU.is_ge)
            select(heads2[:, 1:2], heads2[:, 1:2], [[0, 1]], -P // 2, 1, ALU.is_ge)
            pool.wait_ge(const_ready, 6 + 3 * LEVELS + 4)
            for l in range(LEVELS):
                hb, nb = P >> (l + 1), 1 << l
                e = cum[:, l * P:(l + 1) * P]
                select(second_halves(e, l), second_halves(e.bitcast(F32), l), [[-2 * hb, nb], [0, hb]], -hb, 1,
                       ALU.is_ge)
                select(first_halves(e, l), first_halves(e.bitcast(F32), l), [[2 * hb, nb], [0, hb]], hb - 1, -1,
                       ALU.is_ge)
                m = blocks(mask[:, l * P // 2:(l + 1) * P // 2], l)
                select(m, m, [[2 * hb, nb], [0, hb]], hb - 1, -1, ALU.is_ge)

            def split_unit(n, slot, loads):
                pool.wait_ge(w_in_sem[slot], 16 * loads)
                if not (isinstance(n, int) and n < SLOTS):
                    pool.wait_ge(unit_done, n - SLOTS + 1)
                pool.sem_inc(w_go, 1)
                nc.gpsimd.tensor_scalar(w_hi[:, slot, :], w_raw[:, slot, :], 1.0, 0.0,
                                        ALU.mult, ALU.add).then_inc(w_high, 1)
                pool.wait_ge(w_high, n + 1)
                nc.gpsimd.tensor_tensor(w_lo[:, slot, :], w_raw[:, slot, :], w_hi[:, slot, :].bitcast(F32),
                                        ALU.subtract).then_inc(w_split, 1)

            def straight(n0, count):
                for n in range(n0, n0 + count):
                    split_unit(n, n % SLOTS, n // SLOTS + 1)

            def ffn(f):
                straight(BASE[f], 4)
                with pool.Fori(1, GROUPS) as g:
                    n = unit0(f, g)
                    for i in range(6):
                        split_unit(n + i, (1 + i) % SLOTS, (BASE[f] // 3 + 2 + 2 * (g - 1)) + (i + 1) // 3)
                straight(unit0(f, GROUPS), 2)
            ffn(0)
            pool.wait_ge(mod_ready, N_MOD)
            nc.gpsimd.memset(low, 1.0).then_inc(low_init, 1)
            straight(MB, U_HEAD + SLOTS)
            for t in range(TT):
                if t == 0:
                    pool.wait_ge(gqk_act, 4)
                    pool.wait_ge(gqk_dve, 4)
                decay_products(pool, t, 1, mult_pool)
            pool.wait_ge(o_done, TT)
            nc.gpsimd.iota(rel, [[-1, S]], base=S - P, channel_multiplier=1,
                           allow_small_or_imprecise_dtypes=True).then_inc(rel_ready, 1)
            pool.wait_ge(rel_ready, 1)
            nc.gpsimd.affine_select(out=rel, in_=rel, compare_op=ALU.is_ge, fill=1e36, base=S - P,
                                    pattern=[[-1, S]], channel_multiplier=1).then_inc(rel_ready, 1)
            pool.wait_ge(rel_ready, 2)
            for hd in range(DIFF_H):
                if hd > 0:
                    pool.wait_ge(max_ready, 2 * (pair_at[hd - 1, TT - 1, 1] + 1))
                slope = 2.0 ** (-ALIBI * (hd + 1) / DIFF_H)
                nc.gpsimd.tensor_scalar(bias_b, rel, -8.0 * slope, 0.0, ALU.mult, ALU.add).then_inc(bias_ready, 1)
                straight(MB + U_HEAD + SLOTS + 4 * hd, 4)
            straight(MB + U_HEAD + SLOTS + 16, MIX_UNITS - U_HEAD - SLOTS - 16)
            ffn(1)

        @block.scalar
        def _(act):
            def squares(n):
                for hf in range(2):
                    s = slice(hf * HALF, (hf + 1) * HALF)
                    for k in range(KT):
                        i = n * 2 * KT + hf * KT + k
                        if i >= 2:
                            act.wait_ge(sq_used, i - 1)
                        nc.scalar.activation(sq_b[k % 2], h[:, k, s], ACT.Square).then_inc(sq_ready, 1)
                    act.wait_ge(sq_used, n * 2 * KT + hf * KT + KT)
                    nc.scalar.activation(rstd[hf], ps[6 + hf][:], ACT.Ln, bias=eps_c[:, 0:1],
                                         scale=1.0 / D).then_inc(ln_ready, 1)
                    act.wait_ge(ln_ready, 2 * n + hf + 1)
                    nc.scalar.activation(rstd[hf], rstd[hf], ACT.Exp, scale=-0.5).then_inc(rstd_ready, 1)

            def modulate(n):
                act.wait_ge(scale_ready, n + 1)
                for i in range(2 * KT):
                    k, hf = i // 2, i % 2
                    j = n * 2 * KT + i
                    s = slice(hf * HALF, (hf + 1) * HALF)
                    act.wait_ge(xn_ready, j + 1)
                    if j >= 2:
                        act.wait_ge(ulo_ready, j - 1)
                    sc, sh = scale_c[:, n, k:k + 1], mod[:, 3 * n * KT + k:3 * n * KT + k + 1]
                    nc.scalar.activation(un_b[j % 2], xn_b[j % 2], ACT.Identity, bias=sh, scale=sc).then_inc(un_ready, 1)
                    nc.scalar.activation(u_hi[:, k, s], xn_b[j % 2], ACT.Identity, bias=sh, scale=sc).then_inc(uhi_ready, 1)

            def hidden(f, j, jj):
                t = f * FT + j
                act.wait_ge(unit_done, gate_unit(f, j, jj) + 1)
                if not (isinstance(t, int) and t == 0):
                    act.wait_ge(prod_ready, 2 * t)
                for hf in range(2):
                    nc.scalar.activation(silu_b[:, hf * HALF:(hf + 1) * HALF], ps[4 * jj + hf][:],
                                         ACT.Silu).then_inc(silu_ready, 1)
                for hf in range(2):
                    act.wait_ge(prod_ready, 2 * t + hf + 1)
                    if hf == 0 and not (isinstance(j, int) and j < 2):
                        act.wait_ge(unit_done, unit0(f, 0) + 3 * (j - jj) + 4)
                    nc.scalar.activation(hid_hi[:, jj, hf * HALF:(hf + 1) * HALF],
                                         prod_b[:, hf * HALF:(hf + 1) * HALF], ACT.Copy).then_inc(hhi_ready, 1)

            def ffn(f):
                hidden(f, 0, 0)
                with act.Fori(1, GROUPS) as g:
                    hidden(f, 2 * g - 1, 1)
                    hidden(f, 2 * g, 0)
                hidden(f, FT - 1, 1)

            def copy(out_, in_, done, scale=1.0):
                nc.scalar.activation(out_, in_, ACT.Copy, scale=scale).then_inc(done, 1)

            def mixer():
                act.wait_ge(low_init, 1)
                act.wait_ge(unit_done, MB + U_GA + 1)
                for hf in range(2):
                    copy(low[0:GLA_RANK, half(hf)], ps[hf][0:GLA_RANK, :], low_ready)
                for b in range(4):
                    act.wait_ge(z_done, b + 1)
                    nc.scalar.activation(la_b[b], ps[4 + b][:], ACT.Abs).then_inc(abs_ready, 1)
                for b in range(4):
                    act.wait_ge(abs_ready, b + 1)
                    nc.scalar.activation(la_b[b], la_b[b], ACT.Exp, scale=-1.0).then_inc(ez_ready, 1)
                for b in range(4):
                    act.wait_ge(ez_ready, b + 1)
                    nc.scalar.activation(la_b[b], la_b[b], ACT.Ln, bias=ones[:, 0:1]).then_inc(lz_ready, 1)
                for b in range(4):
                    act.wait_ge(la_ready, b + 1)
                    copy(rar[:, b * HALF:(b + 1) * HALF], la_b[b], lahi_ready, 1.0 / GLA_TAU)
                act.wait_ge(spill, 16)
                for j in range(2):
                    act.wait_ge(unit_done, MB + U_GQ + j + 1)
                    for hf in range(2):
                        copy(gq[j][:, half(hf)], ps[2 * ((U_GQ + j) % 2) + hf][:], gqk_act, GLA_DK ** -0.5)
                act.wait_ge(lalo_ready, 4)
                for hd in range(GLA_H + 1):
                    if hd < GLA_H:
                        act.wait_ge(unit_done, MB + U_GV + hd + 1)
                        if hd >= 2:
                            act.wait_ge(v_tr, hd - 1)
                        copy(v_t[hd % 2][:, half(0)], ps[2 * ((U_GV + hd) % 2)][:], vt_act)
                    if hd >= 1:
                        act.wait_ge(v_tr, hd)
                        copy(gv[:, 0:4, tile(hd - 1)], ps[4 + 2 * ((hd - 1) % 2)][:].rearrange("p (t d) -> p t d", t=4),
                             gv_act)

                def decays(t, c):
                    for p in range(3):
                        n = piece_at["E", t, c, p]
                        act.wait_ge(piece_ready, n + 1)
                        lo, hi = p * HALF, min((p + 1) * HALF, EC)
                        e = nc.scalar.activation(ed[c][:, lo:hi], ps[4 + n % 2][:, 0:hi - lo], ACT.Exp)
                        if p == 1:
                            if t >= 2:
                                act.wait_ge(state_ready, CT * (t - 2) + c + 1)
                            e = nc.scalar.activation(dec[:, t % 2, c:c + 1], ps[4 + n % 2][:, HALF - 1:HALF], ACT.Exp)
                        e.then_inc(piece_used, 1)

                def gla_rms(t):
                    n = piece_at["ms", t]
                    act.wait_ge(piece_ready, n + 1)
                    nc.scalar.activation(og_rs, ps[4 + n % 2][:], ACT.Ln, bias=eps_c[:, 0:1],
                                         scale=1.0 / GLA_DV).then_inc(piece_used, 1)
                    act.wait_ge(piece_used, n + 1)
                    nc.scalar.activation(og_rs, og_rs, ACT.Exp, scale=-0.5).then_inc(grs_ready, 1)

                for c in range(CT):
                    decays(0, c)
                for t in range(TT):
                    for c in range(CT):
                        if t < TT - 1:
                            n = piece_at["T", t, c]
                            act.wait_ge(piece_ready, n + 1)
                            if t >= 1:
                                act.wait_ge(kv_done, t)
                            copy(kd[:, tile(c)], ps[4 + n % 2][:, 0:P], piece_used)
                            decays(t + 1, c)
                    if t > 0:
                        gla_rms(t - 1)
                        act.wait_ge(ya_ready, t)
                    act.wait_ge(o_done, t + 1)
                    for hh in range(2):
                        copy(og.rearrange("p (c hh t) -> p c hh t", c=CT, hh=2)[:, :, hh, :],
                             ps[2 + hh][:, 0:2 * P].rearrange("p (c t) -> p c t", c=CT), og_ready)
                    act.wait_ge(og_ready, 2 * t + 2)
                    nc.scalar.activation(og_sq, og, ACT.Square).then_inc(ogsq_ready, 1)
                gla_rms(TT - 1)

                def silu_r(hd, hf):
                    n = 2 * hd + hf
                    if hf == 0:
                        act.wait_ge(r_half, hd + 1)
                    else:
                        act.wait_ge(unit_done, MB + U_HEAD + 4 * hd + 4)
                    if n >= 1:
                        act.wait_ge(rt_ready, n)
                    nc.scalar.activation(r_b, ps[0][:], ACT.Silu).then_inc(r_ready, 1)

                def out_b(hd, hf):
                    n = 2 * hd + hf
                    act.wait_ge(pv_done, chunk_at["T", hd, 4 * hf + 3, hf] + 1)
                    if n >= 1:
                        act.wait_ge(yb_ready, n)
                    copy(og, ps[3][:], ob_ready)
                    act.wait_ge(ob_ready, n + 1)
                    nc.scalar.activation(og_sq, og, ACT.Square).then_inc(obsq_ready, 1)

                def rms_b(hd, hf):
                    n = 2 * hd + hf
                    act.wait_ge(bms_done, n + 1)
                    nc.scalar.activation(og_rs, ps[1 + ring_at["ms", hd, hf] % 2][:], ACT.Ln, bias=eps_c[:, 0:1],
                                         scale=1.0 / DIFF_DV).then_inc(bln_ready, 1)
                    act.wait_ge(bln_ready, n + 1)
                    nc.scalar.activation(og_rs, og_rs, ACT.Exp, scale=-0.5).then_inc(brs_ready, 1)

                for hd in range(DIFF_H):
                    u = MB + U_HEAD + 4 * hd
                    act.wait_ge(unit_done, u + 1)
                    for hf in range(2):
                        copy(dq_hi[:, half(hf)], ps[hf][:], dqhi)
                    act.wait_ge(unit_done, u + 2)
                    for hf in range(2):
                        copy(dk_hi[:, half(hf)], ps[2 + hf][:], dqhi)
                    act.wait_ge(unit_done, u + 3)
                    copy(v_t[1][:, half(0)], ps[0][:], vt_act)
                    for b in range(2):
                        act.wait_ge(v_tr, GLA_H + 2 * hd + b + 1)
                        copy(dv_hi[:, half(b)], ps[4 + b][:], dvhi)
                    for i in range(TT + 1):
                        if i < TT:
                            w = (i + 1) * P
                            act.wait_ge(nmx_ready, TT * hd + i + 1)
                            for m in range(2):
                                x = sc_b[i % 2][m][:, 0:w]
                                nc.scalar.activation(x, x, ACT.Exp, bias=nmx[:, i % 2, m:m + 1],
                                                     accum_out=lsum[:, i % 2, m:m + 1]).then_inc(exp_ready, 1)
                        if i >= 1:
                            b = i - 1
                            act.wait_ge(comb_ready, TT * hd + b + 1)
                            x = sc_b[b % 2][0][:, 0:(b + 1) * P]
                            nc.scalar.activation(x, x, ACT.Copy, scale=rec[:, b % 2, 0:1]).then_inc(a_ready, 1)
                            if b == 5:
                                rms_b(hd, 0)
                            for cc in range(b // 4 + 1):
                                n = chunk_at["T", hd, b, cc]
                                act.wait_ge(at_done, n + 1)
                                if n >= 2:
                                    act.wait_ge(pv_done, n - 1)
                                w = width(b, cc)
                                copy(at_hi[n % 2][:, 0:w], ps[1 + ring_at["T", hd, b, cc] % 2][:, 0:w], athi_ready)
                            if b == 3:
                                silu_r(hd, 0)
                            if b == 4:
                                out_b(hd, 0)
                    silu_r(hd, 1)
                    out_b(hd, 1)
                    rms_b(hd, 1)

                for br in range(2):
                    if br == 0:
                        act.wait_ge(rt_ready, 2 * GLA_H)
                        act.wait_ge(pv_done, chunk_at["T", DIFF_H - 1, TT - 1, 1] + 1)
                    else:
                        act.wait_ge(unit_done, MB + U_BRANCH + 12)
                    act.wait_ge(yb_ready, 2 * DIFF_H)
                    for j in range(4):
                        copy(y_hi[:, j, :], (ya if br == 0 else yb)[:, j, :], yhi_ready)
                    for m in range(KT):
                        act.wait_ge(unit_done, MB + U_BRANCH + 12 * br + 3 * (m // 2) + m % 2 + 1)
                        for hf in range(2):
                            n = 2 * KT * br + 2 * m + hf
                            if n >= 2:
                                act.wait_ge(zz_ready, n - 1)
                            nc.scalar.activation(sig_b[hf], ps[2 + 4 * (m % 2) + hf][:],
                                                 ACT.Sigmoid).then_inc(sig_ready, 1)
                act.wait_ge(unit_done, MB + U_BRANCH + 24)
                for k in range(KT):
                    for hf in range(2):
                        act.wait_ge(zz_ready, 2 * KT + 2 * k + hf + 1)
                        copy(u_hi[:, k, half(hf)], z[k][:, half(hf)], zhi_ready)
                act.wait_ge(res_ready, 2 * KT)

            act.wait_ge(lam_ps, 1)
            nc.scalar.activation(lams[:, 2:4], ps[5][:, 0:2], ACT.Exp).then_inc(lam_e, 1)
            act.wait_ge(vecT_ready, 1)
            nc.scalar.activation(c_act[:], fm("c"), ACT.Silu).then_inc(c_ready, 1)
            for i in range(0, 2 * TT, 2):
                t, k0 = i // 2, 0
                act.wait_ge(x_t, i + 1)
                nc.scalar.activation(h[:, k0:k0 + 4, t * P:(t + 1) * P],
                                     ps[i % 4][:].rearrange("p (k s) -> p k s", k=4), ACT.Copy).then_inc(h_act, 1)
            act.wait_ge(x_t, 2 * TT)
            act.wait_ge(h_act, TT)
            act.wait_ge(h_dve, TT)
            squares(0)
            modulate(0)
            ffn(0)
            act.wait_ge(acc_done, 2 * KT * GROUPS)
            squares(1)
            modulate(1)
            mixer()
            squares(2)
            modulate(2)
            ffn(1)
            act.wait_ge(acc_done, 2 * 2 * KT * GROUPS)
            squares(3)
            for i in range(0, 2 * TT, 2):
                t = i // 2
                act.wait_ge(y_t, i + 1)
                if t >= 2:
                    act.wait_ge(o_stored[t % 2], 16 * (t // 2))
                nc.scalar.activation(o_tile[t % 2][:, 0:HALF], ps[i % 4][:], ACT.Copy).then_inc(o_act, 1)

        @block.vector
        def _(dve):
            def chunk(m):
                for k in range(KT):
                    i = m * KT + k
                    dve.wait_ge(ada_in[k % ADA_SLOTS], 16 * (m * (KT // ADA_SLOTS) + k // ADA_SLOTS + 1))
                    if not (isinstance(i, int) and i == 0):
                        dve.wait_ge(ada_used, i)
                    if k == 0:
                        if not (isinstance(m, int) and m == 0):
                            dve.wait_ge(ada_sum, m)
                        nc.vector.tensor_scalar(ada_acc, ada_raw[:, 0, :], c_act[:, 0:1], None,
                                                ALU.mult).then_inc(ada_used, 1)
                    else:
                        nc.vector.scalar_tensor_tensor(ada_acc, ada_raw[:, k % ADA_SLOTS, :], c_act[:, k:k + 1],
                                                       ada_acc, ALU.mult, ALU.add).then_inc(ada_used, 1)

            def chunk_out(m):
                dve.wait_ge(ada_sum, m + 1)
                nc.vector.tensor_tensor(mod[:, bass.ds(m * KT, KT)], ps[7][:, 0:KT], vecT[:, bass.ds(m * KT, KT)],
                                        ALU.add).then_inc(mod_ready, 1)

            def scale(n, g):
                m = 3 * n + 1
                dve.wait_ge(mod_ready, m + 1)
                nc.vector.scalar_tensor_tensor(scale_c[:, n, :], mod[:, m * KT:(m + 1) * KT], 1.0, fm(g),
                                               ALU.add, ALU.mult).then_inc(scale_ready, 1)

            def norm(n):
                for i in range(2 * KT + 1):
                    if i < 2 * KT:
                        k, hf = i // 2, i % 2
                        j = n * 2 * KT + i
                        dve.wait_ge(rstd_ready, 2 * n + hf + 1)
                        if j >= 2:
                            dve.wait_ge(uhi_ready, j - 1)
                        nc.vector.tensor_tensor(xn_b[j % 2], h[:, k, hf * HALF:(hf + 1) * HALF], rstd[hf],
                                                ALU.mult).then_inc(xn_ready, 1)
                    if i >= 1:
                        k, hf = (i - 1) // 2, (i - 1) % 2
                        j = n * 2 * KT + i - 1
                        s = slice(hf * HALF, (hf + 1) * HALF)
                        dve.wait_ge(uhi_ready, j + 1)
                        nc.vector.tensor_tensor(u_lo[:, k, s], un_b[j % 2], u_hi[:, k, s].bitcast(F32),
                                                ALU.subtract).then_inc(ulo_ready, 1)

            def hidden(f, j, jj):
                t = f * FT + j
                dve.wait_ge(unit_done, gate_unit(f, j, jj) + 2)
                for hf in range(2):
                    s = slice(hf * HALF, (hf + 1) * HALF)
                    dve.wait_ge(silu_ready, 2 * t + hf + 1)
                    if hf == 0 and not (isinstance(t, int) and t == 0):
                        dve.wait_ge(hlo_ready, 2 * t)
                    nc.vector.tensor_tensor(prod_b[:, s], silu_b[:, s], ps[4 * jj + 2 + hf][:],
                                            ALU.mult).then_inc(prod_ready, 1)
                for hf in range(2):
                    s = slice(hf * HALF, (hf + 1) * HALF)
                    dve.wait_ge(hhi_ready, 2 * t + hf + 1)
                    nc.vector.tensor_tensor(hid_lo[:, jj, s], prod_b[:, s], hid_hi[:, jj, s].bitcast(F32),
                                            ALU.subtract).then_inc(hlo_ready, 1)

            def residual(f, g, last=False):
                for i in range(2 * KT):
                    hf, m = i // KT, i % KT
                    s = slice(hf * HALF, (hf + 1) * HALF)
                    if i < DOWN - 1:
                        dve.wait_ge(out_done, (DOWN - 1) * (f * GROUPS + g) + i + 1)
                    else:
                        dve.wait_ge(unit_done, unit0(f, g) + (10 if last is False else 8))
                    nc.vector.scalar_tensor_tensor(h[:, m, s], ps[4 + i % 4][:], gate_c[:, f, m:m + 1], h[:, m, s],
                                                   ALU.mult, ALU.add).then_inc(acc_done, 1)

            def ffn(f):
                if f == 0:
                    chunk(2)
                    chunk_out(2)
                    dve.wait_ge(mod_ready, 3)
                    nc.vector.tensor_scalar(gate_c[:, 0, :], mod[:, 2 * KT:3 * KT], 0.5, None, ALU.mult)
                hidden(f, 0, 0)

                def body(g, with_ada):
                    hidden(f, 2 * g - 1, 1)
                    if with_ada:
                        chunk(g + ADA_FIRST - 1)
                    residual(f, g - 1)
                    if with_ada:
                        chunk_out(g + ADA_FIRST - 1)
                    hidden(f, 2 * g, 0)
                first = 1
                if f == 0:
                    first = 1 + N_MOD - ADA_FIRST
                    with dve.Fori(1, first) as g:
                        body(g, True)
                with dve.Fori(first, GROUPS) as g:
                    body(g, False)
                hidden(f, FT - 1, 1)
                residual(f, GROUPS - 1, last=True)

            def low_part(out_, x, hi, done):
                nc.vector.tensor_tensor(out_, x, hi.bitcast(F32), ALU.subtract).then_inc(done, 1)

            def low_scaled(out_, x, scale, hi, done):
                nc.vector.scalar_tensor_tensor(out_, x, scale, hi.bitcast(F32), ALU.mult, ALU.subtract).then_inc(done, 1)

            def mixer():
                for b in range(4):
                    dve.wait_ge(lz_ready, b + 1)
                    nc.vector.scalar_tensor_tensor(la_b[b], ps[4 + b][:], 0.0, la_b[b], ALU.min,
                                                   ALU.subtract).then_inc(la_ready, 1)
                for b in range(4):
                    dve.wait_ge(lahi_ready, b + 1)
                    low_scaled(rar[:, 2 * S + b * HALF:2 * S + (b + 1) * HALF], la_b[b], 1.0 / GLA_TAU,
                               rar[:, b * HALF:(b + 1) * HALF], lalo_ready)
                dve.wait_ge(spill, 16)
                for j in range(2):
                    dve.wait_ge(unit_done, MB + U_GK + j + 1)
                    for hf in range(2):
                        nc.vector.tensor_copy(gk[j][:, half(hf)],
                                              ps[2 * ((U_GK + j) % 2) + hf][:]).then_inc(gqk_dve, 1)
                for hd in range(GLA_H + 1):
                    if hd < GLA_H:
                        dve.wait_ge(unit_done, MB + U_GV + hd + 1)
                        if hd >= 2:
                            dve.wait_ge(v_tr, hd - 1)
                        nc.vector.tensor_copy(v_t[hd % 2][:, half(1)],
                                              ps[2 * ((U_GV + hd) % 2) + 1][:]).then_inc(vt_dve, 1)
                    if hd >= 1:
                        dve.wait_ge(v_tr, hd)
                        nc.vector.tensor_copy(gv[:, 4:8, tile(hd - 1)],
                                              ps[5 + 2 * ((hd - 1) % 2)][:].rearrange("p (t d) -> p t d", t=4)
                                              ).then_inc(gv_dve, 1)

                def diagonal(t, c):
                    nc.vector.tensor_tensor(qk[c], gq[c][:, tile(t)], gk[c][:, tile(t)],
                                            ALU.mult).then_inc(qk_ready, 1)

                def scores(t, c):
                    dve.wait_ge(score_done, CT * t + c + 1)
                    if t >= 1:
                        dve.wait_ge(o_done, t)
                    for hh in range(2):
                        s_h = st[:, tile(2 * c + hh)]
                        nc.vector.tensor_scalar(s_h, ident[:], ps[6][:, 448 + hh:449 + hh], None,
                                                ALU.mult).then_inc(chain, 1)
                    n = (2 * LEVELS + 1) * (CT * t + c)
                    for l in range(LEVELS):
                        for hh in range(2):
                            cols = slice(l * P // 2, (l + 1) * P // 2)
                            dve.wait_ge(chain, n + 2 * l + hh + 1)
                            last = nc.vector.copy_predicated(second_halves(st[:, tile(2 * c + hh)], l),
                                                             blocks(mask[:, cols], l), blocks(ps[6 + hh][:, cols], l))
                            last.then_inc(pred_ready if (l, hh) == (LEVELS - 1, 1) else chain, 1)

                def update_state(t, c):
                    dve.wait_ge(kv_done, t + 1)
                    if t == 0:
                        nc.vector.tensor_copy(state[:, c, :], ps[0][:, tile(c)]).then_inc(state_ready, 1)
                    else:
                        nc.vector.scalar_tensor_tensor(state[:, c, :], state[:, c, :], dec[:, t % 2, c:c + 1],
                                                       ps[0][:, tile(c)], ALU.mult, ALU.add).then_inc(state_ready, 1)

                def norm_a(t):
                    dve.wait_ge(grs_ready, t + 1)
                    nc.vector.tensor_tensor(ya[:, :, tile(t)], og.rearrange("p (h t) -> p h t", h=GLA_H),
                                            og_rs.rearrange("p (h t) -> p h t", h=GLA_H), ALU.mult).then_inc(ya_ready, 1)

                dve.wait_ge(gqk_act, 4)
                dve.wait_ge(gqk_dve, 4)
                for c in range(CT):
                    diagonal(0, c)
                decay_products(dve, 0, 0, mult_dve)
                for t in range(TT):
                    for c in range(CT):
                        scores(t, c)
                        if t < TT - 1:
                            diagonal(t + 1, c)
                            if c == 0:
                                decay_products(dve, t + 1, 0, mult_dve)
                    if t < TT - 1:
                        for c in range(CT):
                            update_state(t, c)
                    if t > 0:
                        norm_a(t - 1)
                norm_a(TT - 1)

                def maxima(hd, i):
                    if i >= 2:
                        dve.wait_ge(at_done, chunk_at["T", hd, i - 2, (i - 2) // 4] + 1)
                    if TT * hd + i >= 2:
                        dve.wait_ge(nmx_ready, TT * hd + i - 1)
                    for cc in range(i // 4 + 1):
                        n = pair_at[hd, i, cc]
                        w = width(i, cc)
                        c0 = S - P - i * P + cc * HALF
                        dve.wait_ge(s_done, n + 1)
                        if cc == 1:
                            dve.wait_ge(max_ready, 2 * n)
                        for m in range(2):
                            nc.vector.tensor_tensor_reduce(
                                out=sc_b[i % 2][m][:, cc * HALF:cc * HALF + w], in0=ps[4 + 2 * (n % 2) + m][:, 0:w],
                                in1=bias_b[:, c0:c0 + w], scale=DIFF_DH ** -0.5,
                                scalar=-3e38 if cc == 0 else mx[:, i % 2, 0, m:m + 1], op0=ALU.add, op1=ALU.max,
                                accum_out=mx[:, i % 2, cc, m:m + 1]).then_inc(max_ready, 1)
                    dve.wait_ge(max_ready, 2 * n + 2)
                    if i >= 2:
                        dve.wait_ge(exp_ready, 2 * (TT * hd + i - 1))
                    nc.vector.tensor_scalar(nmx[:, i % 2, :], mx[:, i % 2, i // 4, :], -1.0, None,
                                            ALU.mult).then_inc(nmx_ready, 1)

                def combine(hd, i):
                    n = TT * hd + i
                    dve.wait_ge(exp_ready, 2 * n + 2)
                    if n >= 2:
                        dve.wait_ge(a_ready, n - 1)
                    nc.vector.reciprocal(rec[:, i % 2, :], lsum[:, i % 2, :]).then_inc(ratio_ready, 1)
                    dve.wait_ge(ratio_ready, 2 * n + 1)
                    nc.vector.scalar_tensor_tensor(ratio[:, i % 2:i % 2 + 1], lsum[:, i % 2, 0:1], rec[:, i % 2, 1:2],
                                                   lams[:, 5:6], ALU.mult, ALU.mult).then_inc(ratio_ready, 1)
                    dve.wait_ge(ratio_ready, 2 * n + 2)
                    w = (i + 1) * P
                    nc.vector.scalar_tensor_tensor(sc_b[i % 2][0][:, 0:w], sc_b[i % 2][1][:, 0:w],
                                                   ratio[:, i % 2:i % 2 + 1], sc_b[i % 2][0][:, 0:w],
                                                   ALU.mult, ALU.add).then_inc(comb_ready, 1)

                def low_a(hd, i):
                    for cc in range(i // 4 + 1):
                        n = chunk_at["T", hd, i, cc]
                        w = width(i, cc)
                        dve.wait_ge(athi_ready, n + 1)
                        low_part(at_lo[n % 2][:, 0:w], ps[1 + ring_at["T", hd, i, cc] % 2][:, 0:w],
                                 at_hi[n % 2][:, 0:w], atlo_ready)

                def gate_r(hd, hf):
                    dve.wait_ge(r_ready, 2 * hd + hf + 1)
                    nc.vector.scalar_tensor_tensor(ya[:, hd, half(hf)], ya[:, hd, half(hf)], gains[:, 0:1], r_b,
                                                   ALU.mult, ALU.mult).then_inc(rt_ready, 1)

                def norm_b(hd, hf):
                    dve.wait_ge(brs_ready, 2 * hd + hf + 1)
                    nc.vector.scalar_tensor_tensor(yb[:, hd, half(hf)], og, gains[:, 1:2], og_rs,
                                                   ALU.mult, ALU.mult).then_inc(yb_ready, 1)

                dve.wait_ge(lam_ready, 2)
                for hd in range(DIFF_H):
                    u = MB + U_HEAD + 4 * hd
                    for j, (lo, hi) in enumerate(((dq_lo, dq_hi), (dk_lo, dk_hi))):
                        for hf in range(2):
                            dve.wait_ge(dqhi, 4 * hd + 2 * j + hf + 1)
                            low_part(lo[:, half(hf)], ps[2 * j + hf][:], hi[:, half(hf)], dqlo)
                    dve.wait_ge(unit_done, u + 3)
                    nc.vector.tensor_copy(v_t[1][:, half(1)], ps[1][:]).then_inc(vt_dve, 1)
                    for b in range(2):
                        dve.wait_ge(dvhi, 2 * hd + b + 1)
                        low_part(dv_lo[:, half(b)], ps[4 + b][:], dv_hi[:, half(b)], dvlo)
                    dve.wait_ge(bias_ready, hd + 1)
                    for i in range(TT + 2):
                        if i < TT:
                            maxima(hd, i)
                        if 1 <= i <= TT:
                            combine(hd, i - 1)
                        if i >= 2:
                            low_a(hd, i - 2)
                            if i - 2 == 3:
                                gate_r(hd, 0)
                            if i - 2 == 5:
                                norm_b(hd, 0)
                    gate_r(hd, 1)
                    norm_b(hd, 1)

                for br in range(2):
                    y = ya if br == 0 else yb
                    for j in range(4):
                        dve.wait_ge(yhi_ready, 4 * br + j + 1)
                        low_part(y_lo[:, j, :], y[:, j, :], y_hi[:, j, :], ylo_ready)
                    for m in range(KT):
                        i = m // 2
                        if m % 2 == 0:
                            dve.wait_ge(pa_done, 4 * br + i + 1)
                        else:
                            dve.wait_ge(unit_done, MB + U_BRANCH + 12 * br + 3 * i + 3)
                        for hf in range(2):
                            n = 2 * KT * br + 2 * m + hf
                            dve.wait_ge(sig_ready, n + 1)
                            product = ps[4 * (m % 2) + hf][:]
                            if br == 0:
                                nc.vector.tensor_tensor(z[m][:, half(hf)], sig_b[hf], product,
                                                        ALU.mult).then_inc(zz_ready, 1)
                            else:
                                nc.vector.tensor_tensor(sig_b[hf], sig_b[hf], product, ALU.mult).then_inc(gz_ready, 1)
                                dve.wait_ge(gz_ready, 2 * m + hf + 1)
                                nc.vector.tensor_tensor(z[m][:, half(hf)], z[m][:, half(hf)], sig_b[hf],
                                                        ALU.add).then_inc(zz_ready, 1)
                for k in range(KT):
                    for hf in range(2):
                        dve.wait_ge(zhi_ready, 2 * k + hf + 1)
                        low_part(u_lo[:, k, half(hf)], z[k][:, half(hf)], u_hi[:, k, half(hf)], zlo_ready)
                dve.wait_ge(h_back, 16)
                for m in range(KT):
                    dve.wait_ge(unit_done, MB + U_OUT + m + 1)
                    for hf in range(2):
                        nc.vector.scalar_tensor_tensor(h[:, m, half(hf)], ps[2 * (m % 4) + hf][:],
                                                       mod[:, 5 * KT + m:5 * KT + m + 1], h[:, m, half(hf)],
                                                       ALU.mult, ALU.add).then_inc(res_ready, 1)

            dve.wait_ge(lam_in, 64)
            for j in range(2):
                nc.vector.tensor_tensor_reduce(out=lamj[:], in0=lamv[0:1, 2 * j, :], in1=lamv[0:1, 2 * j + 1, :],
                                               scale=1.0, scalar=0.0, op0=ALU.mult, op1=ALU.add,
                                               accum_out=lams[0:1, j:j + 1]).then_inc(lam_s, 1)
                dve.wait_ge(lam_s, j + 1)
            dve.wait_ge(lam_e, 1)
            nc.vector.tensor_tensor(lams[:, 4:5], lams[:, 3:4], lams[:, 2:3], ALU.subtract).then_inc(lam_ready, 1)
            dve.wait_ge(lam_ready, 1)
            nc.vector.tensor_scalar(lams[:, 5:6], lams[:, 4:5], -LAM_INIT, None, ALU.add).then_inc(lam_ready, 1)
            dve.wait_ge(vec_t, 1)
            nc.vector.tensor_copy(vecT[:, 0:N_ROWS], ps[4][:, 0:N_ROWS]).then_inc(vecT_ready, 1)
            dve.wait_ge(vecT_ready, 1)
            nc.vector.tensor_copy(gains[:, 0:1], fm("gla_head_norm")).then_inc(gains_ready, 1)
            nc.vector.tensor_scalar(gains[:, 1:2], fm("diff_head_norm"), 1.0 - LAM_INIT, None,
                                    ALU.mult).then_inc(gains_ready, 1)
            dve.wait_ge(gains_ready, 2)
            for i in range(1, 2 * TT, 2):
                t = i // 2
                dve.wait_ge(x_t, i + 1)
                nc.vector.tensor_copy(h[:, 4:8, t * P:(t + 1) * P],
                                      ps[i % 4][:].rearrange("p (k s) -> p k s", k=4)).then_inc(h_dve, 1)
            dve.wait_ge(c_ready, 1)
            chunk(0)
            chunk_out(0)
            chunk(1)
            chunk_out(1)
            scale(0, "ffn1_norm")
            norm(0)
            ffn(0)
            scale(1, "mix_norm")
            scale(2, "ffn2_norm")
            nc.vector.tensor_scalar(gate_c[:, 1, :], mod[:, 8 * KT:9 * KT], 0.5, None, ALU.mult)
            norm(1)
            mixer()
            norm(2)
            ffn(1)
            for hf in range(2):
                dve.wait_ge(rstd_ready, 6 + hf + 1)
                for k in range(KT):
                    s = slice(hf * HALF, (hf + 1) * HALF)
                    g0 = ROWS["final_norm"][0] + k
                    nc.vector.scalar_tensor_tensor(h[:, k, s], h[:, k, s], vecT[:, g0:g0 + 1], rstd[hf],
                                                   ALU.mult, ALU.mult).then_inc(y_ready, 1)
            for i in range(1, 2 * TT, 2):
                t = i // 2
                dve.wait_ge(y_t, i + 1)
                if t >= 2:
                    dve.wait_ge(o_stored[t % 2], 16 * (t // 2))
                nc.vector.tensor_copy(o_tile[t % 2][:, HALF:S], ps[i % 4][:]).then_inc(o_dve, 1)

        @block.tensor
        def _(pe):
            def mean_square(n):
                for hf in range(2):
                    for k in range(KT):
                        pe.wait_ge(sq_ready, n * 2 * KT + hf * KT + k + 1)
                        nc.tensor.matmul(ps[6 + hf][:], ones[:], sq_b[k % 2], start=(k == 0),
                                         stop=(k == KT - 1)).then_inc(sq_used, 1)

            def column_sums(m):
                pe.wait_ge(ada_used, (m + 1) * KT)
                for j in range(KT):
                    mm = nc.tensor.matmul(ps[7][:, j:j + 1], ada_acc[:, j * P:(j + 1) * P], ones[:, 0:1],
                                          start=True, stop=True)
                mm.then_inc(ada_sum, 1)

            def project(n, slot, bank, first=None, made=ulo_ready):
                pe.wait_ge(w_split, n + 1)
                for k in range(KT):
                    if first is not None:
                        pe.wait_ge(made, first + 2 * k + 2)
                    c = slice(k * P, (k + 1) * P)
                    for w, u in ((w_hi, u_hi), (w_hi, u_lo), (w_lo, u_hi)):
                        for hf in range(2):
                            mm = nc.tensor.matmul(ps[bank + hf][:], w[:, slot, c], u[:, k, hf * HALF:(hf + 1) * HALF],
                                                  start=(k == 0 and u is u_hi and w is w_hi),
                                                  stop=(k == KT - 1 and w is w_lo))
                return mm

            def hidden_in(f, j, jj, n, slot, first=None):
                mm = project(n, slot % SLOTS, 4 * jj, first)
                mm.then_inc(unit_done, 1)
                if f == 0 and isinstance(j, int) and j == 1:
                    pe.wait_ge(mod_ready, 3)
                mm = project(n + 1, (slot + 1) % SLOTS, 4 * jj + 2)
                mm.then_inc(unit_done, 1)

            def down(f, g, n, slot):
                pe.wait_ge(w_split, n + 2)
                pe.wait_ge(hlo_ready, 2 * (f * FT + 2 * g + 2))
                for i in range(2 * KT):
                    hf, m = i // KT, i % KT
                    s = slice(hf * HALF, (hf + 1) * HALF)
                    if i >= 4:
                        pe.wait_ge(acc_done, 2 * KT * (f * GROUPS + g) + i - 3)
                    for j in range(2):
                        c = slice(m * P, (m + 1) * P)
                        for q, (w, x) in enumerate(((w_hi, hid_hi), (w_hi, hid_lo), (w_lo, hid_hi))):
                            mm = nc.tensor.matmul(ps[4 + i % 4][:], w[:, (slot + j) % SLOTS, c], x[:, j, s],
                                                  start=(j == 0 and q == 0), stop=(j == 1 and q == 2))
                    if i < DOWN - 1:
                        mm.then_inc(out_done, 1)
                mm.then_inc(unit_done, 2)

            def ffn(f):
                t0 = f * FT
                hidden_in(f, 0, 0, BASE[f], 0, f * 4 * KT)
                if f == 0:
                    column_sums(2)
                hidden_in(f, 1, 1, BASE[f] + 2, 2)

                def body(g, with_ada):
                    n = unit0(f, g)
                    pe.wait_ge(prod_ready, 2 * (t0 + 2 * g - 1))
                    hidden_in(f, 2 * g, 0, n, 1)
                    down(f, g - 1, n + 2, 0)
                    pe.wait_ge(acc_done, 2 * KT * (f * GROUPS + g))
                    if with_ada:
                        column_sums(g + ADA_FIRST - 1)
                    mm = project(n + 4, 2, 4)
                    mm.then_inc(unit_done, 1)
                    if with_ada:
                        pe.wait_ge(mod_ready, g + ADA_FIRST)
                    mm = project(n + 5, 0, 6)
                    mm.then_inc(unit_done, 1)
                first = 1
                if f == 0:
                    first = 1 + N_MOD - ADA_FIRST
                    with pe.Fori(1, first) as g:
                        body(g, True)
                with pe.Fori(first, GROUPS) as g:
                    body(g, False)
                down(f, GROUPS - 1, unit0(f, GROUPS), 1)

            def three(out_, w, x, start, stop):
                for q, (i, j) in enumerate(((0, 0), (0, 1), (1, 0))):
                    mm = nc.tensor.matmul(out_, w[i], x[j], start=(start and q == 0), stop=(stop and q == 2))
                return mm

            def mixer():
                pe.wait_ge(rstd_ready, 4)
                project(MB, 0, 0, 2 * KT).then_inc(unit_done, 1)
                free = [None, (low_ready, 2), (gqk_act, 2), (gqk_act, 4), (gqk_dve, 2), (gqk_dve, 4)]

                def unit(u):
                    if 2 <= u <= 6:
                        pe.wait_ge(*free[u - 1])
                    elif u > 6:
                        pe.wait_ge(vt_act, u - 6)
                        pe.wait_ge(vt_dve, u - 6)
                    project(MB + u, u % SLOTS, 2 * (u % 2)).then_inc(unit_done, 1)

                def turn_v(src, bank, gate):
                    for t in range(TT):
                        mm = nc.tensor.transpose(ps[bank + t // 4][:, tile(t % 4)], src[:, tile(t)], ident[:])
                        if gate and t % 4 == 3:
                            mm.then_inc(v_tr, 1)
                    if not gate:
                        mm.then_inc(v_tr, 1)

                unit(1)
                pe.wait_ge(low_ready, 2)
                pe.wait_ge(w2_in, 32)
                for t in range(TT):
                    mm = nc.tensor.matmul(ps[4 + t // 2][:, (t % 2) * KW:(t % 2 + 1) * KW], low[:, tile(t)], w2b[:],
                                          start=True, stop=True)
                    if t % 2:
                        mm.then_inc(z_done, 1)
                for u in range(2, U_GV + 1):
                    unit(u)
                pe.wait_ge(la_ready, 4)
                for hd in range(GLA_H):
                    if hd + 1 < GLA_H:
                        unit(U_GV + hd + 1)
                    pe.wait_ge(vt_act, hd + 1)
                    pe.wait_ge(vt_dve, hd + 1)
                    if hd >= 2:
                        pe.wait_ge(gv_act, hd - 1)
                        pe.wait_ge(gv_dve, hd - 1)
                    turn_v(v_t[hd % 2], 4 + 2 * (hd % 2), False)
                pe.wait_ge(gv_act, GLA_H)
                pe.wait_ge(gv_dve, GLA_H)

                def free_piece(n):
                    if n >= 2:
                        pe.wait_ge(piece_used, n - 1)

                def decays(t, c):
                    for p in range(3):
                        n = piece_at["E", t, c, p]
                        free_piece(n)
                        lo, hi = p * HALF, min((p + 1) * HALF, EC)
                        for q, la in enumerate((la_hi, la_lo)):
                            mm = nc.tensor.matmul(ps[4 + n % 2][:, 0:hi - lo], la[:, t, tile(c)], cum[:, lo:hi],
                                                  start=(q == 0), stop=(q == 1))
                        mm.then_inc(piece_ready, 1)

                def scores(t, c):
                    pe.wait_ge(mult_dve if c == 0 else mult_pool, t + 1)
                    pe.wait_ge(qk_ready, CT * t + c + 1)
                    if t + c > 0:
                        pe.wait_ge(pred_ready, CT * t + c)
                    nc.tensor.matmul(ps[6][:, 448:450], qk[c], heads2[:], start=True, stop=True)
                    for l in range(LEVELS):
                        for hh in range(2):
                            ch = slice(hh * GLA_DK, (hh + 1) * GLA_DK)
                            e = ed[c][ch, l * P:(l + 1) * P]
                            mm = nc.tensor.matmul(blocks(ps[6 + hh][:, l * P // 2:(l + 1) * P // 2], l), e,
                                                  second_halves(e, l), start=True, stop=True)
                    mm.then_inc(score_done, 1)
                    if t > 0:
                        pe.wait_ge(state_ready, CT * (t - 1) + c + 1)
                        if c == 0:
                            pe.wait_ge(og_ready, 2 * t)
                        for hh in range(2):
                            ch = slice(hh * GLA_DK, (hh + 1) * GLA_DK)
                            nc.tensor.matmul(ps[2 + hh][:, tile(c)], state[ch, c, :], ed[c][ch, LEVELS * P:(LEVELS + 1) * P],
                                             start=(c == 0), stop=False, skip_group_check=True)
                    if t < TT - 1:
                        n = piece_at["T", t, c]
                        free_piece(n)
                        nc.tensor.transpose(ps[4 + n % 2][:, 0:P], ed[c][:, (LEVELS + 1) * P:EC],
                                            ident[:]).then_inc(piece_ready, 1)

                def sum_squares(t):
                    n = piece_at["ms", t]
                    free_piece(n)
                    pe.wait_ge(ogsq_ready, t + 1)
                    nc.tensor.matmul(ps[4 + n % 2][:], ones[:], og_sq, start=True, stop=True).then_inc(piece_ready, 1)

                pe.wait_ge(lalo_ready, 4)
                for c in range(CT):
                    decays(0, c)
                for t in range(TT):
                    for c in range(CT):
                        scores(t, c)
                        if t < TT - 1:
                            decays(t + 1, c)
                    if t < TT - 1:
                        pe.wait_ge(piece_used, piece_at["T", t, 1] + 1)
                        for c in range(CT):
                            for hh in range(2):
                                ch = slice(hh * GLA_DK, (hh + 1) * GLA_DK)
                                mm = nc.tensor.matmul(ps[0][ch, tile(c)], kd[:, c * P + hh * GLA_DK:c * P + (hh + 1) * GLA_DK],
                                                      gv[:, t, tile(2 * c + hh)], start=True, stop=True)
                        mm.then_inc(kv_done, 1)
                    if t > 0:
                        sum_squares(t - 1)
                    pe.wait_ge(pred_ready, CT * (t + 1))
                    for c in range(CT):
                        for hh in range(2):
                            mm = nc.tensor.matmul(ps[2 + hh][:, tile(c)], gv[:, t, tile(2 * c + hh)], st[:, tile(2 * c + hh)],
                                                  start=(t == 0), stop=True, skip_group_check=True)
                    mm.then_inc(o_done, 1)
                sum_squares(TT - 1)

                def key_scores(hd, i):
                    for cc in range(i // 4 + 1):
                        n = pair_at[hd, i, cc]
                        if n >= 2 and not (i < 2 and cc == 0 and False):
                            pe.wait_ge(max_ready, 2 * (n - 1))
                        w = width(i, cc)
                        for q, (x, y) in enumerate(((dq_hi, dk_hi), (dq_hi, dk_lo), (dq_lo, dk_hi))):
                            for m in range(2):
                                ch = slice(m * DIFF_DH, (m + 1) * DIFF_DH)
                                mm = nc.tensor.matmul(ps[4 + 2 * (n % 2) + m][:, 0:w], x[ch, tile(i)],
                                                      y[ch, cc * HALF:cc * HALF + w], start=(q == 0), stop=(q == 2))
                        mm.then_inc(s_done, 1)

                def free_ring(n):
                    if n >= 2:
                        what = ring[n - 2]
                        if what[0] == "T":
                            pe.wait_ge(atlo_ready, chunk_at[what] + 1)
                        else:
                            pe.wait_ge(bln_ready, ms_at[what] + 1)

                def turn_a(hd, i):
                    pe.wait_ge(a_ready, TT * hd + i + 1)
                    for cc in range(i // 4 + 1):
                        n = ring_at["T", hd, i, cc]
                        free_ring(n)
                        for j in range(width(i, cc) // P):
                            mm = nc.tensor.transpose(ps[1 + n % 2][:, tile(j)], sc_b[i % 2][0][:, tile(4 * cc + j)], ident[:])
                        mm.then_inc(at_done, 1)

                def values(hd, i):
                    if i == 4:
                        pe.wait_ge(ob_ready, 2 * hd + 1)
                    for cc in range(i // 4 + 1):
                        n = chunk_at["T", hd, i, cc]
                        pe.wait_ge(atlo_ready, n + 1)
                        for j in range(width(i, cc) // P):
                            kb = 4 * cc + j
                            mm = three(ps[3][:, tile(i % 4)], (dv_hi[:, tile(kb)], dv_lo[:, tile(kb)]),
                                       (at_hi[n % 2][:, tile(j)], at_lo[n % 2][:, tile(j)]), kb == 0, kb == i)
                        mm.then_inc(pv_done, 1)

                def sum_squares_b(hd, hf):
                    n = ring_at["ms", hd, hf]
                    free_ring(n)
                    pe.wait_ge(obsq_ready, 2 * hd + hf + 1)
                    nc.tensor.matmul(ps[1 + n % 2][:], ones[:], og_sq, start=True, stop=True).then_inc(bms_done, 1)

                def project_r(hd, i):
                    u = U_HEAD + 4 * hd + 3
                    hf = i // 4
                    if i == 0:
                        pe.wait_ge(w_split, MB + u + 1)
                    if i == 4:
                        pe.wait_ge(r_ready, 2 * hd + 1)
                    for k in (2 * (i % 4), 2 * (i % 4) + 1):
                        mm = three(ps[0][:], (w_hi[:, u % SLOTS, tile(k)], w_lo[:, u % SLOTS, tile(k)]),
                                   (u_hi[:, k, half(hf)], u_lo[:, k, half(hf)]), k == 0, k == KT - 1)
                    if i == 3:
                        mm.then_inc(r_half, 1)
                    if i == 7:
                        mm.then_inc(unit_done, 1)

                pe.wait_ge(state_ready, CT * (TT - 1))
                pe.wait_ge(og_ready, 2 * TT)
                for hd in range(DIFF_H):
                    u = U_HEAD + 4 * hd
                    if hd > 0:
                        pe.wait_ge(r_ready, 2 * hd)
                        pe.wait_ge(ob_ready, 2 * hd)
                        pe.wait_ge(bln_ready, 2 * hd)
                    project(MB + u, u % SLOTS, 0).then_inc(unit_done, 1)
                    project(MB + u + 1, (u + 1) % SLOTS, 2).then_inc(unit_done, 1)
                    pe.wait_ge(dqlo, 4 * hd + 2)
                    project(MB + u + 2, (u + 2) % SLOTS, 0).then_inc(unit_done, 1)
                    pe.wait_ge(vt_act, GLA_H + hd + 1)
                    pe.wait_ge(vt_dve, GLA_H + hd + 1)
                    if hd == 0:
                        pe.wait_ge(piece_used, len(pieces))
                    else:
                        pe.wait_ge(max_ready, 2 * (pair_at[hd - 1, TT - 1, 1] + 1))
                    turn_v(v_t[1], 4, True)
                    pe.wait_ge(dvlo, 2 * hd + 2)
                    pe.wait_ge(dqlo, 4 * hd + 4)
                    key_scores(hd, 0)
                    key_scores(hd, 1)
                    for i in range(TT):
                        if i + 2 < TT:
                            key_scores(hd, i + 2)
                        turn_a(hd, i)
                        project_r(hd, i)
                        values(hd, i)
                        if i == 4:
                            sum_squares_b(hd, 0)
                    sum_squares_b(hd, 1)

                for br in range(2):
                    for i in range(4):
                        u = U_BRANCH + 12 * br + 3 * i
                        for j in range(2):
                            m = 2 * i + j
                            n = 2 * KT * br + 2 * m
                            if n >= 4:
                                pe.wait_ge(sig_ready, n - 2)
                            elif j == 0:
                                pe.wait_ge(ob_ready, 2 * DIFF_H)
                                pe.wait_ge(bln_ready, 2 * DIFF_H)
                            project(MB + u + j, (u + j) % SLOTS, 2 + 4 * j).then_inc(unit_done, 1)
                        if i == 0:
                            pe.wait_ge(ylo_ready, 4 * br + 4)
                        pe.wait_ge(w_split, MB + u + 3)
                        for j in range(2):
                            m = 2 * i + j
                            n = 2 * KT * br + 2 * m
                            if n >= 4:
                                pe.wait_ge(zz_ready, n - 2)
                            slot = (u + 2) % SLOTS
                            for k in range(4):
                                c = slice(k * 2 * P + j * P, k * 2 * P + (j + 1) * P)
                                for hf in range(2):
                                    mm = three(ps[4 * j + hf][:], (w_hi[:, slot, c], w_lo[:, slot, c]),
                                               (y_hi[:, k, half(hf)], y_lo[:, k, half(hf)]), k == 0, k == 3)
                            mm.then_inc(pa_done if j == 0 else unit_done, 1)
                pe.wait_ge(zz_ready, 4 * KT)
                for m in range(KT):
                    if m >= 4:
                        pe.wait_ge(res_ready, 2 * (m - 3))
                    project(MB + U_OUT + m, (U_OUT + m) % SLOTS, 2 * (m % 4), 0 if m == 0 else None,
                            zlo_ready).then_inc(unit_done, 1)

            pe.wait_ge(const_ready, 6 + 6 * LEVELS + 4)
            pe.wait_ge(lam_s, 2)
            nc.tensor.matmul(ps[5][:, 0:2], ones[0:1, :], lams[0:1, 0:2], start=True, stop=True).then_inc(lam_ps, 1)
            pe.wait_ge(vec_in, 16 * len(ROWS))
            nc.tensor.transpose(ps[4][:, 0:N_ROWS], vec[0:N_ROWS, :], ident[0:N_ROWS, 0:N_ROWS]).then_inc(vec_t, 1)
            for i in range(2 * TT):
                t, k0 = i // 2, 4 * (i % 2)
                if i % 2 == 0:
                    pe.wait_ge(x_in[t % 4], 16 * (t // 4 + 1))
                if i >= 4:
                    pe.wait_ge(h_act if i % 2 == 0 else h_dve, (i - 4) // 2 + 1)
                for k in range(k0, k0 + 4):
                    mm = nc.tensor.transpose(ps[i % 4][:, (k - k0) * P:(k - k0 + 1) * P],
                                             x_tile[t % 4][:, k * P:(k + 1) * P], ident[:])
                mm.then_inc(x_t, 1)
            mean_square_first = mean_square
            column_sums(0)
            pe.wait_ge(mod_ready, 1)
            column_sums(1)
            pe.wait_ge(mod_ready, 2)
            mean_square_first(0)
            ffn(0)
            mean_square(1)
            mixer()
            mean_square(2)
            ffn(1)
            mean_square(3)
            for i in range(2 * TT):
                t, k0 = i // 2, 4 * (i % 2)
                if i == 0:
                    pe.wait_ge(y_ready, KT)
                if t == TT // 2:
                    pe.wait_ge(y_ready, 2 * KT)
                if i >= 4:
                    pe.wait_ge(o_act if i % 2 == 0 else o_dve, (i - 4) // 2 + 1)
                for k in range(k0, k0 + 4):
                    mm = nc.tensor.transpose(ps[i % 4][:, (k - k0) * P:(k - k0 + 1) * P],
                                             h[:, k, t * P:(t + 1) * P], ident[:])
                mm.then_inc(y_t, 1)


NAMES = ["x", "c", "w_ada", "b_ada", "ffn1_norm", "ffn1_w_in", "ffn1_w_out", "mix_norm", "w_in",
         "gla_alpha_w2", "gla_alpha_b", "gla_head_norm", "diff_lq1", "diff_lk1", "diff_lq2", "diff_lk2",
         "diff_head_norm", "w_branch_a", "w_branch_b", "w_out", "ffn2_norm", "ffn2_w_in", "ffn2_w_out",
         "final_norm"]


def kernel(**inputs):
    import concourse.bacc as bacc
    from concourse.bass_utils import run_bass_kernel_spmd

    nc = bacc.Bacc("TRN2", target_bir_lowering=False, num_devices=1)
    arrays, args = {}, {}
    for name in NAMES:
        arr = np.ascontiguousarray(inputs[name])
        arrays[f"in_{name}"] = arr
        args[name] = nc.dram_tensor(f"in_{name}", arr.shape, mybir.dt.from_np(arr.dtype), kind="ExternalInput").ap()
    out = nc.dram_tensor("out_h", (1, S, D), F32, kind="ExternalOutput").ap()
    build_program(nc, args, out)
    result = run_bass_kernel_spmd(nc, [arrays], core_ids=[0])
    return result.results[0]["out_h"]
```

```python
import numpy as np
import concourse.bass as bass
from concourse import mybir
from contextlib import ExitStack

F32 = mybir.dt.float32
F32R = mybir.dt.float32r
I32 = mybir.dt.int32
ALU = mybir.AluOpType
ACT = mybir.ActivationFunctionType
AX = mybir.AxisListType

P = 128
D = 1024
S = 1024
KT = D // P
TT = S // P
HALF = S // 2
D_FF = 2816
FT = D_FF // P
GROUPS = FT // 2
DOWN = 2 * KT
EPS = 1e-6
N_MOD = 9
ADA_FIRST = 3
SLOTS = 3
ADA_SLOTS = 4
FFN_UNITS = 3 * FT
GLA_H, GLA_DK, GLA_DV, GLA_RANK, GLA_TAU = 4, 64, 128, 16, 16.0
DIFF_H, DIFF_DH, DIFF_DV, ALIBI = 4, 64, 128, 8.0
LAM_INIT = 0.2
KW, VW = GLA_H * GLA_DK, GLA_H * GLA_DV
QW, DVW = DIFF_H * 2 * DIFF_DH, DIFF_H * DIFF_DV
C_GQ, C_GK, C_GV, C_GR = 0, KW, 2 * KW, 2 * KW + VW
C_GA = C_GR + VW
C_DQ = C_GA + GLA_RANK
C_DK, C_DV = C_DQ + QW, C_DQ + 2 * QW
C_GATE = C_DV + DVW
CT = KW // P
LEVELS = 7
EC = (LEVELS + 2) * P
U_GA, U_GQ, U_GK, U_GV = 0, 1, 3, 5
U_HEAD, U_BRANCH = 9, 25
U_OUT = U_BRANCH + 24
MIX_UNITS = U_OUT + KT
MB = FFN_UNITS
BASE = [0, FFN_UNITS + MIX_UNITS]
ROWS = {}
_n = 0
for _name, _rows in (("b_ada", N_MOD * KT), ("ffn1_norm", KT), ("mix_norm", KT), ("ffn2_norm", KT),
                     ("final_norm", KT), ("c", KT), ("gla_head_norm", 1), ("diff_head_norm", 1)):
    ROWS[_name] = (_n, _n + _rows)
    _n += _rows
N_ROWS = _n


def build_program(nc, a, out):
    ctx = ExitStack()
    with ctx:
        def sb(name, shape, dt=F32):
            return ctx.enter_context(nc.sbuf_tensor(name, shape, dt))

        def sem(name):
            return ctx.enter_context(nc.semaphore(name))

        h = sb("h", [P, KT, S])
        u_hi = sb("u_hi", [P, KT, S], F32R)
        u_lo = sb("u_lo", [P, KT, S], F32R)
        w_raw = sb("w_raw", [P, SLOTS, D])
        w_hi = sb("w_hi", [P, SLOTS, D], F32R)
        w_lo = sb("w_lo", [P, SLOTS, D], F32R)
        ident = sb("ident", [P, P])
        ones = sb("ones", [P, P])
        vec = sb("vec", [P, P])
        vecT = sb("vecT", [P, P])
        mod = sb("mod", [P, N_MOD * KT])
        scale_c = sb("scale_c", [P, 3, KT])
        gate_c = sb("gate_c", [P, 2, KT])
        c_act = sb("c_act", [P, KT])
        eps_c = sb("eps_c", [P, 1])
        rar = sb("rar", [P, 8 * S], F32R)
        far = sb("far", [P, 9 * S])

        hid_hi = rar[:, 0:2 * S].rearrange("p (j s) -> p j s", j=2)
        hid_lo = rar[:, 2 * S:4 * S].rearrange("p (j s) -> p j s", j=2)
        silu_b = far[:, 0:S]
        prod_b = far[:, S:2 * S]
        ada_raw = far[:, 2 * S:6 * S].rearrange("p (j s) -> p j s", j=ADA_SLOTS)
        ada_acc = far[:, 6 * S:7 * S]
        x_tile = [far[:, j * S:(j + 1) * S] for j in (0, 1, 7, 8)]
        sq_b = [far[:, j * HALF:(j + 1) * HALF] for j in (0, 1)]
        rstd = [far[:, j * HALF:(j + 1) * HALF] for j in (2, 3)]
        xn_b = [far[:, j * HALF:(j + 1) * HALF] for j in (14, 15)]
        un_b = [far[:, j * HALF:(j + 1) * HALF] for j in (16, 17)]

        gq = [h[:, j, :] for j in (0, 1)]
        gk = [h[:, j, :] for j in (2, 3)]
        gv = h[:, 4:8, :].rearrange("p a (b c) -> p (a b) c", b=2)
        ya = far[:, 0:4 * S].rearrange("p (j s) -> p j s", j=4)
        v_t = [far[:, 4 * S:5 * S], far[:, 6 * S:7 * S]]
        low = far[0:GLA_RANK + 1, 5 * S:6 * S]
        la_b = [far[:, 6 * S + j * HALF:6 * S + (j + 1) * HALF] for j in range(4)]
        la_hi = rar[:, 0:2 * S].rearrange("p (t c) -> p t c", t=TT)
        la_lo = rar[:, 2 * S:4 * S].rearrange("p (t c) -> p t c", t=TT)
        cum = rar[:, 4 * S:4 * S + EC]
        ed = [far[:, 6 * S + c * EC:6 * S + (c + 1) * EC] for c in range(CT)]
        st = far[:, 6 * S + 2 * EC:6 * S + 2 * EC + HALF]
        og = far[:, 4 * S:4 * S + HALF]
        og_sq = far[:, 4 * S + HALF:5 * S]
        og_rs = far[:, 5 * S:5 * S + HALF]
        kd = far[:, 5 * S + HALF:5 * S + HALF + 2 * P]
        qk = [far[:, 5 * S + HALF + (2 + c) * P:5 * S + HALF + (3 + c) * P] for c in range(CT)]
        state = sb("state", [P, CT, GLA_DV])
        dec = sb("dec", [P, 2, CT])
        w2b = sb("w2b", [GLA_RANK + 1, KW])
        mask = sb("mask", [P, LEVELS * (P // 2)], mybir.dt.int8)
        heads2 = sb("heads2", [P, 2])
        dq_hi, dq_lo, dk_hi, dk_lo = [rar[:, j * S:(j + 1) * S] for j in range(4)]
        dv = rar[:, 4 * S:6 * S].rearrange("p (t two d) -> p t two d", t=TT, two=2)
        at_hi = [rar[:, 6 * S + j * HALF:6 * S + (j + 1) * HALF] for j in range(2)]
        at_lo = [rar[:, 7 * S + j * HALF:7 * S + (j + 1) * HALF] for j in range(2)]
        sc_b = [[h[:, 2 * j + m, :] for m in range(2)] for j in range(2)]
        yb = h[:, 4:8, :]
        on = far[:, 4 * S + HALF:5 * S]
        sq_junk = far[:, 5 * S:5 * S + P]
        ssq = sb("ssq", [P, 4])
        r_b = far[:, 5 * S + HALF:6 * S]
        raw_b = [far[:, 7 * S + j * HALF:7 * S + (j + 1) * HALF] for j in range(2)]
        bias_b = far[:, 8 * S:9 * S]
        mx = sb("mx", [P, 2, 2, 2])
        nmx = sb("nmx", [P, 2, 2])
        lsum = sb("lsum", [P, 2, 2])
        rec = sb("rec", [P, 2, 2])
        ratio = sb("ratio", [P, 2])
        lamv = sb("lamv", [1, 4, DIFF_DH])
        lams = sb("lams", [P, 6])
        lamj = sb("lamj", [1, DIFF_DH])
        gains = sb("gains", [P, 2])
        y_hi = rar[:, 0:4 * S].rearrange("p (j s) -> p j s", j=4)
        y_lo = rar[:, 4 * S:8 * S].rearrange("p (j s) -> p j s", j=4)
        z = [far[:, j * S:(j + 1) * S] for j in (5, 6, 7, 8, 0, 1, 2, 3)]
        sig_b = [far[:, 4 * S + j * HALF:4 * S + (j + 1) * HALF] for j in range(2)]
        h_dram = nc.dram_tensor("h_dram", (P, KT * S), F32).ap()
        o_tile = [far[:, j * S:(j + 1) * S] for j in (7, 8)]

        ps = [ctx.enter_context(nc.psum_tensor(f"ps{i}", [P, HALF], F32)) for i in range(8)]

        def fm(name):
            return vecT[:, ROWS[name][0]:ROWS[name][1]]

        vec_in = sem("vec_in")
        const_ready = sem("const_ready")
        vec_t = sem("vec_t")
        vecT_ready = sem("vecT_ready")
        c_ready = sem("c_ready")
        x_in = [sem(f"x_in{j}") for j in range(4)]
        x_t = sem("x_t")
        h_act = sem("h_act")
        h_dve = sem("h_dve")
        ada_in = [sem(f"ada_in{j}") for j in range(ADA_SLOTS)]
        ada_used = sem("ada_used")
        ada_sum = sem("ada_sum")
        mod_ready = sem("mod_ready")
        scale_ready = sem("scale_ready")
        w_in_sem = [sem(f"w_loaded{j}") for j in range(SLOTS)]
        w_go = sem("w_go")
        w_high = sem("w_high")
        w_split = sem("w_split")
        unit_done = sem("unit_done")
        sq_ready = sem("sq_ready")
        sq_used = sem("sq_used")
        ln_ready = sem("ln_ready")
        rstd_ready = sem("rstd_ready")
        xn_ready = sem("xn_ready")
        un_ready = sem("un_ready")
        uhi_ready = sem("uhi_ready")
        ulo_ready = sem("ulo_ready")
        silu_ready = sem("silu_ready")
        prod_ready = sem("prod_ready")
        hhi_ready = sem("hhi_ready")
        hlo_ready = sem("hlo_ready")
        out_done = sem("out_done")
        acc_done = sem("acc_done")
        y_ready = sem("y_ready")
        low_init = sem("low_init")
        w2_in = sem("w2_in")
        lam_in = sem("lam_in")
        spill = sem("spill")
        low_ready = sem("low_ready")
        z_done = sem("z_done")
        abs_ready = sem("abs_ready")
        ez_ready = sem("ez_ready")
        lz_ready = sem("lz_ready")
        la_ready = sem("la_ready")
        lahi_ready = sem("lahi_ready")
        lalo_ready = sem("lalo_ready")
        gqk_act = sem("gqk_act")
        gqk_dve = sem("gqk_dve")
        vt_act = sem("vt_act")
        vt_dve = sem("vt_dve")
        v_tr = sem("v_tr")
        gv_act = sem("gv_act")
        gv_dve = sem("gv_dve")
        piece_ready = sem("piece_ready")
        piece_used = sem("piece_used")
        mult_dve = sem("mult_dve")
        mult_pool = sem("mult_pool")
        qk_ready = sem("qk_ready")
        score_done = sem("score_done")
        pred_ready = sem("pred_ready")
        kv_done = sem("kv_done")
        state_ready = sem("state_ready")
        o_done = sem("o_done")
        og_ready = sem("og_ready")
        ogsq_ready = sem("ogsq_ready")
        gln_ready = sem("gln_ready")
        grs_ready = sem("grs_ready")
        ya_ready = sem("ya_ready")
        bias_ready = sem("bias_ready")
        s_done = sem("s_done")
        max_ready = sem("max_ready")
        nmx_ready = sem("nmx_ready")
        exp_ready = sem("exp_ready")
        ratio_ready = sem("ratio_ready")
        comb_ready = sem("comb_ready")
        a_ready = sem("a_ready")
        at_done = sem("at_done")
        athi_ready = sem("athi_ready")
        atlo_ready = sem("atlo_ready")
        pv_done = sem("pv_done")
        dqhi = sem("dqhi")
        dqlo = sem("dqlo")
        dvhi = sem("dvhi")
        dvlo = sem("dvlo")
        oh_ready = sem("oh_ready")
        ob_ready = sem("ob_ready")
        obsq_ready = sem("obsq_ready")
        on_ready = sem("on_ready")
        on_t = sem("on_t")
        bln_ready = sem("bln_ready")
        brs_ready = sem("brs_ready")
        yb_ready = sem("yb_ready")
        r_done = sem("r_done")
        r_ready = sem("r_ready")
        rt_ready = sem("rt_ready")
        lam_s = sem("lam_s")
        lam_ps = sem("lam_ps")
        lam_e = sem("lam_e")
        lam_ready = sem("lam_ready")
        yhi_ready = sem("yhi_ready")
        ylo_ready = sem("ylo_ready")
        sig_ready = sem("sig_ready")
        zz_ready = sem("zz_ready")
        zhi_ready = sem("zhi_ready")
        zlo_ready = sem("zlo_ready")
        res_ready = sem("res_ready")
        h_back = sem("h_back")
        chain = sem("chain")
        fill_done = sem("fill_done")
        raw_ready = sem("raw_ready")
        pa_done = sem("pa_done")
        gz_ready = sem("gz_ready")
        gains_ready = sem("gains_ready")
        y_t = sem("y_t")
        o_act = sem("o_act")
        o_dve = sem("o_dve")
        o_stored = [sem(f"o_stored{j}") for j in range(2)]

        block = ctx.enter_context(nc.Block())

        W_IN = [a["ffn1_w_in"][0], a["ffn2_w_in"][0]]
        W_OUT = [a["ffn1_w_out"][0], a["ffn2_w_out"][0]]

        pieces = [("E", 0, c, p) for c in range(CT) for p in range(3)]
        for t in range(TT):
            for c in range(CT):
                if t < TT - 1:
                    pieces += [("T", t, c)] + [("E", t + 1, c, p) for p in range(3)]
            if t > 0:
                pieces.append(("ms", t - 1))
        pieces.append(("ms", TT - 1))
        piece_at = {what: n for n, what in enumerate(pieces)}
        ring = []
        for hd in range(DIFF_H):
            for i in range(TT):
                ring += [("T", hd, i, cc) for cc in range(i // 4 + 1)]
                if i == 5:
                    ring.append(("out", hd, 0))
                if i == 1 and hd > 0:
                    ring.append(("out", hd - 1, 1))
        ring.append(("out", DIFF_H - 1, 1))
        ring_at = {what: n for n, what in enumerate(ring)}
        chunk_at = {what: n for n, what in enumerate(w for w in ring if w[0] == "T")}
        pairs = [(hd, i, cc) for hd in range(DIFF_H) for i in range(TT) for cc in range(i // 4 + 1)]
        pair_at = {what: n for n, what in enumerate(pairs)}

        FILL = [("r", 0), ("r", 1), ("q", 0), ("k", 0), ("v", 0), ("v", 1), ("q", 1), ("k", 1)]
        FILL_UNIT = {"r": 0, "q": 1, "k": 2, "v": 3}

        def fill_of(hd, i):
            what, hf = FILL[i]
            return (what, hf) if what == "r" or hd + 1 < DIFF_H else (None, hf)

        def r_unit(hd):
            return U_HEAD + 3 + 4 * hd

        def fill_count(hd, i):
            return 5 * hd + (1 if i == 0 else i)

        def unit_count(hd, i):
            return MB + r_unit(hd) + {1: 1, 6: 2, 7: 4}[i]

        def q_scale(hd):
            return 4.0 ** hd

        def width(i, cc):
            return min(HALF, (i + 1) * P - cc * HALF)

        def half(hf):
            return slice(hf * HALF, (hf + 1) * HALF)

        def tile(t):
            return slice(t * P, (t + 1) * P)

        def first_halves(x, l):
            return x.rearrange("p (j two r) -> p j two r", two=2, r=P >> (l + 1))[:, :, 0, :]

        def second_halves(x, l):
            return x.rearrange("p (j two r) -> p j two r", two=2, r=P >> (l + 1))[:, :, 1, :]

        def blocks(x, l):
            return x.rearrange("p (j r) -> p j r", r=P >> (l + 1))

        def decay_products(eng, t, c, done):
            eng.wait_ge(piece_used, piece_at["E", t, c, 2] + 1)
            q, k = gq[c][:, tile(t)], gk[c][:, tile(t)]
            for l in range(LEVELS):
                e = ed[c][:, l * P:(l + 1) * P]
                eng.tensor_tensor(first_halves(e, l), first_halves(e, l), first_halves(k, l), ALU.mult)
                eng.tensor_tensor(second_halves(e, l), second_halves(e, l), second_halves(q, l), ALU.mult)
            e = ed[c][:, LEVELS * P:(LEVELS + 1) * P]
            eng.tensor_tensor(e, e, q, ALU.mult)
            e = ed[c][:, (LEVELS + 1) * P:EC]
            eng.tensor_tensor(e, e, k, ALU.mult).then_inc(done, 1)

        def unit0(f, g):
            return BASE[f] + 4 + 6 * (g - 1)

        def gate_unit(f, j, jj):
            if isinstance(j, int) and j < 2:
                return BASE[f] + 2 * j
            return unit0(f, 0) + 3 * (j - jj) + 4 * jj

        @block.sync
        def _(sp):
            def columns(n, slot, w, c):
                if not (isinstance(n, int) and n < SLOTS):
                    sp.wait_ge(w_split, n - SLOTS + 1)
                sp.dma_start(w_raw[:, slot, :].rearrange("p (k m) -> p k m", k=KT),
                             w[:, c].rearrange("(k p) m -> p k m", p=P)).then_inc(w_in_sem[slot], 16)

            def rows(n, slot, w, r):
                sp.wait_ge(w_split, n - SLOTS + 1)
                sp.dma_start(w_raw[:, slot, :], w[r, :]).then_inc(w_in_sem[slot], 16)

            def ada(m, k):
                i = m * KT + k
                if not (isinstance(i, int) and i < ADA_SLOTS):
                    sp.wait_ge(ada_used, i - ADA_SLOTS + 1)
                sp.dma_start(ada_raw[:, k % ADA_SLOTS, :],
                             a["w_ada"][0][k * P:(k + 1) * P, bass.ds(m * D, D)]).then_inc(ada_in[k % ADA_SLOTS], 16)

            def pair(f, n, slot, j):
                columns(n, slot % SLOTS, W_IN[f], bass.ds(j * P, P))
                columns(n + 1, (slot + 1) % SLOTS, W_IN[f], bass.ds(D_FF + j * P, P))

            def outs(f, n, slot, g):
                rows(n, slot % SLOTS, W_OUT[f], bass.ds(g * 2 * P, P))
                rows(n + 1, (slot + 1) % SLOTS, W_OUT[f], bass.ds(g * 2 * P + P, P))

            def ffn(f):
                pair(f, BASE[f], 0, 0)
                if f == 0:
                    for k in range(KT):
                        ada(2, k)
                pair(f, BASE[f] + 2, 2, 1)

                def body(g, with_ada):
                    n = unit0(f, g)
                    pair(f, n, 1, 2 * g)
                    if with_ada:
                        for k in range(KT):
                            ada(g + ADA_FIRST - 1, k)
                    outs(f, n + 2, 0, g - 1)
                    pair(f, n + 4, 2, 2 * g + 1)
                first = 1
                if f == 0:
                    first = 1 + N_MOD - ADA_FIRST
                    with sp.Fori(1, first) as g:
                        body(g, True)
                with sp.Fori(first, GROUPS) as g:
                    body(g, False)
                outs(f, unit0(f, GROUPS), 1, GROUPS - 1)

            for name, (r0, r1) in ROWS.items():
                src = a[name] if name in ("final_norm",) else a[name][0]
                sp.dma_start(vec[r0:r1, :], src.rearrange("(r c) -> r c", c=P)).then_inc(vec_in, 16)
            sp.dma_start(w2b[0:GLA_RANK, :], a["gla_alpha_w2"][0]).then_inc(w2_in, 16)
            sp.dma_start(w2b[GLA_RANK:GLA_RANK + 1, :], a["gla_alpha_b"]).then_inc(w2_in, 16)
            for j, name in enumerate(("diff_lq1", "diff_lk1", "diff_lq2", "diff_lk2")):
                sp.dma_start(lamv[0:1, j, :], a[name]).then_inc(lam_in, 16)
            for t in range(TT):
                if t >= 4:
                    sp.wait_ge(x_t, 2 * (t - 4) + 2)
                sp.dma_start(x_tile[t % 4], a["x"][0][t * P:(t + 1) * P, :]).then_inc(x_in[t % 4], 16)
                if t == 3:
                    for k in range(ADA_SLOTS):
                        ada(0, k)
            for k in range(ADA_SLOTS, KT):
                ada(0, k)
            for k in range(KT):
                ada(1, k)
            ffn(0)
            W = a["w_in"][0]

            def mix_columns(u, w, c):
                columns(MB + u, u % SLOTS, w, slice(c, c + P))
            starts = [C_GA, C_GQ, C_GQ + P, C_GK, C_GK + P] + [C_GV + P * hd for hd in range(GLA_H)]
            starts += [C_DV, C_DQ, C_DK]
            for hd in range(DIFF_H):
                starts.append(C_GR + P * hd)
                if hd + 1 < DIFF_H:
                    starts += [C_DQ + P * (hd + 1), C_DK + P * (hd + 1), C_DV + P * (hd + 1)]
            for u, c in enumerate(starts):
                mix_columns(u, W, c)
                if u == SLOTS - 1:
                    sp.wait_ge(acc_done, DOWN * GROUPS)
                    sp.dma_start(h_dram, h[:].rearrange("p k s -> p (k s)")).then_inc(spill, 16)
            for br, wb in enumerate((a["w_branch_a"][0], a["w_branch_b"][0])):
                for i in range(4):
                    u = U_BRANCH + 12 * br + 3 * i
                    mix_columns(u, W, C_GATE + D * br + 2 * P * i)
                    mix_columns(u + 1, W, C_GATE + D * br + 2 * P * i + P)
                    n = MB + u + 2
                    sp.wait_ge(w_split, n - SLOTS + 1)
                    sp.dma_start(w_raw[:, (u + 2) % SLOTS, :].rearrange("p (k m) -> p k m", k=4),
                                 wb[:, 2 * P * i:2 * P * (i + 1)].rearrange("(k p) m -> p k m", p=P)
                                 ).then_inc(w_in_sem[(u + 2) % SLOTS], 16)
                    if br == 1 and i == 1:
                        sp.wait_ge(yhi_ready, 8)
                        sp.wait_ge(ylo_ready, 8)
                        sp.dma_start(h[:].rearrange("p k s -> p (k s)"), h_dram).then_inc(h_back, 16)
            for m in range(KT):
                mix_columns(U_OUT + m, a["w_out"][0], m * P)
            ffn(1)
            for t in range(TT):
                sp.wait_ge(o_act, t + 1)
                sp.wait_ge(o_dve, t + 1)
                sp.dma_start(out[0][t * P:(t + 1) * P, :], o_tile[t % 2]).then_inc(o_stored[t % 2], 16)
            for j in range(2):
                sp.wait_ge(o_stored[j], 16 * TT // 2)

        @block.gpsimd
        def _(pool):
            nc.gpsimd.memset(ident[:], 0.0).then_inc(const_ready, 1)
            nc.gpsimd.memset(ones[:], 1.0).then_inc(const_ready, 1)
            nc.gpsimd.memset(eps_c[:], EPS).then_inc(const_ready, 1)
            pool.wait_ge(const_ready, 3)
            nc.gpsimd.affine_select(out=ident[:], in_=ident[:], compare_op=ALU.not_equal, fill=1.0, base=0,
                                    pattern=[[-1, P]], channel_multiplier=1).then_inc(const_ready, 1)

            def select(out_, in_, pattern, base, step, op):
                nc.gpsimd.affine_select(out=out_, in_=in_, compare_op=op, fill=0.0, base=base, pattern=pattern,
                                        channel_multiplier=step).then_inc(const_ready, 1)

            nc.gpsimd.memset(mask[:], 1).then_inc(const_ready, 1)
            nc.gpsimd.memset(heads2[:], 1.0).then_inc(const_ready, 1)
            pool.wait_ge(const_ready, 6)
            for l in range(LEVELS):
                hb, nb = P >> (l + 1), 1 << l
                e = cum[:, l * P:(l + 1) * P]
                one = blocks(ones[:, 0:P // 2], l)
                select(second_halves(e, l), one, [[2 * hb, nb], [1, hb]], hb, -1, ALU.is_ge)
                select(first_halves(e, l), one, [[-2 * hb, nb], [-1, hb]], 0, 1, ALU.is_gt)
                m = blocks(mask[:, l * P // 2:(l + 1) * P // 2], l)
                select(m, m, [[-2 * hb, nb], [0, hb]], 0, 1, ALU.is_ge)
            select(cum[:, LEVELS * P:(LEVELS + 1) * P], ones[:], [[1, P]], 0, -1, ALU.is_ge)
            select(cum[:, (LEVELS + 1) * P:EC], ones[:], [[-1, P]], 0, 1, ALU.is_gt)
            select(heads2[:, 0:1], heads2[:, 0:1], [[0, 1]], P // 2 - 1, -1, ALU.is_ge)
            select(heads2[:, 1:2], heads2[:, 1:2], [[0, 1]], -P // 2, 1, ALU.is_ge)
            pool.wait_ge(const_ready, 6 + 3 * LEVELS + 4)
            for l in range(LEVELS):
                hb, nb = P >> (l + 1), 1 << l
                e = cum[:, l * P:(l + 1) * P]
                select(second_halves(e, l), second_halves(e.bitcast(F32), l), [[-2 * hb, nb], [0, hb]], -hb, 1,
                       ALU.is_ge)
                select(first_halves(e, l), first_halves(e.bitcast(F32), l), [[2 * hb, nb], [0, hb]], hb - 1, -1,
                       ALU.is_ge)
                m = blocks(mask[:, l * P // 2:(l + 1) * P // 2], l)
                select(m, m, [[2 * hb, nb], [0, hb]], hb - 1, -1, ALU.is_ge)

            def split_unit(n, slot, loads):
                pool.wait_ge(w_in_sem[slot], 16 * loads)
                if not (isinstance(n, int) and n < SLOTS):
                    pool.wait_ge(unit_done, n - SLOTS + 1)
                pool.sem_inc(w_go, 1)
                nc.gpsimd.tensor_scalar(w_hi[:, slot, :], w_raw[:, slot, :], 1.0, 0.0,
                                        ALU.mult, ALU.add).then_inc(w_high, 1)
                pool.wait_ge(w_high, n + 1)
                nc.gpsimd.tensor_tensor(w_lo[:, slot, :], w_raw[:, slot, :], w_hi[:, slot, :].bitcast(F32),
                                        ALU.subtract).then_inc(w_split, 1)

            def straight(n0, count):
                for n in range(n0, n0 + count):
                    split_unit(n, n % SLOTS, n // SLOTS + 1)

            def ffn(f):
                straight(BASE[f], 4)
                with pool.Fori(1, GROUPS) as g:
                    n = unit0(f, g)
                    for i in range(6):
                        split_unit(n + i, (1 + i) % SLOTS, (BASE[f] // 3 + 2 + 2 * (g - 1)) + (i + 1) // 3)
                straight(unit0(f, GROUPS), 2)
            ffn(0)
            pool.wait_ge(mod_ready, N_MOD)
            nc.gpsimd.memset(low, 1.0).then_inc(low_init, 1)
            straight(MB, U_HEAD + SLOTS)
            for t in range(TT):
                if t == 0:
                    pool.wait_ge(gqk_act, 4)
                    pool.wait_ge(gqk_dve, 4)
                decay_products(pool, t, 1, mult_pool)
            pool.wait_ge(o_done, TT)
            nc.gpsimd.iota(bias_b, [[-1, S]], base=S - P, channel_multiplier=1,
                           allow_small_or_imprecise_dtypes=True).then_inc(bias_ready, 1)
            pool.wait_ge(bias_ready, 1)
            nc.gpsimd.tensor_scalar(bias_b, bias_b, -DIFF_DH ** 0.5 * 2.0 ** (-ALIBI / DIFF_H), 0.0, ALU.mult,
                                    ALU.add).then_inc(bias_ready, 1)
            pool.wait_ge(bias_ready, 2)
            nc.gpsimd.affine_select(out=bias_b, in_=bias_b, compare_op=ALU.is_ge, fill=-2e36, base=S - P,
                                    pattern=[[-1, S]], channel_multiplier=1).then_inc(bias_ready, 1)
            straight(MB + U_HEAD + SLOTS, MIX_UNITS - U_HEAD - SLOTS)
            ffn(1)

        @block.scalar
        def _(act):
            def squares(n):
                nc.scalar.preload_act_table_set("natural_log_exp_and_others")
                for hf in range(2):
                    s = slice(hf * HALF, (hf + 1) * HALF)
                    for k in range(KT):
                        i = n * 2 * KT + hf * KT + k
                        if i >= 2:
                            act.wait_ge(sq_used, i - 1)
                        nc.scalar.activation(sq_b[k % 2], h[:, k, s], ACT.Square).then_inc(sq_ready, 1)
                    act.wait_ge(sq_used, n * 2 * KT + hf * KT + KT)
                    nc.scalar.activation(rstd[hf], ps[6 + hf][:], ACT.Ln, bias=eps_c[:, 0:1],
                                         scale=1.0 / D).then_inc(ln_ready, 1)
                    act.wait_ge(ln_ready, 2 * n + hf + 1)
                    nc.scalar.activation(rstd[hf], rstd[hf], ACT.Exp, scale=-0.5).then_inc(rstd_ready, 1)

            def modulate(n):
                act.wait_ge(scale_ready, n + 1)
                for i in range(2 * KT):
                    k, hf = i // 2, i % 2
                    j = n * 2 * KT + i
                    s = slice(hf * HALF, (hf + 1) * HALF)
                    act.wait_ge(xn_ready, j + 1)
                    if j >= 2:
                        act.wait_ge(ulo_ready, j - 1)
                    sc, sh = scale_c[:, n, k:k + 1], mod[:, 3 * n * KT + k:3 * n * KT + k + 1]
                    nc.scalar.activation(un_b[j % 2], xn_b[j % 2], ACT.Identity, bias=sh, scale=sc).then_inc(un_ready, 1)
                    nc.scalar.activation(u_hi[:, k, s], xn_b[j % 2], ACT.Identity, bias=sh, scale=sc).then_inc(uhi_ready, 1)

            def hidden(f, j, jj):
                t = f * FT + j
                act.wait_ge(unit_done, gate_unit(f, j, jj) + 1)
                if not (isinstance(t, int) and t == 0):
                    act.wait_ge(prod_ready, 2 * t)
                for hf in range(2):
                    nc.scalar.activation(silu_b[:, hf * HALF:(hf + 1) * HALF], ps[4 * jj + hf][:],
                                         ACT.Silu).then_inc(silu_ready, 1)
                for hf in range(2):
                    act.wait_ge(prod_ready, 2 * t + hf + 1)
                    if hf == 0 and not (isinstance(j, int) and j < 2):
                        act.wait_ge(unit_done, unit0(f, 0) + 3 * (j - jj) + 4)
                    nc.scalar.activation(hid_hi[:, jj, hf * HALF:(hf + 1) * HALF],
                                         prod_b[:, hf * HALF:(hf + 1) * HALF], ACT.Copy).then_inc(hhi_ready, 1)

            def ffn(f):
                hidden(f, 0, 0)
                with act.Fori(1, GROUPS) as g:
                    hidden(f, 2 * g - 1, 1)
                    hidden(f, 2 * g, 0)
                hidden(f, FT - 1, 1)

            def copy(out_, in_, done, scale=1.0):
                nc.scalar.activation(out_, in_, ACT.Copy, scale=scale).then_inc(done, 1)

            def mixer():
                act.wait_ge(low_init, 1)
                act.wait_ge(unit_done, MB + U_GA + 1)
                for hf in range(2):
                    copy(low[0:GLA_RANK, half(hf)], ps[hf][0:GLA_RANK, :], low_ready)
                for b in range(4):
                    act.wait_ge(z_done, b + 1)
                    nc.scalar.activation(la_b[b], ps[4 + b][:], ACT.Abs).then_inc(abs_ready, 1)
                for b in range(4):
                    act.wait_ge(abs_ready, b + 1)
                    nc.scalar.activation(la_b[b], la_b[b], ACT.Exp, scale=-1.0).then_inc(ez_ready, 1)
                for b in range(4):
                    act.wait_ge(ez_ready, b + 1)
                    nc.scalar.activation(la_b[b], la_b[b], ACT.Ln, bias=ones[:, 0:1]).then_inc(lz_ready, 1)
                for b in range(4):
                    act.wait_ge(la_ready, b + 1)
                    copy(rar[:, b * HALF:(b + 1) * HALF], la_b[b], lahi_ready, 1.0 / GLA_TAU)
                act.wait_ge(spill, 16)
                for j in range(2):
                    act.wait_ge(unit_done, MB + U_GQ + j + 1)
                    for hf in range(2):
                        copy(gq[j][:, half(hf)], ps[2 * ((U_GQ + j) % 2) + hf][:], gqk_act, GLA_DK ** -0.5)
                act.wait_ge(lalo_ready, 4)
                for hd in range(GLA_H + 1):
                    if hd < GLA_H:
                        act.wait_ge(unit_done, MB + U_GV + hd + 1)
                        if hd >= 2:
                            act.wait_ge(v_tr, hd - 1)
                        copy(v_t[hd % 2][:, half(0)], ps[2 * ((U_GV + hd) % 2)][:], vt_act)
                    if hd >= 1:
                        act.wait_ge(v_tr, hd)
                        copy(gv[:, 0:4, tile(hd - 1)], ps[4 + 2 * ((hd - 1) % 2)][:].rearrange("p (t d) -> p t d", t=4),
                             gv_act)

                def decays(t, c):
                    for p in range(3):
                        n = piece_at["E", t, c, p]
                        act.wait_ge(piece_ready, n + 1)
                        lo, hi = p * HALF, min((p + 1) * HALF, EC)
                        e = nc.scalar.activation(ed[c][:, lo:hi], ps[4 + n % 2][:, 0:hi - lo], ACT.Exp)
                        if p == 1:
                            if t >= 2:
                                act.wait_ge(state_ready, CT * (t - 2) + c + 1)
                            e = nc.scalar.activation(dec[:, t % 2, c:c + 1], ps[4 + n % 2][:, HALF - 1:HALF], ACT.Exp)
                        e.then_inc(piece_used, 1)

                def gla_rms(t):
                    n = piece_at["ms", t]
                    act.wait_ge(piece_ready, n + 1)
                    nc.scalar.activation(og_rs, ps[4 + n % 2][:], ACT.Ln, bias=eps_c[:, 0:1],
                                         scale=1.0 / GLA_DV).then_inc(piece_used, 1)
                    act.wait_ge(piece_used, n + 1)
                    nc.scalar.activation(og_rs, og_rs, ACT.Exp, scale=-0.5).then_inc(grs_ready, 1)

                for c in range(CT):
                    decays(0, c)
                for t in range(TT):
                    for c in range(CT):
                        if t < TT - 1:
                            n = piece_at["T", t, c]
                            act.wait_ge(piece_ready, n + 1)
                            if t >= 1:
                                act.wait_ge(kv_done, t)
                            copy(kd[:, tile(c)], ps[4 + n % 2][:, 0:P], piece_used)
                            decays(t + 1, c)
                    if t > 0:
                        gla_rms(t - 1)
                        act.wait_ge(ya_ready, t)
                    act.wait_ge(o_done, t + 1)
                    for hh in range(2):
                        copy(og.rearrange("p (c hh t) -> p c hh t", c=CT, hh=2)[:, :, hh, :],
                             ps[2 + hh][:, 0:2 * P].rearrange("p (c t) -> p c t", c=CT), og_ready)
                    act.wait_ge(og_ready, 2 * t + 2)
                    nc.scalar.activation(og_sq, og, ACT.Square).then_inc(ogsq_ready, 1)
                gla_rms(TT - 1)

                def fill_out(hd, i):
                    what, hf = fill_of(hd, i)
                    if what is None:
                        return
                    if i in (1, 6, 7):
                        act.wait_ge(unit_done, unit_count(hd, i))
                    else:
                        act.wait_ge(fill_done, fill_count(hd, i))
                    if what == "r":
                        n = 2 * hd + hf
                        if n >= 1:
                            act.wait_ge(rt_ready, n)
                        nc.scalar.activation(r_b, ps[0][:], ACT.Silu).then_inc(r_ready, 1)
                        nc.scalar.preload_act_table_set("natural_log_exp_and_others")
                    elif what == "v":
                        copy(v_t[1][:, half(hf)], ps[0][:], vt_act)
                    elif hf == 0:
                        copy(raw_b[0 if what == "q" else 1], ps[0][:], raw_ready)
                    elif what == "q":
                        copy(dq_hi[:, half(1)], ps[0][:], dqhi, q_scale(hd + 1))
                    else:
                        copy(dk_hi[:, half(1)], ps[0][:], dqhi)

                def squares_b(hd, i):
                    n = TT * hd + i
                    act.wait_ge(ob_ready, n + 1)
                    if n >= 1:
                        act.wait_ge(obsq_ready, n)
                    if i % 4 == 0 and n >= 4:
                        act.wait_ge(on_ready, n // 4)
                    nc.scalar.activation(sq_junk, og[:, tile(i % 4)], ACT.Square,
                                         accum_out=ssq[:, i % 4:i % 4 + 1]).then_inc(obsq_ready, 1)

                def rms_b(hd, hf):
                    n = 2 * hd + hf
                    act.wait_ge(obsq_ready, 4 * n + 4)
                    nc.scalar.activation(ssq[:], ssq[:], ACT.Ln, bias=eps_c[:, 0:1],
                                         scale=1.0 / DIFF_DV).then_inc(bln_ready, 1)
                    act.wait_ge(bln_ready, n + 1)
                    nc.scalar.activation(ssq[:], ssq[:], ACT.Exp, scale=-0.5).then_inc(brs_ready, 1)

                def exps(hd, i):
                    w = (i + 1) * P
                    act.wait_ge(nmx_ready, TT * hd + i + 1)
                    for m in range(2):
                        x = sc_b[i % 2][m][:, 0:w]
                        nc.scalar.activation(x, x, ACT.Exp, bias=nmx[:, i % 2, m:m + 1],
                                             accum_out=lsum[:, i % 2, m:m + 1]).then_inc(exp_ready, 1)

                def divide(hd, i):
                    act.wait_ge(comb_ready, TT * hd + i + 1)
                    x = sc_b[i % 2][0][:, 0:(i + 1) * P]
                    nc.scalar.activation(x, x, ACT.Copy, scale=rec[:, i % 2, 0:1]).then_inc(a_ready, 1)

                def high_a(hd, i):
                    for cc in range(i // 4 + 1):
                        n = chunk_at["T", hd, i, cc]
                        act.wait_ge(at_done, n + 1)
                        if n >= 2:
                            act.wait_ge(pv_done, n - 1)
                        w = width(i, cc)
                        copy(at_hi[n % 2][:, 0:w], ps[1 + ring_at["T", hd, i, cc] % 2][:, 0:w], athi_ready)

                act.wait_ge(unit_done, MB + U_HEAD + 1)
                for hf in range(2):
                    copy(v_t[1][:, half(hf)], ps[hf][:], vt_act)
                for j, hi in enumerate((dq_hi, dk_hi)):
                    act.wait_ge(unit_done, MB + U_HEAD + j + 2)
                    for hf in range(2):
                        copy(hi[:, half(hf)], ps[2 + 4 * j + hf][:], dqhi)
                for i in range(2):
                    exps(0, i)
                    divide(0, i)
                for hd in range(DIFF_H):
                    for i in range(TT):
                        if i < 2:
                            act.wait_ge(v_tr, GLA_H + 2 * hd + i + 1)
                            copy(dv[:, 4 * i:4 * i + 4, 0, :], ps[0][:].rearrange("p (t d) -> p t d", t=4), dvhi)
                        high_a(hd, i)
                        if i == 6:
                            fill_out(hd, i)
                        ahead = (hd, i + 2) if i + 2 < TT else (hd + 1, i + 2 - TT)
                        if ahead[0] < DIFF_H:
                            exps(*ahead)
                        if hd + i > 0:
                            squares_b(*((hd, i - 1) if i > 0 else (hd - 1, TT - 1)))
                        if i == 4:
                            rms_b(hd, 0)
                        if i == 0 and hd > 0:
                            rms_b(hd - 1, 1)
                        if i != 6:
                            fill_out(hd, i)
                        if ahead[0] < DIFF_H:
                            divide(*ahead)
                        if i == 5 and hd + 1 < DIFF_H:
                            act.wait_ge(s_done, pair_at[hd, TT - 1, 1] + 1)
                            copy(dq_hi[:, half(0)], raw_b[0], dqhi, q_scale(hd + 1))
                            copy(dk_hi[:, half(0)], raw_b[1], dqhi)
                squares_b(DIFF_H - 1, TT - 1)
                rms_b(DIFF_H - 1, 1)

                for br in range(2):
                    if br == 0:
                        act.wait_ge(rt_ready, 2 * GLA_H)
                        act.wait_ge(pv_done, chunk_at["T", DIFF_H - 1, TT - 1, 1] + 1)
                    else:
                        act.wait_ge(unit_done, MB + U_BRANCH + 12)
                    act.wait_ge(yb_ready, 2 * DIFF_H)
                    for j in range(4):
                        copy(y_hi[:, j, :], (ya if br == 0 else yb)[:, j, :], yhi_ready)
                    for m in range(KT):
                        act.wait_ge(unit_done, MB + U_BRANCH + 12 * br + 3 * (m // 2) + m % 2 + 1)
                        for hf in range(2):
                            n = 2 * KT * br + 2 * m + hf
                            if n >= 2:
                                act.wait_ge(zz_ready, n - 1)
                            nc.scalar.activation(sig_b[hf], ps[2 + 4 * (m % 2) + hf][:],
                                                 ACT.Sigmoid).then_inc(sig_ready, 1)
                act.wait_ge(unit_done, MB + U_BRANCH + 24)
                for k in range(KT):
                    for hf in range(2):
                        act.wait_ge(zz_ready, 2 * KT + 2 * k + hf + 1)
                        copy(u_hi[:, k, half(hf)], z[k][:, half(hf)], zhi_ready)
                act.wait_ge(res_ready, 2 * KT)

            act.wait_ge(lam_ps, 1)
            nc.scalar.activation(lams[:, 2:4], ps[5][:, 0:2], ACT.Exp).then_inc(lam_e, 1)
            act.wait_ge(vecT_ready, 1)
            nc.scalar.activation(c_act[:], fm("c"), ACT.Silu).then_inc(c_ready, 1)
            for i in range(0, 2 * TT, 2):
                t, k0 = i // 2, 0
                act.wait_ge(x_t, i + 1)
                nc.scalar.activation(h[:, k0:k0 + 4, t * P:(t + 1) * P],
                                     ps[i % 4][:].rearrange("p (k s) -> p k s", k=4), ACT.Copy).then_inc(h_act, 1)
            act.wait_ge(x_t, 2 * TT)
            act.wait_ge(h_act, TT)
            act.wait_ge(h_dve, TT)
            squares(0)
            modulate(0)
            ffn(0)
            act.wait_ge(acc_done, 2 * KT * GROUPS)
            squares(1)
            modulate(1)
            mixer()
            squares(2)
            modulate(2)
            ffn(1)
            act.wait_ge(acc_done, 2 * 2 * KT * GROUPS)
            squares(3)
            for i in range(0, 2 * TT, 2):
                t = i // 2
                act.wait_ge(y_t, i + 1)
                if t >= 2:
                    act.wait_ge(o_stored[t % 2], 16 * (t // 2))
                nc.scalar.activation(o_tile[t % 2][:, 0:HALF], ps[i % 4][:], ACT.Copy).then_inc(o_act, 1)

        @block.vector
        def _(dve):
            def chunk(m):
                for k in range(KT):
                    i = m * KT + k
                    dve.wait_ge(ada_in[k % ADA_SLOTS], 16 * (m * (KT // ADA_SLOTS) + k // ADA_SLOTS + 1))
                    if not (isinstance(i, int) and i == 0):
                        dve.wait_ge(ada_used, i)
                    if k == 0:
                        if not (isinstance(m, int) and m == 0):
                            dve.wait_ge(ada_sum, m)
                        nc.vector.tensor_scalar(ada_acc, ada_raw[:, 0, :], c_act[:, 0:1], None,
                                                ALU.mult).then_inc(ada_used, 1)
                    else:
                        nc.vector.scalar_tensor_tensor(ada_acc, ada_raw[:, k % ADA_SLOTS, :], c_act[:, k:k + 1],
                                                       ada_acc, ALU.mult, ALU.add).then_inc(ada_used, 1)

            def chunk_out(m):
                dve.wait_ge(ada_sum, m + 1)
                nc.vector.tensor_tensor(mod[:, bass.ds(m * KT, KT)], ps[7][:, 0:KT], vecT[:, bass.ds(m * KT, KT)],
                                        ALU.add).then_inc(mod_ready, 1)

            def scale(n, g):
                m = 3 * n + 1
                dve.wait_ge(mod_ready, m + 1)
                nc.vector.scalar_tensor_tensor(scale_c[:, n, :], mod[:, m * KT:(m + 1) * KT], 1.0, fm(g),
                                               ALU.add, ALU.mult).then_inc(scale_ready, 1)

            def norm(n):
                for i in range(2 * KT + 1):
                    if i < 2 * KT:
                        k, hf = i // 2, i % 2
                        j = n * 2 * KT + i
                        dve.wait_ge(rstd_ready, 2 * n + hf + 1)
                        if j >= 2:
                            dve.wait_ge(uhi_ready, j - 1)
                        nc.vector.tensor_tensor(xn_b[j % 2], h[:, k, hf * HALF:(hf + 1) * HALF], rstd[hf],
                                                ALU.mult).then_inc(xn_ready, 1)
                    if i >= 1:
                        k, hf = (i - 1) // 2, (i - 1) % 2
                        j = n * 2 * KT + i - 1
                        s = slice(hf * HALF, (hf + 1) * HALF)
                        dve.wait_ge(uhi_ready, j + 1)
                        nc.vector.tensor_tensor(u_lo[:, k, s], un_b[j % 2], u_hi[:, k, s].bitcast(F32),
                                                ALU.subtract).then_inc(ulo_ready, 1)

            def hidden(f, j, jj):
                t = f * FT + j
                dve.wait_ge(unit_done, gate_unit(f, j, jj) + 2)
                for hf in range(2):
                    s = slice(hf * HALF, (hf + 1) * HALF)
                    dve.wait_ge(silu_ready, 2 * t + hf + 1)
                    if hf == 0 and not (isinstance(t, int) and t == 0):
                        dve.wait_ge(hlo_ready, 2 * t)
                    nc.vector.tensor_tensor(prod_b[:, s], silu_b[:, s], ps[4 * jj + 2 + hf][:],
                                            ALU.mult).then_inc(prod_ready, 1)
                for hf in range(2):
                    s = slice(hf * HALF, (hf + 1) * HALF)
                    dve.wait_ge(hhi_ready, 2 * t + hf + 1)
                    nc.vector.tensor_tensor(hid_lo[:, jj, s], prod_b[:, s], hid_hi[:, jj, s].bitcast(F32),
                                            ALU.subtract).then_inc(hlo_ready, 1)

            def residual(f, g, last=False):
                for i in range(2 * KT):
                    hf, m = i // KT, i % KT
                    s = slice(hf * HALF, (hf + 1) * HALF)
                    if i < DOWN - 1:
                        dve.wait_ge(out_done, (DOWN - 1) * (f * GROUPS + g) + i + 1)
                    else:
                        dve.wait_ge(unit_done, unit0(f, g) + (10 if last is False else 8))
                    nc.vector.scalar_tensor_tensor(h[:, m, s], ps[4 + i % 4][:], gate_c[:, f, m:m + 1], h[:, m, s],
                                                   ALU.mult, ALU.add).then_inc(acc_done, 1)

            def ffn(f):
                if f == 0:
                    chunk(2)
                    chunk_out(2)
                    dve.wait_ge(mod_ready, 3)
                    nc.vector.tensor_scalar(gate_c[:, 0, :], mod[:, 2 * KT:3 * KT], 0.5, None, ALU.mult)
                hidden(f, 0, 0)

                def body(g, with_ada):
                    hidden(f, 2 * g - 1, 1)
                    if with_ada:
                        chunk(g + ADA_FIRST - 1)
                    residual(f, g - 1)
                    if with_ada:
                        chunk_out(g + ADA_FIRST - 1)
                    hidden(f, 2 * g, 0)
                first = 1
                if f == 0:
                    first = 1 + N_MOD - ADA_FIRST
                    with dve.Fori(1, first) as g:
                        body(g, True)
                with dve.Fori(first, GROUPS) as g:
                    body(g, False)
                hidden(f, FT - 1, 1)
                residual(f, GROUPS - 1, last=True)

            def low_part(out_, x, hi, done):
                nc.vector.tensor_tensor(out_, x, hi.bitcast(F32), ALU.subtract).then_inc(done, 1)

            def low_scaled(out_, x, scale, hi, done):
                nc.vector.scalar_tensor_tensor(out_, x, scale, hi.bitcast(F32), ALU.mult, ALU.subtract).then_inc(done, 1)

            def mixer():
                for b in range(4):
                    dve.wait_ge(lz_ready, b + 1)
                    nc.vector.scalar_tensor_tensor(la_b[b], ps[4 + b][:], 0.0, la_b[b], ALU.min,
                                                   ALU.subtract).then_inc(la_ready, 1)
                for b in range(4):
                    dve.wait_ge(lahi_ready, b + 1)
                    low_scaled(rar[:, 2 * S + b * HALF:2 * S + (b + 1) * HALF], la_b[b], 1.0 / GLA_TAU,
                               rar[:, b * HALF:(b + 1) * HALF], lalo_ready)
                dve.wait_ge(spill, 16)
                for j in range(2):
                    dve.wait_ge(unit_done, MB + U_GK + j + 1)
                    for hf in range(2):
                        nc.vector.tensor_copy(gk[j][:, half(hf)],
                                              ps[2 * ((U_GK + j) % 2) + hf][:]).then_inc(gqk_dve, 1)
                for hd in range(GLA_H + 1):
                    if hd < GLA_H:
                        dve.wait_ge(unit_done, MB + U_GV + hd + 1)
                        if hd >= 2:
                            dve.wait_ge(v_tr, hd - 1)
                        nc.vector.tensor_copy(v_t[hd % 2][:, half(1)],
                                              ps[2 * ((U_GV + hd) % 2) + 1][:]).then_inc(vt_dve, 1)
                    if hd >= 1:
                        dve.wait_ge(v_tr, hd)
                        nc.vector.tensor_copy(gv[:, 4:8, tile(hd - 1)],
                                              ps[5 + 2 * ((hd - 1) % 2)][:].rearrange("p (t d) -> p t d", t=4)
                                              ).then_inc(gv_dve, 1)

                def diagonal(t, c):
                    nc.vector.tensor_tensor(qk[c], gq[c][:, tile(t)], gk[c][:, tile(t)],
                                            ALU.mult).then_inc(qk_ready, 1)

                def scores(t, c):
                    dve.wait_ge(score_done, CT * t + c + 1)
                    if t >= 1:
                        dve.wait_ge(o_done, t)
                    for hh in range(2):
                        s_h = st[:, tile(2 * c + hh)]
                        nc.vector.tensor_scalar(s_h, ident[:], ps[6][:, 448 + hh:449 + hh], None,
                                                ALU.mult).then_inc(chain, 1)
                    n = (2 * LEVELS + 1) * (CT * t + c)
                    for l in range(LEVELS):
                        for hh in range(2):
                            cols = slice(l * P // 2, (l + 1) * P // 2)
                            dve.wait_ge(chain, n + 2 * l + hh + 1)
                            last = nc.vector.copy_predicated(second_halves(st[:, tile(2 * c + hh)], l),
                                                             blocks(mask[:, cols], l), blocks(ps[6 + hh][:, cols], l))
                            last.then_inc(pred_ready if (l, hh) == (LEVELS - 1, 1) else chain, 1)

                def update_state(t, c):
                    dve.wait_ge(kv_done, t + 1)
                    if t == 0:
                        nc.vector.tensor_copy(state[:, c, :], ps[0][:, tile(c)]).then_inc(state_ready, 1)
                    else:
                        nc.vector.scalar_tensor_tensor(state[:, c, :], state[:, c, :], dec[:, t % 2, c:c + 1],
                                                       ps[0][:, tile(c)], ALU.mult, ALU.add).then_inc(state_ready, 1)

                def norm_a(t):
                    dve.wait_ge(grs_ready, t + 1)
                    nc.vector.tensor_tensor(ya[:, :, tile(t)], og.rearrange("p (h t) -> p h t", h=GLA_H),
                                            og_rs.rearrange("p (h t) -> p h t", h=GLA_H), ALU.mult).then_inc(ya_ready, 1)

                dve.wait_ge(gqk_act, 4)
                dve.wait_ge(gqk_dve, 4)
                for c in range(CT):
                    diagonal(0, c)
                decay_products(dve, 0, 0, mult_dve)
                for t in range(TT):
                    for c in range(CT):
                        scores(t, c)
                        if t < TT - 1:
                            diagonal(t + 1, c)
                            if c == 0:
                                decay_products(dve, t + 1, 0, mult_dve)
                    if t < TT - 1:
                        for c in range(CT):
                            update_state(t, c)
                    if t > 0:
                        norm_a(t - 1)
                norm_a(TT - 1)

                def maxima(hd, i):
                    if i >= 2:
                        dve.wait_ge(at_done, chunk_at["T", hd, i - 2, (i - 2) // 4] + 1)
                    elif hd > 0:
                        dve.wait_ge(at_done, chunk_at["T", hd - 1, i - 2 + TT, 1] + 1)
                    if TT * hd + i >= 2:
                        dve.wait_ge(nmx_ready, TT * hd + i - 1)
                    for cc in range(i // 4 + 1):
                        n = pair_at[hd, i, cc]
                        w = width(i, cc)
                        c0 = S - P - i * P + cc * HALF
                        dve.wait_ge(s_done, n + 1)
                        if cc == 1:
                            dve.wait_ge(max_ready, 2 * n)
                        for m in range(2):
                            nc.vector.tensor_tensor_reduce(
                                out=sc_b[i % 2][m][:, cc * HALF:cc * HALF + w], in0=ps[4 + 2 * (n % 2) + m][:, 0:w],
                                in1=bias_b[:, c0:c0 + w], scale=DIFF_DH ** -0.5 / q_scale(hd),
                                scalar=-3e38 if cc == 0 else mx[:, i % 2, 0, m:m + 1], op0=ALU.add, op1=ALU.max,
                                accum_out=mx[:, i % 2, cc, m:m + 1]).then_inc(max_ready, 1)
                    dve.wait_ge(max_ready, 2 * n + 2)
                    if TT * hd + i >= 2:
                        dve.wait_ge(exp_ready, 2 * (TT * hd + i - 1))
                    nc.vector.tensor_scalar(nmx[:, i % 2, :], mx[:, i % 2, i // 4, :], -1.0, None,
                                            ALU.mult).then_inc(nmx_ready, 1)

                def combine(hd, i):
                    n = TT * hd + i
                    dve.wait_ge(exp_ready, 2 * n + 2)
                    if n >= 2:
                        dve.wait_ge(a_ready, n - 1)
                    nc.vector.reciprocal(rec[:, i % 2, :], lsum[:, i % 2, :]).then_inc(ratio_ready, 1)
                    dve.wait_ge(ratio_ready, 2 * n + 1)
                    nc.vector.scalar_tensor_tensor(ratio[:, i % 2:i % 2 + 1], lsum[:, i % 2, 0:1], rec[:, i % 2, 1:2],
                                                   lams[:, 5:6], ALU.mult, ALU.mult).then_inc(ratio_ready, 1)
                    dve.wait_ge(ratio_ready, 2 * n + 2)
                    w = (i + 1) * P
                    nc.vector.scalar_tensor_tensor(sc_b[i % 2][0][:, 0:w], sc_b[i % 2][1][:, 0:w],
                                                   ratio[:, i % 2:i % 2 + 1], sc_b[i % 2][0][:, 0:w],
                                                   ALU.mult, ALU.add).then_inc(comb_ready, 1)

                def low_a(hd, i):
                    for cc in range(i // 4 + 1):
                        n = chunk_at["T", hd, i, cc]
                        w = width(i, cc)
                        dve.wait_ge(athi_ready, n + 1)
                        low_part(at_lo[n % 2][:, 0:w], ps[1 + ring_at["T", hd, i, cc] % 2][:, 0:w],
                                 at_hi[n % 2][:, 0:w], atlo_ready)

                def gate_r(hd, hf):
                    dve.wait_ge(r_ready, 2 * hd + hf + 1)
                    nc.vector.scalar_tensor_tensor(ya[:, hd, half(hf)], ya[:, hd, half(hf)], gains[:, 0:1], r_b,
                                                   ALU.mult, ALU.mult).then_inc(rt_ready, 1)

                def out_b(hd, i):
                    n = TT * hd + i
                    dve.wait_ge(pv_done, chunk_at["T", hd, i, i // 4] + 1)
                    if i % 4 == 0 and n >= 4:
                        dve.wait_ge(on_ready, n // 4)
                    nc.vector.tensor_copy(og[:, tile(i % 4)], ps[3][:, 0:P]).then_inc(oh_ready, 1)
                    dve.wait_ge(oh_ready, n + 1)
                    nc.vector.tensor_tensor(og[:, tile(i % 4)], og[:, tile(i % 4)], ps[3][:, P:2 * P],
                                            ALU.add).then_inc(ob_ready, 1)

                def norm_b(hd, hf):
                    n = 2 * hd + hf
                    dve.wait_ge(brs_ready, n + 1)
                    if n >= 1:
                        dve.wait_ge(on_t, n)
                    nc.vector.tensor_tensor(on.rearrange("p (t d) -> p t d", t=4), og.rearrange("p (t d) -> p t d", t=4),
                                            ssq[:].rearrange("p (t o) -> p t o", o=1).broadcast_to([P, 4, P]),
                                            ALU.mult).then_inc(on_ready, 1)

                def keep_b(hd, hf):
                    dve.wait_ge(on_t, 2 * hd + hf + 1)
                    nc.vector.tensor_scalar(yb[:, hd, half(hf)], ps[1 + ring_at["out", hd, hf] % 2][:], gains[:, 1:2],
                                            None, ALU.mult).then_inc(yb_ready, 1)

                def fill_out(hd, i):
                    what, hf = fill_of(hd, i)
                    if what == "r":
                        gate_r(hd, hf)
                    elif what in ("q", "k") and hf == 1:
                        dve.wait_ge(dqhi, 4 * (hd + 1) + (3 if what == "q" else 4))
                        if what == "q":
                            low_scaled(dq_lo[:, half(1)], ps[0][:], q_scale(hd + 1), dq_hi[:, half(1)], dqlo)
                        else:
                            low_part(dk_lo[:, half(1)], ps[0][:], dk_hi[:, half(1)], dqlo)

                dve.wait_ge(lam_ready, 2)
                for j, (lo, hi) in enumerate(((dq_lo, dq_hi), (dk_lo, dk_hi))):
                    for hf in range(2):
                        dve.wait_ge(dqhi, 2 * j + hf + 1)
                        low_part(lo[:, half(hf)], ps[2 + 4 * j + hf][:], hi[:, half(hf)], dqlo)
                dve.wait_ge(bias_ready, 3)
                for i in range(2):
                    maxima(0, i)
                    combine(0, i)
                for hd in range(DIFF_H):
                    for i in range(TT):
                        if i < 2:
                            dve.wait_ge(dvhi, 2 * hd + i + 1)
                            low_part(dv[:, 4 * i:4 * i + 4, 1, :], ps[0][:].rearrange("p (t d) -> p t d", t=4),
                                     dv[:, 4 * i:4 * i + 4, 0, :], dvlo)
                        if hd + i > 0:
                            out_b(*((hd, i - 1) if i > 0 else (hd - 1, TT - 1)))
                        low_a(hd, i)
                        if i == 5:
                            keep_b(hd, 0)
                        if i == 1 and hd > 0:
                            keep_b(hd - 1, 1)
                        if i == 6:
                            fill_out(hd, i)
                        ahead = (hd, i + 2) if i + 2 < TT else (hd + 1, i + 2 - TT)
                        if ahead[0] < DIFF_H:
                            maxima(*ahead)
                            combine(*ahead)
                        if i == 4:
                            norm_b(hd, 0)
                        if i == 0 and hd > 0:
                            norm_b(hd - 1, 1)
                        if i != 6:
                            fill_out(hd, i)
                        if i == 5 and hd + 1 < DIFF_H:
                            dve.wait_ge(dqhi, 4 * (hd + 1) + 1)
                            low_scaled(dq_lo[:, half(0)], raw_b[0], q_scale(hd + 1), dq_hi[:, half(0)], dqlo)
                            dve.wait_ge(dqhi, 4 * (hd + 1) + 2)
                            low_part(dk_lo[:, half(0)], raw_b[1], dk_hi[:, half(0)], dqlo)
                out_b(DIFF_H - 1, TT - 1)
                norm_b(DIFF_H - 1, 1)
                keep_b(DIFF_H - 1, 1)

                for br in range(2):
                    y = ya if br == 0 else yb
                    for j in range(4):
                        dve.wait_ge(yhi_ready, 4 * br + j + 1)
                        low_part(y_lo[:, j, :], y[:, j, :], y_hi[:, j, :], ylo_ready)
                    for m in range(KT):
                        i = m // 2
                        if m % 2 == 0:
                            dve.wait_ge(pa_done, 4 * br + i + 1)
                        else:
                            dve.wait_ge(unit_done, MB + U_BRANCH + 12 * br + 3 * i + 3)
                        for hf in range(2):
                            n = 2 * KT * br + 2 * m + hf
                            dve.wait_ge(sig_ready, n + 1)
                            product = ps[4 * (m % 2) + hf][:]
                            if br == 0:
                                nc.vector.tensor_tensor(z[m][:, half(hf)], sig_b[hf], product,
                                                        ALU.mult).then_inc(zz_ready, 1)
                            else:
                                nc.vector.tensor_tensor(sig_b[hf], sig_b[hf], product, ALU.mult).then_inc(gz_ready, 1)
                                dve.wait_ge(gz_ready, 2 * m + hf + 1)
                                nc.vector.tensor_tensor(z[m][:, half(hf)], z[m][:, half(hf)], sig_b[hf],
                                                        ALU.add).then_inc(zz_ready, 1)
                for k in range(KT):
                    for hf in range(2):
                        dve.wait_ge(zhi_ready, 2 * k + hf + 1)
                        low_part(u_lo[:, k, half(hf)], z[k][:, half(hf)], u_hi[:, k, half(hf)], zlo_ready)
                dve.wait_ge(h_back, 16)
                for m in range(KT):
                    dve.wait_ge(unit_done, MB + U_OUT + m + 1)
                    for hf in range(2):
                        nc.vector.scalar_tensor_tensor(h[:, m, half(hf)], ps[2 * (m % 4) + hf][:],
                                                       mod[:, 5 * KT + m:5 * KT + m + 1], h[:, m, half(hf)],
                                                       ALU.mult, ALU.add).then_inc(res_ready, 1)

            dve.wait_ge(lam_in, 64)
            for j in range(2):
                nc.vector.tensor_tensor_reduce(out=lamj[:], in0=lamv[0:1, 2 * j, :], in1=lamv[0:1, 2 * j + 1, :],
                                               scale=1.0, scalar=0.0, op0=ALU.mult, op1=ALU.add,
                                               accum_out=lams[0:1, j:j + 1]).then_inc(lam_s, 1)
                dve.wait_ge(lam_s, j + 1)
            dve.wait_ge(lam_e, 1)
            nc.vector.tensor_tensor(lams[:, 4:5], lams[:, 3:4], lams[:, 2:3], ALU.subtract).then_inc(lam_ready, 1)
            dve.wait_ge(lam_ready, 1)
            nc.vector.tensor_scalar(lams[:, 5:6], lams[:, 4:5], -LAM_INIT, None, ALU.add).then_inc(lam_ready, 1)
            dve.wait_ge(vec_t, 1)
            nc.vector.tensor_copy(vecT[:, 0:N_ROWS], ps[4][:, 0:N_ROWS]).then_inc(vecT_ready, 1)
            dve.wait_ge(vecT_ready, 1)
            nc.vector.tensor_copy(gains[:, 0:1], fm("gla_head_norm")).then_inc(gains_ready, 1)
            nc.vector.tensor_scalar(gains[:, 1:2], fm("diff_head_norm"), 1.0 - LAM_INIT, None,
                                    ALU.mult).then_inc(gains_ready, 1)
            dve.wait_ge(gains_ready, 2)
            for i in range(1, 2 * TT, 2):
                t = i // 2
                dve.wait_ge(x_t, i + 1)
                nc.vector.tensor_copy(h[:, 4:8, t * P:(t + 1) * P],
                                      ps[i % 4][:].rearrange("p (k s) -> p k s", k=4)).then_inc(h_dve, 1)
            dve.wait_ge(c_ready, 1)
            chunk(0)
            chunk_out(0)
            chunk(1)
            chunk_out(1)
            scale(0, "ffn1_norm")
            norm(0)
            ffn(0)
            scale(1, "mix_norm")
            scale(2, "ffn2_norm")
            nc.vector.tensor_scalar(gate_c[:, 1, :], mod[:, 8 * KT:9 * KT], 0.5, None, ALU.mult)
            norm(1)
            mixer()
            norm(2)
            ffn(1)
            for hf in range(2):
                dve.wait_ge(rstd_ready, 6 + hf + 1)
                for k in range(KT):
                    s = slice(hf * HALF, (hf + 1) * HALF)
                    g0 = ROWS["final_norm"][0] + k
                    nc.vector.scalar_tensor_tensor(h[:, k, s], h[:, k, s], vecT[:, g0:g0 + 1], rstd[hf],
                                                   ALU.mult, ALU.mult).then_inc(y_ready, 1)
            for i in range(1, 2 * TT, 2):
                t = i // 2
                dve.wait_ge(y_t, i + 1)
                if t >= 2:
                    dve.wait_ge(o_stored[t % 2], 16 * (t // 2))
                nc.vector.tensor_copy(o_tile[t % 2][:, HALF:S], ps[i % 4][:]).then_inc(o_dve, 1)

        @block.tensor
        def _(pe):
            def mean_square(n):
                for hf in range(2):
                    for k in range(KT):
                        pe.wait_ge(sq_ready, n * 2 * KT + hf * KT + k + 1)
                        nc.tensor.matmul(ps[6 + hf][:], ones[:], sq_b[k % 2], start=(k == 0),
                                         stop=(k == KT - 1)).then_inc(sq_used, 1)

            def column_sums(m):
                pe.wait_ge(ada_used, (m + 1) * KT)
                for j in range(KT):
                    mm = nc.tensor.matmul(ps[7][:, j:j + 1], ada_acc[:, j * P:(j + 1) * P], ones[:, 0:1],
                                          start=True, stop=True)
                mm.then_inc(ada_sum, 1)

            def project(n, slot, bank, first=None, made=ulo_ready):
                pe.wait_ge(w_split, n + 1)
                for k in range(KT):
                    if first is not None:
                        pe.wait_ge(made, first + 2 * k + 2)
                    c = slice(k * P, (k + 1) * P)
                    for w, u in ((w_hi, u_hi), (w_hi, u_lo), (w_lo, u_hi)):
                        for hf in range(2):
                            mm = nc.tensor.matmul(ps[bank + hf][:], w[:, slot, c], u[:, k, hf * HALF:(hf + 1) * HALF],
                                                  start=(k == 0 and u is u_hi and w is w_hi),
                                                  stop=(k == KT - 1 and w is w_lo))
                return mm

            def hidden_in(f, j, jj, n, slot, first=None):
                mm = project(n, slot % SLOTS, 4 * jj, first)
                mm.then_inc(unit_done, 1)
                if f == 0 and isinstance(j, int) and j == 1:
                    pe.wait_ge(mod_ready, 3)
                mm = project(n + 1, (slot + 1) % SLOTS, 4 * jj + 2)
                mm.then_inc(unit_done, 1)

            def down(f, g, n, slot):
                pe.wait_ge(w_split, n + 2)
                pe.wait_ge(hlo_ready, 2 * (f * FT + 2 * g + 2))
                for i in range(2 * KT):
                    hf, m = i // KT, i % KT
                    s = slice(hf * HALF, (hf + 1) * HALF)
                    if i >= 4:
                        pe.wait_ge(acc_done, 2 * KT * (f * GROUPS + g) + i - 3)
                    for j in range(2):
                        c = slice(m * P, (m + 1) * P)
                        for q, (w, x) in enumerate(((w_hi, hid_hi), (w_hi, hid_lo), (w_lo, hid_hi))):
                            mm = nc.tensor.matmul(ps[4 + i % 4][:], w[:, (slot + j) % SLOTS, c], x[:, j, s],
                                                  start=(j == 0 and q == 0), stop=(j == 1 and q == 2))
                    if i < DOWN - 1:
                        mm.then_inc(out_done, 1)
                mm.then_inc(unit_done, 2)

            def ffn(f):
                t0 = f * FT
                hidden_in(f, 0, 0, BASE[f], 0, f * 4 * KT)
                if f == 0:
                    column_sums(2)
                hidden_in(f, 1, 1, BASE[f] + 2, 2)

                def body(g, with_ada):
                    n = unit0(f, g)
                    pe.wait_ge(prod_ready, 2 * (t0 + 2 * g - 1))
                    hidden_in(f, 2 * g, 0, n, 1)
                    down(f, g - 1, n + 2, 0)
                    pe.wait_ge(acc_done, 2 * KT * (f * GROUPS + g))
                    if with_ada:
                        column_sums(g + ADA_FIRST - 1)
                    mm = project(n + 4, 2, 4)
                    mm.then_inc(unit_done, 1)
                    if with_ada:
                        pe.wait_ge(mod_ready, g + ADA_FIRST)
                    mm = project(n + 5, 0, 6)
                    mm.then_inc(unit_done, 1)
                first = 1
                if f == 0:
                    first = 1 + N_MOD - ADA_FIRST
                    with pe.Fori(1, first) as g:
                        body(g, True)
                with pe.Fori(first, GROUPS) as g:
                    body(g, False)
                down(f, GROUPS - 1, unit0(f, GROUPS), 1)

            def three(out_, w, x, start, stop):
                for q, (i, j) in enumerate(((0, 0), (0, 1), (1, 0))):
                    mm = nc.tensor.matmul(out_, w[i], x[j], start=(start and q == 0), stop=(stop and q == 2))
                return mm

            def mixer():
                pe.wait_ge(rstd_ready, 4)
                project(MB, 0, 0, 2 * KT).then_inc(unit_done, 1)
                free = [None, (low_ready, 2), (gqk_act, 2), (gqk_act, 4), (gqk_dve, 2), (gqk_dve, 4)]

                def unit(u):
                    if 2 <= u <= 6:
                        pe.wait_ge(*free[u - 1])
                    elif u > 6:
                        pe.wait_ge(vt_act, u - 6)
                        pe.wait_ge(vt_dve, u - 6)
                    project(MB + u, u % SLOTS, 2 * (u % 2)).then_inc(unit_done, 1)

                def turn_v(src, bank, gate):
                    for t in range(TT):
                        mm = nc.tensor.transpose(ps[bank + t // 4][:, tile(t % 4)], src[:, tile(t)], ident[:])
                        if gate and t % 4 == 3:
                            mm.then_inc(v_tr, 1)
                    if not gate:
                        mm.then_inc(v_tr, 1)

                unit(1)
                pe.wait_ge(low_ready, 2)
                pe.wait_ge(w2_in, 32)
                for t in range(TT):
                    mm = nc.tensor.matmul(ps[4 + t // 2][:, (t % 2) * KW:(t % 2 + 1) * KW], low[:, tile(t)], w2b[:],
                                          start=True, stop=True)
                    if t % 2:
                        mm.then_inc(z_done, 1)
                for u in range(2, U_GV + 1):
                    unit(u)
                pe.wait_ge(la_ready, 4)
                for hd in range(GLA_H):
                    if hd + 1 < GLA_H:
                        unit(U_GV + hd + 1)
                    pe.wait_ge(vt_act, hd + 1)
                    pe.wait_ge(vt_dve, hd + 1)
                    if hd >= 2:
                        pe.wait_ge(gv_act, hd - 1)
                        pe.wait_ge(gv_dve, hd - 1)
                    turn_v(v_t[hd % 2], 4 + 2 * (hd % 2), False)
                pe.wait_ge(gv_act, GLA_H)
                pe.wait_ge(gv_dve, GLA_H)

                def free_piece(n):
                    if n >= 2:
                        pe.wait_ge(piece_used, n - 1)

                def decays(t, c):
                    for p in range(3):
                        n = piece_at["E", t, c, p]
                        free_piece(n)
                        lo, hi = p * HALF, min((p + 1) * HALF, EC)
                        for q, la in enumerate((la_hi, la_lo)):
                            mm = nc.tensor.matmul(ps[4 + n % 2][:, 0:hi - lo], la[:, t, tile(c)], cum[:, lo:hi],
                                                  start=(q == 0), stop=(q == 1))
                        mm.then_inc(piece_ready, 1)

                def scores(t, c):
                    pe.wait_ge(mult_dve if c == 0 else mult_pool, t + 1)
                    pe.wait_ge(qk_ready, CT * t + c + 1)
                    if t + c > 0:
                        pe.wait_ge(pred_ready, CT * t + c)
                    nc.tensor.matmul(ps[6][:, 448:450], qk[c], heads2[:], start=True, stop=True)
                    for l in range(LEVELS):
                        for hh in range(2):
                            ch = slice(hh * GLA_DK, (hh + 1) * GLA_DK)
                            e = ed[c][ch, l * P:(l + 1) * P]
                            mm = nc.tensor.matmul(blocks(ps[6 + hh][:, l * P // 2:(l + 1) * P // 2], l), e,
                                                  second_halves(e, l), start=True, stop=True)
                    mm.then_inc(score_done, 1)
                    if t > 0:
                        pe.wait_ge(state_ready, CT * (t - 1) + c + 1)
                        if c == 0:
                            pe.wait_ge(og_ready, 2 * t)
                        for hh in range(2):
                            ch = slice(hh * GLA_DK, (hh + 1) * GLA_DK)
                            nc.tensor.matmul(ps[2 + hh][:, tile(c)], state[ch, c, :], ed[c][ch, LEVELS * P:(LEVELS + 1) * P],
                                             start=(c == 0), stop=False, skip_group_check=True)
                    if t < TT - 1:
                        n = piece_at["T", t, c]
                        free_piece(n)
                        nc.tensor.transpose(ps[4 + n % 2][:, 0:P], ed[c][:, (LEVELS + 1) * P:EC],
                                            ident[:]).then_inc(piece_ready, 1)

                def sum_squares(t):
                    n = piece_at["ms", t]
                    free_piece(n)
                    pe.wait_ge(ogsq_ready, t + 1)
                    nc.tensor.matmul(ps[4 + n % 2][:], ones[:], og_sq, start=True, stop=True).then_inc(piece_ready, 1)

                pe.wait_ge(lalo_ready, 4)
                for c in range(CT):
                    decays(0, c)
                for t in range(TT):
                    for c in range(CT):
                        scores(t, c)
                        if t < TT - 1:
                            decays(t + 1, c)
                    if t < TT - 1:
                        pe.wait_ge(piece_used, piece_at["T", t, 1] + 1)
                        for c in range(CT):
                            for hh in range(2):
                                ch = slice(hh * GLA_DK, (hh + 1) * GLA_DK)
                                mm = nc.tensor.matmul(ps[0][ch, tile(c)], kd[:, c * P + hh * GLA_DK:c * P + (hh + 1) * GLA_DK],
                                                      gv[:, t, tile(2 * c + hh)], start=True, stop=True)
                        mm.then_inc(kv_done, 1)
                    if t > 0:
                        sum_squares(t - 1)
                    pe.wait_ge(pred_ready, CT * (t + 1))
                    for c in range(CT):
                        for hh in range(2):
                            mm = nc.tensor.matmul(ps[2 + hh][:, tile(c)], gv[:, t, tile(2 * c + hh)], st[:, tile(2 * c + hh)],
                                                  start=(t == 0), stop=True, skip_group_check=True)
                    mm.then_inc(o_done, 1)
                sum_squares(TT - 1)

                def key_scores(hd, i):
                    for cc in range(i // 4 + 1):
                        n = pair_at[hd, i, cc]
                        if n >= 2:
                            pe.wait_ge(max_ready, 2 * (n - 1))
                        w = width(i, cc)
                        for q, (x, y) in enumerate(((dq_hi, dk_hi), (dq_hi, dk_lo), (dq_lo, dk_hi))):
                            for m in range(2):
                                ch = slice(m * DIFF_DH, (m + 1) * DIFF_DH)
                                mm = nc.tensor.matmul(ps[4 + 2 * (n % 2) + m][:, 0:w], x[ch, tile(i)],
                                                      y[ch, cc * HALF:cc * HALF + w], start=(q == 0), stop=(q == 2))
                        mm.then_inc(s_done, 1)

                def free_ring(n):
                    if n >= 2:
                        what = ring[n - 2]
                        if what[0] == "T":
                            pe.wait_ge(atlo_ready, chunk_at[what] + 1)
                        else:
                            pe.wait_ge(yb_ready, 2 * what[1] + what[2] + 1)

                def turn_a(hd, i):
                    pe.wait_ge(a_ready, TT * hd + i + 1)
                    for cc in range(i // 4 + 1):
                        n = ring_at["T", hd, i, cc]
                        free_ring(n)
                        for j in range(width(i, cc) // P):
                            mm = nc.tensor.transpose(ps[1 + n % 2][:, tile(j)], sc_b[i % 2][0][:, tile(4 * cc + j)], ident[:])
                        mm.then_inc(at_done, 1)

                def values(hd, i):
                    if hd + i > 0:
                        pe.wait_ge(ob_ready, TT * hd + i)
                    if i in (0, 4):
                        pe.wait_ge(dvlo, 2 * hd + i // 4 + 1)
                    for cc in range(i // 4 + 1):
                        n = chunk_at["T", hd, i, cc]
                        pe.wait_ge(atlo_ready, n + 1)
                        for j in range(width(i, cc) // P):
                            kb = 4 * cc + j
                            for q, at in enumerate((at_hi, at_lo)):
                                mm = nc.tensor.matmul(ps[3][:, 0:2 * P], at[n % 2][:, tile(j)],
                                                      dv[:, kb].rearrange("p two d -> p (two d)"),
                                                      start=(kb == 0 and q == 0), stop=(kb == i and q == 1))
                        mm.then_inc(pv_done, 1)

                def turn_out(hd, hf):
                    n = ring_at["out", hd, hf]
                    free_ring(n)
                    pe.wait_ge(on_ready, 2 * hd + hf + 1)
                    for t in range(4):
                        mm = nc.tensor.transpose(ps[1 + n % 2][:, tile(t)], on[:, tile(t)], ident[:])
                    mm.then_inc(on_t, 1)

                def turn_v_half(hd, hf):
                    if hf == 1:
                        pe.wait_ge(r_ready, 2 * hd + 1)
                    elif hd == 0:
                        pe.wait_ge(vt_act, GLA_H + 2)
                    else:
                        pe.wait_ge(dqlo, 4 * hd + 4)
                    for t in range(4):
                        mm = nc.tensor.transpose(ps[0][:, tile(t)], v_t[1][:, tile(4 * hf + t)], ident[:])
                    mm.then_inc(v_tr, 1)

                def fill(hd, i):
                    what, hf = fill_of(hd, i)
                    if what is None:
                        return
                    if i < 2:
                        pe.wait_ge(dvlo, 2 * hd + i + 1)
                    elif i == 2:
                        pe.wait_ge(r_ready, 2 * hd + 2)
                    elif i in (3, 4):
                        pe.wait_ge(raw_ready, 2 * hd + i - 2)
                    elif i in (5, 6):
                        pe.wait_ge(vt_act, GLA_H + 2 * (hd + 1) + i - 4)
                    else:
                        pe.wait_ge(dqlo, 4 * (hd + 1) + 3)
                    u = r_unit(hd) + FILL_UNIT[what]
                    if hf == 0:
                        pe.wait_ge(w_split, MB + u + 1)
                    for k in range(KT):
                        mm = three(ps[0][:], (w_hi[:, u % SLOTS, tile(k)], w_lo[:, u % SLOTS, tile(k)]),
                                   (u_hi[:, k, half(hf)], u_lo[:, k, half(hf)]), k == 0, k == KT - 1)
                    if i in (1, 6):
                        mm.then_inc(unit_done, 1)
                    elif i == 7:
                        mm.then_inc(unit_done, 2)
                    else:
                        mm.then_inc(fill_done, 1)

                pe.wait_ge(state_ready, CT * (TT - 1))
                project(MB + U_HEAD, U_HEAD % SLOTS, 0).then_inc(unit_done, 1)
                pe.wait_ge(og_ready, 2 * TT)
                project(MB + U_HEAD + 1, (U_HEAD + 1) % SLOTS, 2).then_inc(unit_done, 1)
                project(MB + U_HEAD + 2, (U_HEAD + 2) % SLOTS, 6).then_inc(unit_done, 1)
                pe.wait_ge(piece_used, len(pieces))
                turn_v_half(0, 0)
                pe.wait_ge(dqlo, 4)
                key_scores(0, 0)
                key_scores(0, 1)
                for hd in range(DIFF_H):
                    for i in range(TT):
                        if i == 1 or (i == 0 and hd > 0):
                            turn_v_half(hd, i)
                        turn_a(hd, i)
                        if i == 5:
                            turn_out(hd, 0)
                        if i == 1 and hd > 0:
                            turn_out(hd - 1, 1)
                        if i == 6:
                            fill(hd, i)
                        if i == 6 and hd + 1 < DIFF_H:
                            pe.wait_ge(dqlo, 4 * (hd + 1) + 2)
                        if i == 2 and hd > 0:
                            pe.wait_ge(dqlo, 4 * hd + 4)
                        ahead = (hd, i + 2) if i + 2 < TT else (hd + 1, i + 2 - TT)
                        if ahead[0] < DIFF_H:
                            key_scores(*ahead)
                        if i != 6:
                            fill(hd, i)
                        values(hd, i)
                turn_out(DIFF_H - 1, 1)

                for br in range(2):
                    for i in range(4):
                        u = U_BRANCH + 12 * br + 3 * i
                        for j in range(2):
                            m = 2 * i + j
                            n = 2 * KT * br + 2 * m
                            if n >= 4:
                                pe.wait_ge(sig_ready, n - 2)
                            elif j == 0:
                                pe.wait_ge(ob_ready, TT * DIFF_H)
                                pe.wait_ge(yb_ready, 2 * DIFF_H)
                            project(MB + u + j, (u + j) % SLOTS, 2 + 4 * j).then_inc(unit_done, 1)
                        if i == 0:
                            pe.wait_ge(ylo_ready, 4 * br + 4)
                        pe.wait_ge(w_split, MB + u + 3)
                        for j in range(2):
                            m = 2 * i + j
                            n = 2 * KT * br + 2 * m
                            if n >= 4:
                                pe.wait_ge(zz_ready, n - 2)
                            slot = (u + 2) % SLOTS
                            for k in range(4):
                                c = slice(k * 2 * P + j * P, k * 2 * P + (j + 1) * P)
                                for hf in range(2):
                                    mm = three(ps[4 * j + hf][:], (w_hi[:, slot, c], w_lo[:, slot, c]),
                                               (y_hi[:, k, half(hf)], y_lo[:, k, half(hf)]), k == 0, k == 3)
                            mm.then_inc(pa_done if j == 0 else unit_done, 1)
                pe.wait_ge(zz_ready, 4 * KT)
                for m in range(KT):
                    if m >= 4:
                        pe.wait_ge(res_ready, 2 * (m - 3))
                    project(MB + U_OUT + m, (U_OUT + m) % SLOTS, 2 * (m % 4), 0 if m == 0 else None,
                            zlo_ready).then_inc(unit_done, 1)

            pe.wait_ge(const_ready, 6 + 6 * LEVELS + 4)
            pe.wait_ge(lam_s, 2)
            nc.tensor.matmul(ps[5][:, 0:2], ones[0:1, :], lams[0:1, 0:2], start=True, stop=True).then_inc(lam_ps, 1)
            pe.wait_ge(vec_in, 16 * len(ROWS))
            nc.tensor.transpose(ps[4][:, 0:N_ROWS], vec[0:N_ROWS, :], ident[0:N_ROWS, 0:N_ROWS]).then_inc(vec_t, 1)
            for i in range(2 * TT):
                t, k0 = i // 2, 4 * (i % 2)
                if i % 2 == 0:
                    pe.wait_ge(x_in[t % 4], 16 * (t // 4 + 1))
                if i >= 4:
                    pe.wait_ge(h_act if i % 2 == 0 else h_dve, (i - 4) // 2 + 1)
                for k in range(k0, k0 + 4):
                    mm = nc.tensor.transpose(ps[i % 4][:, (k - k0) * P:(k - k0 + 1) * P],
                                             x_tile[t % 4][:, k * P:(k + 1) * P], ident[:])
                mm.then_inc(x_t, 1)
            mean_square_first = mean_square
            column_sums(0)
            pe.wait_ge(mod_ready, 1)
            column_sums(1)
            pe.wait_ge(mod_ready, 2)
            mean_square_first(0)
            ffn(0)
            mean_square(1)
            mixer()
            mean_square(2)
            ffn(1)
            mean_square(3)
            for i in range(2 * TT):
                t, k0 = i // 2, 4 * (i % 2)
                if i == 0:
                    pe.wait_ge(y_ready, KT)
                if t == TT // 2:
                    pe.wait_ge(y_ready, 2 * KT)
                if i >= 4:
                    pe.wait_ge(o_act if i % 2 == 0 else o_dve, (i - 4) // 2 + 1)
                for k in range(k0, k0 + 4):
                    mm = nc.tensor.transpose(ps[i % 4][:, (k - k0) * P:(k - k0 + 1) * P],
                                             h[:, k, t * P:(t + 1) * P], ident[:])
                mm.then_inc(y_t, 1)


NAMES = ["x", "c", "w_ada", "b_ada", "ffn1_norm", "ffn1_w_in", "ffn1_w_out", "mix_norm", "w_in",
         "gla_alpha_w2", "gla_alpha_b", "gla_head_norm", "diff_lq1", "diff_lk1", "diff_lq2", "diff_lk2",
         "diff_head_norm", "w_branch_a", "w_branch_b", "w_out", "ffn2_norm", "ffn2_w_in", "ffn2_w_out",
         "final_norm"]


def kernel(**inputs):
    import concourse.bacc as bacc
    from concourse.bass_utils import run_bass_kernel_spmd

    nc = bacc.Bacc("TRN2", target_bir_lowering=False, num_devices=1)
    arrays, args = {}, {}
    for name in NAMES:
        arr = np.ascontiguousarray(inputs[name])
        arrays[f"in_{name}"] = arr
        args[name] = nc.dram_tensor(f"in_{name}", arr.shape, mybir.dt.from_np(arr.dtype), kind="ExternalInput").ap()
    out = nc.dram_tensor("out_h", (1, S, D), F32, kind="ExternalOutput").ap()
    build_program(nc, args, out)
    result = run_bass_kernel_spmd(nc, [arrays], core_ids=[0])
    return result.results[0]["out_h"]
```

```python
import numpy as np
import concourse.bass as bass
from concourse import mybir
from contextlib import ExitStack

F32 = mybir.dt.float32
F32R = mybir.dt.float32r
I32 = mybir.dt.int32
ALU = mybir.AluOpType
ACT = mybir.ActivationFunctionType
AX = mybir.AxisListType

P = 128
D = 1024
S = 1024
KT = D // P
TT = S // P
HALF = S // 2
D_FF = 2816
FT = D_FF // P
GROUPS = FT // 2
DOWN = 2 * KT
EPS = 1e-6
N_MOD = 9
ADA_FIRST = 3
SLOTS = 3
ADA_SLOTS = 4
FFN_UNITS = 3 * FT
GLA_H, GLA_DK, GLA_DV, GLA_RANK, GLA_TAU = 4, 64, 128, 16, 16.0
DIFF_H, DIFF_DH, DIFF_DV, ALIBI = 4, 64, 128, 8.0
LAM_INIT = 0.2
KW, VW = GLA_H * GLA_DK, GLA_H * GLA_DV
QW, DVW = DIFF_H * 2 * DIFF_DH, DIFF_H * DIFF_DV
C_GQ, C_GK, C_GV, C_GR = 0, KW, 2 * KW, 2 * KW + VW
C_GA = C_GR + VW
C_DQ = C_GA + GLA_RANK
C_DK, C_DV = C_DQ + QW, C_DQ + 2 * QW
C_GATE = C_DV + DVW
CT = KW // P
LEVELS = 7
EC = (LEVELS + 2) * P
U_GA, U_GQ, U_GK, U_GV = 0, 1, 3, 5
U_HEAD, U_BRANCH = 9, 25
U_OUT = U_BRANCH + 24
MIX_UNITS = U_OUT + KT
EARLY = 3
_order = [("gate", 0, m) for m in range(EARLY)] + [("w", 0, 0), ("gate", 0, 3), ("w", 0, 1)]
for _br in range(2):
    for _i in range(0 if _br else 2, 4):
        _order += [("gate", _br, 2 * _i), ("gate", _br, 2 * _i + 1), ("w", _br, _i)]
BRANCH_UNIT = {what: U_BRANCH + n for n, what in enumerate(_order)}
MB = FFN_UNITS
BASE = [0, FFN_UNITS + MIX_UNITS]
ROWS = {}
_n = 0
for _name, _rows in (("b_ada", N_MOD * KT), ("ffn1_norm", KT), ("mix_norm", KT), ("ffn2_norm", KT),
                     ("final_norm", KT), ("c", KT), ("gla_head_norm", 1), ("diff_head_norm", 1)):
    ROWS[_name] = (_n, _n + _rows)
    _n += _rows
N_ROWS = _n


def build_program(nc, a, out):
    ctx = ExitStack()
    with ctx:
        def sb(name, shape, dt=F32):
            return ctx.enter_context(nc.sbuf_tensor(name, shape, dt))

        def sem(name):
            return ctx.enter_context(nc.semaphore(name))

        h = sb("h", [P, KT, S])
        u_hi = sb("u_hi", [P, KT, S], F32R)
        u_lo = sb("u_lo", [P, KT, S], F32R)
        w_raw = sb("w_raw", [P, SLOTS, D])
        w_hi = sb("w_hi", [P, SLOTS, D], F32R)
        w_lo = sb("w_lo", [P, SLOTS, D], F32R)
        ident = sb("ident", [P, P])
        ones = sb("ones", [P, P])
        vec = sb("vec", [P, P])
        vecT = sb("vecT", [P, P])
        mod = sb("mod", [P, N_MOD * KT])
        scale_c = sb("scale_c", [P, 3, KT])
        gate_c = sb("gate_c", [P, 2, KT])
        c_act = sb("c_act", [P, KT])
        eps_c = sb("eps_c", [P, 1])
        rar = sb("rar", [P, 8 * S], F32R)
        far = sb("far", [P, 9 * S])

        hid_hi = rar[:, 0:2 * S].rearrange("p (j s) -> p j s", j=2)
        hid_lo = rar[:, 2 * S:4 * S].rearrange("p (j s) -> p j s", j=2)
        silu_b = far[:, 0:S]
        prod_b = far[:, S:2 * S]
        ada_raw = far[:, 2 * S:6 * S].rearrange("p (j s) -> p j s", j=ADA_SLOTS)
        ada_acc = far[:, 6 * S:7 * S]
        ada_acc1 = far[:, 0:S]
        x_tile = [far[:, j * S:(j + 1) * S] for j in (0, 7, 8)]
        sq_b = [[w_raw[:, SLOTS - 1, j * HALF:(j + 1) * HALF] for j in (0, 1)]] + \
            3 * [[far[:, j * HALF:(j + 1) * HALF] for j in (0, 1)]]
        rstd = [far[:, j * HALF:(j + 1) * HALF] for j in (2, 3)]
        un_b = [far[:, j * HALF:(j + 1) * HALF] for j in (14, 15, 16, 17)]

        gq = [h[:, j, :] for j in (0, 1)]
        gk = [h[:, j, :] for j in (2, 3)]
        gv = h[:, 4:8, :].rearrange("p a (b c) -> p (a b) c", b=2)
        ya = far[:, 0:4 * S].rearrange("p (j s) -> p j s", j=4)
        v_t = [far[:, 4 * S:5 * S], far[:, 6 * S:7 * S]]
        low = far[0:GLA_RANK + 1, 5 * S:6 * S]
        la_b = [far[:, 6 * S + j * HALF:6 * S + (j + 1) * HALF] for j in range(4)]
        la_hi = rar[:, 0:2 * S].rearrange("p (t c) -> p t c", t=TT)
        la_lo = rar[:, 2 * S:4 * S].rearrange("p (t c) -> p t c", t=TT)
        cum = rar[:, 4 * S:4 * S + EC]
        ed = [far[:, 6 * S + c * EC:6 * S + (c + 1) * EC] for c in range(CT)]
        st = far[:, 6 * S + 2 * EC:6 * S + 2 * EC + HALF]
        og = far[:, 4 * S:4 * S + HALF]
        og_sq = far[:, 4 * S + HALF:5 * S]
        og_rs = far[:, 5 * S:5 * S + HALF]
        kd = far[:, 5 * S + HALF:5 * S + HALF + 2 * P]
        qk = [far[:, 5 * S + HALF + (2 + c) * P:5 * S + HALF + (3 + c) * P] for c in range(CT)]
        state = sb("state", [P, CT, GLA_DV])
        dec = sb("dec", [P, 2, CT])
        w2b = sb("w2b", [GLA_RANK + 1, KW])
        mask = sb("mask", [P, LEVELS * (P // 2)], mybir.dt.int8)
        heads2 = sb("heads2", [P, 2])
        dq_hi, dq_lo, dk_hi, dk_lo = [rar[:, j * S:(j + 1) * S] for j in (0, 2, 6, 7)]
        dv = rar[:, 4 * S:6 * S].rearrange("p (t two d) -> p t two d", t=TT, two=2)
        at_hi = [rar[:, S + j * HALF:S + (j + 1) * HALF] for j in range(2)]
        at_lo = [rar[:, 3 * S + j * HALF:3 * S + (j + 1) * HALF] for j in range(2)]
        sc_b = [[h[:, 2 * j + m, :] for m in range(2)] for j in range(2)]
        yb = h[:, 4:8, :]
        on = far[:, 4 * S + HALF:5 * S]
        sq_junk = vec[:]
        ssq = sb("ssq", [P, 4])
        r_b = far[:, 5 * S + HALF:6 * S]
        raw_b = [far[:, 7 * S + j * HALF:7 * S + (j + 1) * HALF] for j in range(2)]
        bias_b = far[:, 8 * S:9 * S]
        mx = sb("mx", [P, 2, 2, 2])
        nmx = sb("nmx", [P, 2, 2])
        lsum = sb("lsum", [P, 2, 2])
        rec = sb("rec", [P, 2, 2])
        ratio = sb("ratio", [P, 2])
        lamv = sb("lamv", [1, 4, DIFF_DH])
        lams = sb("lams", [P, 6])
        lamj = sb("lamj", [1, DIFF_DH])
        gains = sb("gains", [P, 2])
        y_hi = [rar[:, j * S:(j + 1) * S] for j in (0, 6, 1, 4)]
        y_lo = [rar[:, j * S:(j + 1) * S] for j in (2, 7, 3, 5)]
        z = [far[:, j * S:(j + 1) * S] for j in (6, 7, 5, 8, 0, 1, 2, 3)]
        sig_b = [far[:, 4 * S + j * HALF:4 * S + (j + 1) * HALF] for j in range(2)]
        h_dram = nc.dram_tensor("h_dram", (P, KT * S), F32).ap()
        o_tile = [far[:, j * S:(j + 1) * S] for j in range(9) if j != 1]

        ps = [ctx.enter_context(nc.psum_tensor(f"ps{i}", [P, HALF], F32)) for i in range(8)]

        def fm(name):
            return vecT[:, ROWS[name][0]:ROWS[name][1]]

        vec_in = sem("vec_in")
        const_ready = sem("const_ready")
        vec_t = sem("vec_t")
        vecT_ready = sem("vecT_ready")
        c_ready = sem("c_ready")
        x_in = [sem(f"x_in{j}") for j in range(3)]
        x_t = sem("x_t")
        h_act = sem("h_act")
        ada_in = [sem(f"ada_in{j}") for j in range(ADA_SLOTS)]
        ada_used = sem("ada_used")
        ada_sum = sem("ada_sum")
        mod_ready = sem("mod_ready")
        scale_ready = sem("scale_ready")
        w_in_sem = [sem(f"w_loaded{j}") for j in range(SLOTS)]
        w_go = sem("w_go")
        w_high = sem("w_high")
        w_split = sem("w_split")
        unit_done = sem("unit_done")
        sq_ready = sem("sq_ready")
        sq_used = sem("sq_used")
        ln_ready = sem("ln_ready")
        rstd_ready = sem("rstd_ready")
        un_ready = sem("un_ready")
        uhi_ready = sem("uhi_ready")
        un2_ready = sem("un2_ready")
        ulo_dve = sem("ulo_dve")
        ulo_pool = sem("ulo_pool")
        ms_done = sem("ms_done")
        out_half = sem("out_half")
        silu_ready = sem("silu_ready")
        prod_ready = sem("prod_ready")
        hhi_ready = sem("hhi_ready")
        hlo_ready = sem("hlo_ready")
        out_done = sem("out_done")
        acc_done = sem("acc_done")
        y_ready = sem("y_ready")
        low_init = sem("low_init")
        w2_in = sem("w2_in")
        lam_in = sem("lam_in")
        spill = sem("spill")
        low_ready = sem("low_ready")
        z_done = sem("z_done")
        abs_ready = sem("abs_ready")
        ez_ready = sem("ez_ready")
        lz_ready = sem("lz_ready")
        la_ready = sem("la_ready")
        lahi_ready = sem("lahi_ready")
        lalo_ready = sem("lalo_ready")
        gqk_act = sem("gqk_act")
        gqk_dve = sem("gqk_dve")
        vt_act = sem("vt_act")
        vt_dve = sem("vt_dve")
        v_tr = sem("v_tr")
        gv_act = sem("gv_act")
        gv_dve = sem("gv_dve")
        piece_ready = sem("piece_ready")
        piece_used = sem("piece_used")
        mult_dve = sem("mult_dve")
        mult_pool = sem("mult_pool")
        qk_ready = sem("qk_ready")
        score_done = sem("score_done")
        pred_ready = sem("pred_ready")
        kv_done = sem("kv_done")
        state_ready = sem("state_ready")
        o_done = sem("o_done")
        og_ready = sem("og_ready")
        ogsq_ready = sem("ogsq_ready")
        gln_ready = sem("gln_ready")
        grs_ready = sem("grs_ready")
        ya_ready = sem("ya_ready")
        bias_ready = sem("bias_ready")
        s_done = sem("s_done")
        max_ready = sem("max_ready")
        nmx_ready = sem("nmx_ready")
        exp_ready = sem("exp_ready")
        ratio_ready = sem("ratio_ready")
        comb_ready = sem("comb_ready")
        a_ready = sem("a_ready")
        at_done = sem("at_done")
        athi_ready = sem("athi_ready")
        atlo_ready = sem("atlo_ready")
        pv_done = sem("pv_done")
        dqhi = sem("dqhi")
        dqlo = sem("dqlo")
        dvhi = sem("dvhi")
        dvlo = sem("dvlo")
        oh_ready = sem("oh_ready")
        ob_ready = sem("ob_ready")
        obsq_ready = sem("obsq_ready")
        on_ready = sem("on_ready")
        on_t = sem("on_t")
        bln_ready = sem("bln_ready")
        brs_ready = sem("brs_ready")
        yb_ready = sem("yb_ready")
        r_done = sem("r_done")
        r_ready = sem("r_ready")
        rt_ready = sem("rt_ready")
        lam_s = sem("lam_s")
        lam_ps = sem("lam_ps")
        lam_e = sem("lam_e")
        lam_ready = sem("lam_ready")
        yhi_ready = sem("yhi_ready")
        ylo_ready = sem("ylo_ready")
        sig_ready = sem("sig_ready")
        zz_ready = sem("zz_ready")
        zhi_ready = sem("zhi_ready")
        zlo_ready = sem("zlo_ready")
        res_ready = sem("res_ready")
        h_back = sem("h_back")
        chain = sem("chain")
        fill_done = sem("fill_done")
        first_done = sem("first_done")
        raw_ready = sem("raw_ready")
        gate_kept = sem("gate_kept")
        pa_done = sem("pa_done")
        gz_ready = sem("gz_ready")
        gains_ready = sem("gains_ready")
        y_t = sem("y_t")
        o_ready = sem("o_ready")
        o_stored = sem("o_stored")

        block = ctx.enter_context(nc.Block())

        W_IN = [a["ffn1_w_in"][0], a["ffn2_w_in"][0]]
        W_OUT = [a["ffn1_w_out"][0], a["ffn2_w_out"][0]]

        pieces = [("E", 0, c, p) for c in range(CT) for p in range(3)]
        for t in range(TT):
            for c in range(CT):
                if t < TT - 1:
                    pieces += [("T", t, c)] + [("E", t + 1, c, p) for p in range(3)]
            if t > 0:
                pieces.append(("ms", t - 1))
        pieces.append(("ms", TT - 1))
        piece_at = {what: n for n, what in enumerate(pieces)}
        ring = []
        for hd in range(DIFF_H):
            for i in range(TT):
                ring += [("T", hd, i, cc) for cc in range(i // 4 + 1)]
                if i == 5:
                    ring.append(("out", hd, 0))
                if i == 1 and hd > 0:
                    ring.append(("out", hd - 1, 1))
        ring.append(("out", DIFF_H - 1, 1))
        ring_at = {what: n for n, what in enumerate(ring)}
        chunk_at = {what: n for n, what in enumerate(w for w in ring if w[0] == "T")}
        pairs = [(hd, i, cc) for hd in range(DIFF_H) for i in range(TT) for cc in range(i // 4 + 1)]
        pair_at = {what: n for n, what in enumerate(pairs)}

        FILL = [("r", 0), ("r", 1), ("q", 0), ("k", 0), ("v", 0), ("v", 1), ("q", 1), ("k", 1)]
        FILL_UNIT = {"r": 0, "q": 1, "k": 2, "v": 3}

        def fill_of(hd, i):
            if hd == DIFF_H - 1 and i >= 2:
                return "gate", i % 2
            return FILL[i]

        def r_unit(hd):
            return U_HEAD + 3 + 4 * hd

        def completes(hd, i):
            return i in ((1, 6, 7) if hd < DIFF_H - 1 else (1, 3, 5, 7))

        def fill_count(hd, i):
            return 5 * hd + sum(not completes(hd, j) for j in range(i + 1))

        def unit_count(hd, i):
            if hd < DIFF_H - 1:
                return MB + r_unit(hd) + {1: 1, 6: 2, 7: 4}[i]
            return MB + r_unit(hd) + (i + 1) // 2

        FIRST = [("k", 0), ("k", 1), ("q", 0), ("q", 1)]

        def first_ready(engine, n):
            if n % 2 == 0:
                engine.wait_ge(first_done, n // 2 + 1)
            else:
                engine.wait_ge(unit_done, MB + U_HEAD + n // 2 + 1)

        def q_scale(hd):
            return 4.0 ** hd

        X_BANK = (0, 1, 4, 5)
        by_half = [(hf, k) for hf in range(2) for k in range(KT)]
        LATE = KT - SLOTS
        SQUARES = [by_half, by_half, [(hf, k) for k in range(LATE) for hf in range(2)] +
                   [(hf, k) for hf in range(2) for k in range(LATE, KT)], by_half]
        FIRST_RSTD = [12, 12, 14, 12]

        def sq_count(n, hf, k):
            return n * 2 * KT + SQUARES[n].index((hf, k)) + 1

        def add_count(n, hf, k):
            return n * 2 * (KT - 1) + [t for t in SQUARES[n] if t[1] > 0].index((hf, k)) + 1

        def half_added(n, hf):
            return add_count(n, hf, KT - 1)

        def piece(n, hf, k):
            return (2 * n + hf) * KT + k

        def out_res(m, hf):
            return 2 * m + hf + 1 if m < LATE else 2 * LATE + hf * SLOTS + m - LATE + 1

        def width(i, cc):
            return min(HALF, (i + 1) * P - cc * HALF)

        def half(hf):
            return slice(hf * HALF, (hf + 1) * HALF)

        def tile(t):
            return slice(t * P, (t + 1) * P)

        def first_halves(x, l):
            return x.rearrange("p (j two r) -> p j two r", two=2, r=P >> (l + 1))[:, :, 0, :]

        def second_halves(x, l):
            return x.rearrange("p (j two r) -> p j two r", two=2, r=P >> (l + 1))[:, :, 1, :]

        def blocks(x, l):
            return x.rearrange("p (j r) -> p j r", r=P >> (l + 1))

        POOL_LEVELS = 6

        def k_products(eng, t, c, levels):
            for l in levels:
                e = first_halves(ed[c][:, l * P:(l + 1) * P], l)
                mult = eng.tensor_tensor(e, e, first_halves(gk[c][:, tile(t)], l), ALU.mult)
            return mult

        def sum_place(m):
            if isinstance(m, int) and m == 1:
                return ada_acc1, ps[6]
            return ada_acc, ps[7]

        def unit0(f, g):
            return BASE[f] + 4 + 6 * (g - 1)

        def gate_unit(f, j, jj):
            if isinstance(j, int) and j < 2:
                return BASE[f] + 2 * j
            return unit0(f, 0) + 3 * (j - jj) + 4 * jj

        @block.sync
        def _(sp):
            def columns(n, slot, w, c):
                if not (isinstance(n, int) and n < SLOTS):
                    sp.wait_ge(w_split, n - SLOTS + 1)
                elif n == SLOTS - 1:
                    sp.wait_ge(sq_used, half_added(0, 1))
                sp.dma_start(w_raw[:, slot, :].rearrange("p (k m) -> p k m", k=KT),
                             w[:, c].rearrange("(k p) m -> p k m", p=P)).then_inc(w_in_sem[slot], 16)

            def rows(n, slot, w, r):
                sp.wait_ge(w_split, n - SLOTS + 1)
                sp.dma_start(w_raw[:, slot, :], w[r, :]).then_inc(w_in_sem[slot], 16)

            def ada(m, k):
                i = m * KT + k
                if not (isinstance(i, int) and i < ADA_SLOTS):
                    sp.wait_ge(ada_used, i - ADA_SLOTS + 1)
                sp.dma_start(ada_raw[:, k % ADA_SLOTS, :],
                             a["w_ada"][0][k * P:(k + 1) * P, bass.ds(m * D, D)]).then_inc(ada_in[k % ADA_SLOTS], 16)

            def pair(f, n, slot, j):
                if not (isinstance(n, int) and n == 0):
                    columns(n, slot % SLOTS, W_IN[f], bass.ds(j * P, P))
                columns(n + 1, (slot + 1) % SLOTS, W_IN[f], bass.ds(D_FF + j * P, P))

            def outs(f, n, slot, g):
                rows(n, slot % SLOTS, W_OUT[f], bass.ds(g * 2 * P, P))
                rows(n + 1, (slot + 1) % SLOTS, W_OUT[f], bass.ds(g * 2 * P + P, P))

            def ffn(f):
                pair(f, BASE[f], 0, 0)
                pair(f, BASE[f] + 2, 2, 1)
                if f == 0:
                    for k in range(KT):
                        ada(2, k)

                def body(g, with_ada):
                    n = unit0(f, g)
                    pair(f, n, 1, 2 * g)
                    if with_ada:
                        for k in range(KT):
                            ada(g + ADA_FIRST - 1, k)
                    outs(f, n + 2, 0, g - 1)
                    pair(f, n + 4, 2, 2 * g + 1)
                first = 1
                if f == 0:
                    first = 1 + N_MOD - ADA_FIRST
                    with sp.Fori(1, first) as g:
                        body(g, True)
                with sp.Fori(first, GROUPS) as g:
                    body(g, False)
                outs(f, unit0(f, GROUPS), 1, GROUPS - 1)

            for t in range(TT):
                if t >= 3:
                    sp.wait_ge(x_t, 2 * (t - 3) + 2)
                sp.dma_start(x_tile[t % 3], a["x"][0][t * P:(t + 1) * P, :]).then_inc(x_in[t % 3], 16)
                if t == 2:
                    for k in range(ADA_SLOTS):
                        ada(0, k)
                if t == 1:
                    for j, name in enumerate(("diff_lq1", "diff_lk1", "diff_lq2", "diff_lk2")):
                        sp.dma_start(lamv[0:1, j, :], a[name]).then_inc(lam_in, 16)
                    for name, (r0, r1) in ROWS.items():
                        src = a[name] if name in ("final_norm",) else a[name][0]
                        sp.dma_start(vec[r0:r1, :], src.rearrange("(r c) -> r c", c=P)).then_inc(vec_in, 16)
            for k in range(ADA_SLOTS, KT):
                ada(0, k)
            columns(0, 0, W_IN[0], slice(0, P))
            for k in range(KT):
                ada(1, k)
            sp.dma_start(w2b[0:GLA_RANK, :], a["gla_alpha_w2"][0]).then_inc(w2_in, 16)
            sp.dma_start(w2b[GLA_RANK:GLA_RANK + 1, :], a["gla_alpha_b"]).then_inc(w2_in, 16)
            ffn(0)
            W = a["w_in"][0]

            def mix_columns(u, w, c):
                columns(MB + u, u % SLOTS, w, slice(c, c + P))
            starts = [C_GA, C_GQ, C_GQ + P, C_GK, C_GK + P] + [C_GV + P * hd for hd in range(GLA_H)]
            starts += [C_DK, C_DQ, C_DV]
            for hd in range(DIFF_H):
                starts.append(C_GR + P * hd)
                if hd + 1 < DIFF_H:
                    starts += [C_DQ + P * (hd + 1), C_DK + P * (hd + 1), C_DV + P * (hd + 1)]
            for u, c in enumerate(starts):
                mix_columns(u, W, c)
                if u == SLOTS - 1:
                    sp.wait_ge(acc_done, DOWN * GROUPS)
                    sp.dma_start(h_dram, h[:].rearrange("p k s -> p (k s)")).then_inc(spill, 16)
            for (what, br, i), u in BRANCH_UNIT.items():
                if what == "gate":
                    mix_columns(u, W, C_GATE + D * br + P * i)
                else:
                    wb = (a["w_branch_a"][0], a["w_branch_b"][0])[br]
                    n = MB + u
                    sp.wait_ge(w_split, n - SLOTS + 1)
                    sp.dma_start(w_raw[:, u % SLOTS, :].rearrange("p (k m) -> p k m", k=4),
                                 wb[:, 2 * P * i:2 * P * (i + 1)].rearrange("(k p) m -> p k m", p=P)
                                 ).then_inc(w_in_sem[u % SLOTS], 16)
                if (what, br, i) == ("w", 1, 1):
                    sp.wait_ge(yhi_ready, 8)
                    sp.wait_ge(ylo_ready, 8)
                    sp.dma_start(h[:].rearrange("p k s -> p (k s)"), h_dram).then_inc(h_back, 16)
            for m in range(KT):
                mix_columns(U_OUT + m, a["w_out"][0], m * P)
            ffn(1)
            for t in range(TT):
                sp.wait_ge(o_ready, 8 * (t // 4) + 4 + t % 4 + 1)
                sp.dma_start(out[0][t * P:(t + 1) * P, :], o_tile[t]).then_inc(o_stored, 16)
            sp.wait_ge(o_stored, 16 * TT)

        @block.gpsimd
        def _(pool):
            nc.gpsimd.memset(ident[:], 0.0).then_inc(const_ready, 1)
            nc.gpsimd.memset(ones[:], 1.0).then_inc(const_ready, 1)
            nc.gpsimd.memset(eps_c[:], EPS).then_inc(const_ready, 1)
            pool.wait_ge(const_ready, 3)
            nc.gpsimd.affine_select(out=ident[:], in_=ident[:], compare_op=ALU.not_equal, fill=1.0, base=0,
                                    pattern=[[-1, P]], channel_multiplier=1).then_inc(const_ready, 1)

            def select(out_, in_, pattern, base, step, op):
                nc.gpsimd.affine_select(out=out_, in_=in_, compare_op=op, fill=0.0, base=base, pattern=pattern,
                                        channel_multiplier=step).then_inc(const_ready, 1)

            nc.gpsimd.memset(mask[:], 1).then_inc(const_ready, 1)
            nc.gpsimd.memset(heads2[:], 1.0).then_inc(const_ready, 1)
            pool.wait_ge(const_ready, 6)
            for l in range(LEVELS):
                hb, nb = P >> (l + 1), 1 << l
                e = cum[:, l * P:(l + 1) * P]
                one = blocks(ones[:, 0:P // 2], l)
                select(second_halves(e, l), one, [[2 * hb, nb], [1, hb]], hb, -1, ALU.is_ge)
                select(first_halves(e, l), one, [[-2 * hb, nb], [-1, hb]], 0, 1, ALU.is_gt)
                m = blocks(mask[:, l * P // 2:(l + 1) * P // 2], l)
                select(m, m, [[-2 * hb, nb], [0, hb]], 0, 1, ALU.is_ge)
            select(cum[:, LEVELS * P:(LEVELS + 1) * P], ones[:], [[1, P]], 0, -1, ALU.is_ge)
            select(cum[:, (LEVELS + 1) * P:EC], ones[:], [[-1, P]], 0, 1, ALU.is_gt)
            select(heads2[:, 0:1], heads2[:, 0:1], [[0, 1]], P // 2 - 1, -1, ALU.is_ge)
            select(heads2[:, 1:2], heads2[:, 1:2], [[0, 1]], -P // 2, 1, ALU.is_ge)
            pool.wait_ge(const_ready, 6 + 3 * LEVELS + 4)
            for l in range(LEVELS):
                hb, nb = P >> (l + 1), 1 << l
                e = cum[:, l * P:(l + 1) * P]
                select(second_halves(e, l), second_halves(e.bitcast(F32), l), [[-2 * hb, nb], [0, hb]], -hb, 1,
                       ALU.is_ge)
                select(first_halves(e, l), first_halves(e.bitcast(F32), l), [[2 * hb, nb], [0, hb]], hb - 1, -1,
                       ALU.is_ge)
                m = blocks(mask[:, l * P // 2:(l + 1) * P // 2], l)
                select(m, m, [[2 * hb, nb], [0, hb]], hb - 1, -1, ALU.is_ge)

            def split_unit(n, slot, loads):
                pool.wait_ge(w_in_sem[slot], 16 * loads)
                if not (isinstance(n, int) and n < SLOTS):
                    pool.wait_ge(unit_done, n - SLOTS + 1)
                pool.sem_inc(w_go, 1)
                nc.gpsimd.tensor_scalar(w_hi[:, slot, :], w_raw[:, slot, :], 1.0, 0.0,
                                        ALU.mult, ALU.add).then_inc(w_high, 1)
                pool.wait_ge(w_high, n + 1)
                nc.gpsimd.tensor_tensor(w_lo[:, slot, :], w_raw[:, slot, :], w_hi[:, slot, :].bitcast(F32),
                                        ALU.subtract).then_inc(w_split, 1)

            def straight(n0, count):
                for n in range(n0, n0 + count):
                    split_unit(n, n % SLOTS, n // SLOTS + 1)

            def adds(n, first=0, last=2 * KT):
                for hf, k in SQUARES[n][first:last]:
                    if k == 0:
                        continue
                    pool.wait_ge(sq_ready, sq_count(n, hf, k))
                    c = add_count(n, hf, k)
                    if k >= 2:
                        pool.wait_ge(sq_used, add_count(n, hf, k - 1))
                    nc.gpsimd.tensor_tensor(rstd[hf], rstd[hf], sq_b[n][c % 2], ALU.add).then_inc(sq_used, 1)

            def lows(n, hf, ks):
                for k in ks:
                    j = piece(n, hf, k)
                    pool.wait_ge(un2_ready, j // 2 + 1)
                    nc.gpsimd.tensor_tensor(u_lo[:, k, half(hf)], un_b[j % 4], u_hi[:, k, half(hf)].bitcast(F32),
                                            ALU.subtract).then_inc(ulo_pool, 1)

            def norm(n, n0):
                if n == 0:
                    adds(n)
                    straight(n0, 2)
                    lows(n, 0, (1, 3, 5, 7))
                elif n == 1:
                    straight(n0, 1)
                    adds(n)
                    lows(n, 0, (1, 3))
                    straight(n0 + 1, 1)
                    lows(n, 0, (5, 7))
                else:
                    adds(n, 0, 14)
                    straight(n0, 1)
                    lows(n, 0, (1, 3))
                    adds(n, 14, 15)
                    lows(n, 0, (5,))
                    adds(n, 15)
                    lows(n, 0, (7,))
                    straight(n0 + 1, 1)
                lows(n, 1, (1, 3, 5, 7))
                straight(n0 + 2, 1)

            def ffn(f):
                straight(BASE[f] + 3, 1)
                with pool.Fori(1, GROUPS) as g:
                    n = unit0(f, g)
                    for i in range(6):
                        split_unit(n + i, (1 + i) % SLOTS, (BASE[f] // 3 + 2 + 2 * (g - 1)) + (i + 1) // 3)
                straight(unit0(f, GROUPS), 2)
            norm(0, BASE[0])
            ffn(0)
            pool.wait_ge(mod_ready, N_MOD)
            nc.gpsimd.memset(low, 1.0).then_inc(low_init, 1)
            norm(1, MB)
            straight(MB + 3, U_HEAD + SLOTS - 3)
            for t in range(TT):
                if t == 0:
                    pool.wait_ge(gqk_act, 4)
                    pool.wait_ge(gqk_dve, 4)
                for c in range(CT):
                    pool.wait_ge(piece_used, piece_at["E", t, c, 2] + 1)
                    k_products(pool, t, c, range(POOL_LEVELS)).then_inc(mult_pool, 1)
            pool.wait_ge(o_done, TT)
            nc.gpsimd.iota(bias_b, [[-1, S]], base=S - P, channel_multiplier=1,
                           allow_small_or_imprecise_dtypes=True).then_inc(bias_ready, 1)
            pool.wait_ge(bias_ready, 1)
            nc.gpsimd.tensor_scalar(bias_b, bias_b, -DIFF_DH ** 0.5 * 2.0 ** (-ALIBI / DIFF_H), 0.0, ALU.mult,
                                    ALU.add).then_inc(bias_ready, 1)
            pool.wait_ge(bias_ready, 2)
            nc.gpsimd.affine_select(out=bias_b, in_=bias_b, compare_op=ALU.is_ge, fill=-2e36, base=S - P,
                                    pattern=[[-1, S]], channel_multiplier=1).then_inc(bias_ready, 1)
            straight(MB + U_HEAD + SLOTS, MIX_UNITS - U_HEAD - SLOTS)
            norm(2, BASE[1])
            ffn(1)
            adds(3)

        @block.scalar
        def _(act):
            def h_final(n, hf, k):
                if n == 0:
                    act.wait_ge(h_act, 8 * hf + 8)
                elif n == 2:
                    act.wait_ge(res_ready, out_res(k, hf))
                else:
                    act.wait_ge(acc_done, DOWN * ((n // 2 + 1) * GROUPS - 1) + hf * KT + k + 1)

            def squares(n, first, last):
                for hf, k in SQUARES[n][first:last]:
                    h_final(n, hf, k)
                    out_ = rstd[hf]
                    if k > 0:
                        c = add_count(n, hf, k)
                        if c > 2:
                            act.wait_ge(sq_used, c - 2)
                        out_ = sq_b[n][c % 2]
                    nc.scalar.activation(out_, h[:, k, half(hf)], ACT.Square).then_inc(sq_ready, 1)

            def root(n, hf):
                act.wait_ge(ms_done, 2 * n + hf + 1)
                nc.scalar.activation(rstd[hf], ps[2 + hf][:], ACT.Ln, bias=eps_c[:, 0:1],
                                     scale=1.0 / D).then_inc(ln_ready, 1)
                act.wait_ge(ln_ready, 2 * n + hf + 1)
                nc.scalar.activation(rstd[hf], rstd[hf], ACT.Exp, scale=-0.5).then_inc(rstd_ready, 1)

            def first_root(n, first=0):
                squares(n, first, FIRST_RSTD[n])
                root(n, 0)
                if n != 2:
                    squares(n, FIRST_RSTD[n], 2 * KT)

            def norm(n):
                for hf, k in by_half:
                    if n == 1 and (hf, k) == (0, 4):
                        root(n, 1)
                    if n == 2 and (hf, k) == (0, 4):
                        squares(n, 14, 15)
                    if n == 2 and (hf, k) == (1, 0):
                        squares(n, 15, 16)
                        root(n, 1)
                    j = piece(n, hf, k)
                    sh = mod[:, 3 * n * KT + k:3 * n * KT + k + 1]
                    act.wait_ge(un_ready, j + 1)
                    nc.scalar.activation(u_hi[:, k, half(hf)], un_b[j % 4], ACT.Identity, bias=sh).then_inc(uhi_ready, 1)
                    if k % 2:
                        act.wait_ge(uhi_ready, j + 1)
                        nc.scalar.activation(un_b[j % 4], un_b[j % 4], ACT.Identity, bias=sh).then_inc(un2_ready, 1)

            def hidden(f, j, jj):
                t = f * FT + j
                act.wait_ge(unit_done, gate_unit(f, j, jj) + 1)
                if not (isinstance(t, int) and t == 0):
                    act.wait_ge(prod_ready, 2 * t)
                for hf in range(2):
                    nc.scalar.activation(silu_b[:, hf * HALF:(hf + 1) * HALF], ps[4 * jj + hf][:],
                                         ACT.Silu).then_inc(silu_ready, 1)
                for hf in range(2):
                    act.wait_ge(prod_ready, 2 * t + hf + 1)
                    if hf == 0 and not (isinstance(j, int) and j < 2):
                        act.wait_ge(unit_done, unit0(f, 0) + 3 * (j - jj) + 4)
                    nc.scalar.activation(hid_hi[:, jj, hf * HALF:(hf + 1) * HALF],
                                         prod_b[:, hf * HALF:(hf + 1) * HALF], ACT.Copy).then_inc(hhi_ready, 1)

            def ffn(f):
                hidden(f, 0, 0)
                with act.Fori(1, GROUPS) as g:
                    hidden(f, 2 * g - 1, 1)
                    hidden(f, 2 * g, 0)
                hidden(f, FT - 1, 1)

            def copy(out_, in_, done, scale=1.0):
                nc.scalar.activation(out_, in_, ACT.Copy, scale=scale).then_inc(done, 1)

            def mixer():
                act.wait_ge(low_init, 1)
                act.wait_ge(unit_done, MB + U_GA + 1)
                for hf in range(2):
                    copy(low[0:GLA_RANK, half(hf)], ps[hf][0:GLA_RANK, :], low_ready)
                for b in range(4):
                    act.wait_ge(z_done, b + 1)
                    nc.scalar.activation(la_b[b], ps[4 + b][:], ACT.Abs).then_inc(abs_ready, 1)
                for b in range(4):
                    act.wait_ge(abs_ready, b + 1)
                    nc.scalar.activation(la_b[b], la_b[b], ACT.Exp, scale=-1.0).then_inc(ez_ready, 1)
                for b in range(4):
                    act.wait_ge(ez_ready, b + 1)
                    nc.scalar.activation(la_b[b], la_b[b], ACT.Ln, bias=ones[:, 0:1]).then_inc(lz_ready, 1)
                for b in range(4):
                    act.wait_ge(la_ready, b + 1)
                    copy(rar[:, b * HALF:(b + 1) * HALF], la_b[b], lahi_ready, 1.0 / GLA_TAU)
                act.wait_ge(spill, 16)
                for j in range(2):
                    act.wait_ge(unit_done, MB + U_GQ + j + 1)
                    for hf in range(2):
                        copy(gq[j][:, half(hf)], ps[2 * ((U_GQ + j) % 2) + hf][:], gqk_act, GLA_DK ** -0.5)
                act.wait_ge(lalo_ready, 4)
                for hd in range(GLA_H + 1):
                    if hd < GLA_H:
                        act.wait_ge(unit_done, MB + U_GV + hd + 1)
                        if hd >= 2:
                            act.wait_ge(v_tr, hd - 1)
                        copy(v_t[hd % 2][:, half(0)], ps[2 * ((U_GV + hd) % 2)][:], vt_act)
                    if hd >= 1:
                        act.wait_ge(v_tr, hd)
                        copy(gv[:, 0:4, tile(hd - 1)], ps[4 + 2 * ((hd - 1) % 2)][:].rearrange("p (t d) -> p t d", t=4),
                             gv_act)

                def decays(t, c):
                    for p in range(3):
                        n = piece_at["E", t, c, p]
                        act.wait_ge(piece_ready, n + 1)
                        lo, hi = p * HALF, min((p + 1) * HALF, EC)
                        e = nc.scalar.activation(ed[c][:, lo:hi], ps[4 + n % 2][:, 0:hi - lo], ACT.Exp)
                        if p == 1:
                            if t >= 2:
                                act.wait_ge(state_ready, CT * (t - 2) + c + 1)
                            e = nc.scalar.activation(dec[:, t % 2, c:c + 1], ps[4 + n % 2][:, HALF - 1:HALF], ACT.Exp)
                        e.then_inc(piece_used, 1)

                def gla_rms(t):
                    n = piece_at["ms", t]
                    act.wait_ge(piece_ready, n + 1)
                    nc.scalar.activation(og_rs, ps[4 + n % 2][:], ACT.Ln, bias=eps_c[:, 0:1],
                                         scale=1.0 / GLA_DV).then_inc(piece_used, 1)
                    act.wait_ge(piece_used, n + 1)
                    nc.scalar.activation(og_rs, og_rs, ACT.Exp, scale=-0.5).then_inc(grs_ready, 1)

                for c in range(CT):
                    decays(0, c)
                for t in range(TT):
                    for c in range(CT):
                        if t < TT - 1:
                            n = piece_at["T", t, c]
                            act.wait_ge(piece_ready, n + 1)
                            if t >= 1:
                                act.wait_ge(kv_done, t)
                            copy(kd[:, tile(c)], ps[4 + n % 2][:, 0:P], piece_used)
                            decays(t + 1, c)
                    if t > 0:
                        gla_rms(t - 1)
                        act.wait_ge(ya_ready, t)
                    act.wait_ge(o_done, t + 1)
                    for hh in range(2):
                        copy(og.rearrange("p (c hh t) -> p c hh t", c=CT, hh=2)[:, :, hh, :],
                             ps[2 + hh][:, 0:2 * P].rearrange("p (c t) -> p c t", c=CT), og_ready)
                    act.wait_ge(og_ready, 2 * t + 2)
                    nc.scalar.activation(og_sq, og, ACT.Square).then_inc(ogsq_ready, 1)
                    if t % 2:
                        what, hf = FIRST[t // 2]
                        first_ready(act, t // 2)
                        copy((dk_hi if what == "k" else dq_hi)[:, half(hf)], ps[1][:], dqhi)
                gla_rms(TT - 1)

                def fill_out(hd, i):
                    what, hf = fill_of(hd, i)
                    if completes(hd, i):
                        act.wait_ge(unit_done, unit_count(hd, i))
                    else:
                        act.wait_ge(fill_done, fill_count(hd, i))
                    if what == "r":
                        n = 2 * hd + hf
                        if n >= 1:
                            act.wait_ge(rt_ready, n)
                        nc.scalar.activation(r_b, ps[0][:], ACT.Silu).then_inc(r_ready, 1)
                        nc.scalar.preload_act_table_set("natural_log_exp_and_others")
                    elif what == "gate":
                        if i == 6:
                            act.wait_ge(rt_ready, 2 * DIFF_H)
                        copy(z[i // 2 - 1][:, half(hf)], ps[0][:], gate_kept)
                    elif what == "v":
                        copy(v_t[1][:, half(hf)], ps[0][:], vt_act)
                    elif hf == 0:
                        copy(raw_b[0 if what == "q" else 1], ps[0][:], raw_ready)
                    elif what == "q":
                        copy(dq_hi[:, half(1)], ps[0][:], dqhi, q_scale(hd + 1))
                    else:
                        copy(dk_hi[:, half(1)], ps[0][:], dqhi)

                def squares_b(hd, i):
                    n = TT * hd + i
                    act.wait_ge(ob_ready, n + 1)
                    if n >= 1:
                        act.wait_ge(obsq_ready, n)
                    if i % 4 == 0 and n >= 4:
                        act.wait_ge(on_ready, n // 4)
                    nc.scalar.activation(sq_junk, og[:, tile(i % 4)], ACT.Square,
                                         accum_out=ssq[:, i % 4:i % 4 + 1]).then_inc(obsq_ready, 1)

                def rms_b(hd, hf):
                    n = 2 * hd + hf
                    act.wait_ge(obsq_ready, 4 * n + 4)
                    nc.scalar.activation(ssq[:], ssq[:], ACT.Ln, bias=eps_c[:, 0:1],
                                         scale=1.0 / DIFF_DV).then_inc(bln_ready, 1)
                    act.wait_ge(bln_ready, n + 1)
                    nc.scalar.activation(ssq[:], ssq[:], ACT.Exp, scale=-0.5).then_inc(brs_ready, 1)

                def exps(hd, i):
                    w = (i + 1) * P
                    act.wait_ge(nmx_ready, TT * hd + i + 1)
                    for m in range(2):
                        x = sc_b[i % 2][m][:, 0:w]
                        nc.scalar.activation(x, x, ACT.Exp, bias=nmx[:, i % 2, m:m + 1],
                                             accum_out=lsum[:, i % 2, m:m + 1]).then_inc(exp_ready, 1)

                def divide(hd, i):
                    act.wait_ge(comb_ready, TT * hd + i + 1)
                    x = sc_b[i % 2][0][:, 0:(i + 1) * P]
                    nc.scalar.activation(x, x, ACT.Copy, scale=rec[:, i % 2, 0:1]).then_inc(a_ready, 1)

                def high_y(br, j):
                    copy(y_hi[j], (ya if br == 0 else yb)[:, j, :], yhi_ready)

                def high_a(hd, i):
                    for cc in range(i // 4 + 1):
                        n = chunk_at["T", hd, i, cc]
                        act.wait_ge(at_done, n + 1)
                        if n >= 2:
                            act.wait_ge(pv_done, n - 1)
                        w = width(i, cc)
                        copy(at_hi[n % 2][:, 0:w], ps[1 + ring_at["T", hd, i, cc] % 2][:, 0:w], athi_ready)

                act.wait_ge(first_done, 3)
                copy(v_t[1][:, half(0)], ps[0][:], vt_act)
                exps(0, 0)
                divide(0, 0)
                exps(0, 1)
                act.wait_ge(unit_done, MB + U_HEAD + 3)
                copy(v_t[1][:, half(1)], ps[3][:], vt_act)
                divide(0, 1)
                for hd in range(DIFF_H):
                    for i in range(TT):
                        high_a(hd, i)
                        if i < 2:
                            act.wait_ge(v_tr, GLA_H + 2 * hd + i + 1)
                            copy(dv[:, 4 * i:4 * i + 4, 0, :], ps[0][:].rearrange("p (t d) -> p t d", t=4), dvhi)
                        if i == 6:
                            fill_out(hd, i)
                        ahead = (hd, i + 2) if i + 2 < TT else (hd + 1, i + 2 - TT)
                        if ahead[0] < DIFF_H:
                            exps(*ahead)
                        if hd + i > 0:
                            squares_b(*((hd, i - 1) if i > 0 else (hd - 1, TT - 1)))
                        if i == 4:
                            rms_b(hd, 0)
                        if i == 0 and hd > 0:
                            rms_b(hd - 1, 1)
                        if i != 6:
                            fill_out(hd, i)
                        if ahead[0] < DIFF_H:
                            divide(*ahead)
                        if hd == DIFF_H - 1 and i >= 6:
                            act.wait_ge(rt_ready, 2 * DIFF_H)
                            act.wait_ge(s_done, len(pairs))
                            high_y(0, i - 6)
                        if i == 5 and hd + 1 < DIFF_H:
                            act.wait_ge(s_done, pair_at[hd, TT - 1, 1] + 1)
                            copy(dq_hi[:, half(0)], raw_b[0], dqhi, q_scale(hd + 1))
                            copy(dk_hi[:, half(0)], raw_b[1], dqhi)
                squares_b(DIFF_H - 1, TT - 1)
                rms_b(DIFF_H - 1, 1)
                act.wait_ge(pv_done, len(chunk_at))
                for j in (2, 3):
                    high_y(0, j)

                def high_z(ks):
                    for k in ks:
                        for hf in range(2):
                            act.wait_ge(zz_ready, 2 * KT + 2 * k + hf + 1)
                            copy(u_hi[:, k, half(hf)], z[k][:, half(hf)], zhi_ready)

                for br in range(2):
                    if br == 1:
                        act.wait_ge(unit_done, MB + BRANCH_UNIT["w", 0, 3] + 1)
                        act.wait_ge(yb_ready, 2 * DIFF_H)
                        for j in range(4):
                            high_y(1, j)
                    for m in range(KT):
                        if (br, m) == (1, 7):
                            act.wait_ge(unit_done, MB + BRANCH_UNIT["gate", 1, 7] + 1)
                            high_z(range(6))
                        early = br == 0 and m < EARLY
                        if not early:
                            act.wait_ge(unit_done, MB + BRANCH_UNIT["gate", br, m] + 1)
                        for hf in range(2):
                            n = 2 * KT * br + 2 * m + hf
                            if early:
                                act.wait_ge(gate_kept, 2 * m + hf + 1)
                                nc.scalar.activation(z[m][:, half(hf)], z[m][:, half(hf)],
                                                     ACT.Sigmoid).then_inc(sig_ready, 1)
                                continue
                            if br == 0 and m == EARLY:
                                act.wait_ge(on_t, 2 * DIFF_H)
                            else:
                                act.wait_ge(zz_ready, n - 1)
                            nc.scalar.activation(sig_b[hf], ps[2 + 4 * (m % 2) + hf][:],
                                                 ACT.Sigmoid).then_inc(sig_ready, 1)
                high_z((6, 7))

            act.wait_ge(lam_ps, 1)
            nc.scalar.activation(lams[:, 2:4], ps[6][:, 0:2], ACT.Exp).then_inc(lam_e, 1)
            act.wait_ge(vecT_ready, 1)
            nc.scalar.activation(c_act[:], fm("c"), ACT.Silu).then_inc(c_ready, 1)
            nc.scalar.preload_act_table_set("natural_log_exp_and_others")
            for i in range(2 * TT):
                t, k0 = i // 2, 4 * (i % 2)
                act.wait_ge(x_t, i + 1)
                nc.scalar.activation(h[:, k0:k0 + 4, t * P:(t + 1) * P],
                                     ps[X_BANK[i % 4]][:].rearrange("p (k s) -> p k s", k=4), ACT.Copy).then_inc(h_act, 1)
                if i % 2 and t >= 4:
                    squares(0, 2 * (t - 4), 2 * (t - 3))
            first_root(0, KT)
            root(0, 1)
            norm(0)
            ffn(0)
            nc.scalar.preload_act_table_set("natural_log_exp_and_others")
            first_root(1)
            norm(1)
            mixer()
            nc.scalar.preload_act_table_set("natural_log_exp_and_others")
            first_root(2)
            norm(2)
            ffn(1)
            nc.scalar.preload_act_table_set("natural_log_exp_and_others")
            first_root(3)
            root(3, 1)
            for i in range(2 * TT):
                hf, kg, t = i // 8, i // 4 % 2, 4 * (i // 8) + i % 4
                act.wait_ge(y_t, i + 1)
                nc.scalar.activation(o_tile[t][:, half(kg)], ps[i % 4 + 4][:], ACT.Copy).then_inc(o_ready, 1)

        @block.vector
        def _(dve):
            def chunk(m):
                for k in range(KT):
                    i = m * KT + k
                    dve.wait_ge(ada_in[k % ADA_SLOTS], 16 * (m * (KT // ADA_SLOTS) + k // ADA_SLOTS + 1))
                    if not (isinstance(i, int) and i == 0):
                        dve.wait_ge(ada_used, i)
                    acc = sum_place(m)[0]
                    if k == 0:
                        if not (isinstance(m, int) and m < 2):
                            dve.wait_ge(ada_sum, m)
                        nc.vector.tensor_scalar(acc, ada_raw[:, 0, :], c_act[:, 0:1], None,
                                                ALU.mult).then_inc(ada_used, 1)
                    else:
                        nc.vector.scalar_tensor_tensor(acc, ada_raw[:, k % ADA_SLOTS, :], c_act[:, k:k + 1],
                                                       acc, ALU.mult, ALU.add).then_inc(ada_used, 1)

            def chunk_out(m):
                dve.wait_ge(ada_sum, m + 1)
                nc.vector.tensor_tensor(mod[:, bass.ds(m * KT, KT)], sum_place(m)[1][:, 0:KT], vecT[:, bass.ds(m * KT, KT)],
                                        ALU.add).then_inc(mod_ready, 1)

            def scale(n, g):
                m = 3 * n + 1
                dve.wait_ge(mod_ready, m + 1)
                nc.vector.scalar_tensor_tensor(scale_c[:, n, :], mod[:, m * KT:(m + 1) * KT], 1.0, fm(g),
                                               ALU.add, ALU.mult).then_inc(scale_ready, 1)

            def out_residual(m, hf):
                if m >= LATE and hf == 0:
                    dve.wait_ge(out_half, m - LATE + 1)
                else:
                    dve.wait_ge(unit_done, MB + U_OUT + m + 1)
                nc.vector.scalar_tensor_tensor(h[:, m, half(hf)], ps[2 * ((m + 1) % 4) + hf][:],
                                               mod[:, 5 * KT + m:5 * KT + m + 1], h[:, m, half(hf)],
                                               ALU.mult, ALU.add).then_inc(res_ready, 1)

            def norm(n):
                dve.wait_ge(scale_ready, n + 1)
                for i in range(2 * KT + 1):
                    if n == 2 and i in (4, 8):
                        out_residual(KT - 2 if i == 4 else KT - 1, 1)
                    if i < 2 * KT:
                        hf, k = by_half[i]
                        j = piece(n, hf, k)
                        if k == 0:
                            dve.wait_ge(rstd_ready, 2 * n + hf + 1)
                        if j >= 4:
                            dve.wait_ge(ulo_pool if k % 2 else ulo_dve, j // 2 - 1)
                        nc.vector.scalar_tensor_tensor(un_b[j % 4], h[:, k, half(hf)], scale_c[:, n, k:k + 1], rstd[hf],
                                                       ALU.mult, ALU.mult).then_inc(un_ready, 1)
                    if i >= 1:
                        hf, k = by_half[i - 1]
                        if k % 2 == 0:
                            j = piece(n, hf, k)
                            dve.wait_ge(uhi_ready, j + 1)
                            nc.vector.scalar_tensor_tensor(u_lo[:, k, half(hf)], un_b[j % 4],
                                                           mod[:, 3 * n * KT + k:3 * n * KT + k + 1],
                                                           u_hi[:, k, half(hf)].bitcast(F32), ALU.add,
                                                           ALU.subtract).then_inc(ulo_dve, 1)

            def hidden(f, j, jj):
                t = f * FT + j
                dve.wait_ge(unit_done, gate_unit(f, j, jj) + 2)
                for hf in range(2):
                    s = slice(hf * HALF, (hf + 1) * HALF)
                    dve.wait_ge(silu_ready, 2 * t + hf + 1)
                    if hf == 0 and not (isinstance(t, int) and t == 0):
                        dve.wait_ge(hlo_ready, 2 * t)
                    nc.vector.tensor_tensor(prod_b[:, s], silu_b[:, s], ps[4 * jj + 2 + hf][:],
                                            ALU.mult).then_inc(prod_ready, 1)
                for hf in range(2):
                    s = slice(hf * HALF, (hf + 1) * HALF)
                    dve.wait_ge(hhi_ready, 2 * t + hf + 1)
                    nc.vector.tensor_tensor(hid_lo[:, jj, s], prod_b[:, s], hid_hi[:, jj, s].bitcast(F32),
                                            ALU.subtract).then_inc(hlo_ready, 1)

            def residual(f, g, last=False):
                for i in range(2 * KT):
                    hf, m = i // KT, i % KT
                    s = slice(hf * HALF, (hf + 1) * HALF)
                    if i < DOWN - 1:
                        dve.wait_ge(out_done, (DOWN - 1) * (f * GROUPS + g) + i + 1)
                    else:
                        dve.wait_ge(unit_done, unit0(f, g) + (10 if last is False else 8))
                    nc.vector.scalar_tensor_tensor(h[:, m, s], ps[4 + i % 4][:], gate_c[:, f, m:m + 1], h[:, m, s],
                                                   ALU.mult, ALU.add).then_inc(acc_done, 1)

            def ffn(f):
                if f == 0:
                    chunk(2)
                    chunk_out(2)
                    dve.wait_ge(mod_ready, 3)
                    nc.vector.tensor_scalar(gate_c[:, 0, :], mod[:, 2 * KT:3 * KT], 0.5, None, ALU.mult)
                hidden(f, 0, 0)

                def body(g, with_ada):
                    hidden(f, 2 * g - 1, 1)
                    if with_ada:
                        chunk(g + ADA_FIRST - 1)
                    residual(f, g - 1)
                    if with_ada:
                        chunk_out(g + ADA_FIRST - 1)
                    hidden(f, 2 * g, 0)
                first = 1
                if f == 0:
                    first = 1 + N_MOD - ADA_FIRST
                    with dve.Fori(1, first) as g:
                        body(g, True)
                with dve.Fori(first, GROUPS) as g:
                    body(g, False)
                if f == 0:
                    scale(1, "mix_norm")
                    scale(2, "ffn2_norm")
                    nc.vector.tensor_scalar(gate_c[:, 1, :], mod[:, 8 * KT:9 * KT], 0.5, None, ALU.mult)
                hidden(f, FT - 1, 1)
                residual(f, GROUPS - 1, last=True)

            def low_part(out_, x, hi, done):
                nc.vector.tensor_tensor(out_, x, hi.bitcast(F32), ALU.subtract).then_inc(done, 1)

            def low_scaled(out_, x, scale, hi, done):
                nc.vector.scalar_tensor_tensor(out_, x, scale, hi.bitcast(F32), ALU.mult, ALU.subtract).then_inc(done, 1)

            def mixer():
                for b in range(4):
                    dve.wait_ge(lz_ready, b + 1)
                    nc.vector.scalar_tensor_tensor(la_b[b], ps[4 + b][:], 0.0, la_b[b], ALU.min,
                                                   ALU.subtract).then_inc(la_ready, 1)
                for b in range(4):
                    dve.wait_ge(lahi_ready, b + 1)
                    low_scaled(rar[:, 2 * S + b * HALF:2 * S + (b + 1) * HALF], la_b[b], 1.0 / GLA_TAU,
                               rar[:, b * HALF:(b + 1) * HALF], lalo_ready)
                dve.wait_ge(spill, 16)
                for j in range(2):
                    dve.wait_ge(unit_done, MB + U_GK + j + 1)
                    for hf in range(2):
                        nc.vector.tensor_copy(gk[j][:, half(hf)],
                                              ps[2 * ((U_GK + j) % 2) + hf][:]).then_inc(gqk_dve, 1)
                for hd in range(GLA_H + 1):
                    if hd < GLA_H:
                        dve.wait_ge(unit_done, MB + U_GV + hd + 1)
                        if hd >= 2:
                            dve.wait_ge(v_tr, hd - 1)
                        nc.vector.tensor_copy(v_t[hd % 2][:, half(1)],
                                              ps[2 * ((U_GV + hd) % 2) + 1][:]).then_inc(vt_dve, 1)
                    if hd >= 1:
                        dve.wait_ge(v_tr, hd)
                        nc.vector.tensor_copy(gv[:, 4:8, tile(hd - 1)],
                                              ps[5 + 2 * ((hd - 1) % 2)][:].rearrange("p (t d) -> p t d", t=4)
                                              ).then_inc(gv_dve, 1)

                def diagonal(t, c):
                    nc.vector.tensor_tensor(qk[c], gq[c][:, tile(t)], gk[c][:, tile(t)],
                                            ALU.mult).then_inc(qk_ready, 1)

                def scores(t, c):
                    dve.wait_ge(score_done, CT * t + c + 1)
                    if t >= 1:
                        dve.wait_ge(o_done, t)
                    for hh in range(2):
                        s_h = st[:, tile(2 * c + hh)]
                        nc.vector.tensor_scalar(s_h, ident[:], ps[6][:, 448 + hh:449 + hh], None,
                                                ALU.mult).then_inc(chain, 1)
                    n = (2 * LEVELS + 1) * (CT * t + c)
                    for l in range(LEVELS):
                        for hh in range(2):
                            cols = slice(l * P // 2, (l + 1) * P // 2)
                            dve.wait_ge(chain, n + 2 * l + hh + 1)
                            last = nc.vector.copy_predicated(second_halves(st[:, tile(2 * c + hh)], l),
                                                             blocks(mask[:, cols], l), blocks(ps[6 + hh][:, cols], l))
                            last.then_inc(pred_ready if (l, hh) == (LEVELS - 1, 1) else chain, 1)

                def update_state(t, c):
                    dve.wait_ge(kv_done, t + 1)
                    if t == 0:
                        nc.vector.tensor_copy(state[:, c, :], ps[0][:, tile(c)]).then_inc(state_ready, 1)
                    else:
                        nc.vector.scalar_tensor_tensor(state[:, c, :], state[:, c, :], dec[:, t % 2, c:c + 1],
                                                       ps[0][:, tile(c)], ALU.mult, ALU.add).then_inc(state_ready, 1)

                def norm_a(t):
                    dve.wait_ge(grs_ready, t + 1)
                    nc.vector.tensor_tensor(ya[:, :, tile(t)], og.rearrange("p (h t) -> p h t", h=GLA_H),
                                            og_rs.rearrange("p (h t) -> p h t", h=GLA_H), ALU.mult).then_inc(ya_ready, 1)

                dve.wait_ge(gqk_act, 4)
                dve.wait_ge(gqk_dve, 4)
                def products(t, c):
                    dve.wait_ge(piece_used, piece_at["E", t, c, 2] + 1)
                    q, k = gq[c][:, tile(t)], gk[c][:, tile(t)]
                    k_products(dve, t, c, range(POOL_LEVELS, LEVELS))
                    for l in range(LEVELS):
                        e = second_halves(ed[c][:, l * P:(l + 1) * P], l)
                        dve.tensor_tensor(e, e, second_halves(q, l), ALU.mult)
                    e = ed[c][:, LEVELS * P:(LEVELS + 1) * P]
                    dve.tensor_tensor(e, e, q, ALU.mult)
                    e = ed[c][:, (LEVELS + 1) * P:EC]
                    dve.tensor_tensor(e, e, k, ALU.mult).then_inc(mult_dve, 1)

                for c in range(CT):
                    diagonal(0, c)
                    products(0, c)
                for t in range(TT):
                    for c in range(CT):
                        scores(t, c)
                        if t < TT - 1:
                            if c == CT - 1:
                                for j in range(CT):
                                    update_state(t, j)
                            diagonal(t + 1, c)
                            products(t + 1, c)
                    if t > 0:
                        norm_a(t - 1)
                    if t % 2:
                        what, hf = FIRST[t // 2]
                        lo, hi = (dk_lo, dk_hi) if what == "k" else (dq_lo, dq_hi)
                        dve.wait_ge(dqhi, t // 2 + 1)
                        nc.vector.tensor_tensor(lo[:, half(hf)], ps[1][:], hi[:, half(hf)].bitcast(F32),
                                                ALU.subtract).then_inc(dqlo, 1)
                norm_a(TT - 1)

                def maxima(hd, i):
                    if i >= 2:
                        dve.wait_ge(at_done, chunk_at["T", hd, i - 2, (i - 2) // 4] + 1)
                    elif hd > 0:
                        dve.wait_ge(at_done, chunk_at["T", hd - 1, i - 2 + TT, 1] + 1)
                    if TT * hd + i >= 2:
                        dve.wait_ge(nmx_ready, TT * hd + i - 1)
                    for cc in range(i // 4 + 1):
                        n = pair_at[hd, i, cc]
                        w = width(i, cc)
                        c0 = S - P - i * P + cc * HALF
                        dve.wait_ge(s_done, n + 1)
                        if cc == 1:
                            dve.wait_ge(max_ready, 2 * n)
                        for m in range(2):
                            nc.vector.tensor_tensor_reduce(
                                out=sc_b[i % 2][m][:, cc * HALF:cc * HALF + w], in0=ps[4 + 2 * (n % 2) + m][:, 0:w],
                                in1=bias_b[:, c0:c0 + w], scale=DIFF_DH ** -0.5 / q_scale(hd),
                                scalar=-3e38 if cc == 0 else mx[:, i % 2, 0, m:m + 1], op0=ALU.add, op1=ALU.max,
                                accum_out=mx[:, i % 2, cc, m:m + 1]).then_inc(max_ready, 1)
                    dve.wait_ge(max_ready, 2 * n + 2)
                    if TT * hd + i >= 2:
                        dve.wait_ge(exp_ready, 2 * (TT * hd + i - 1))
                    nc.vector.tensor_scalar(nmx[:, i % 2, :], mx[:, i % 2, i // 4, :], -1.0, None,
                                            ALU.mult).then_inc(nmx_ready, 1)

                def combine(hd, i):
                    n = TT * hd + i
                    dve.wait_ge(exp_ready, 2 * n + 2)
                    if n >= 2:
                        dve.wait_ge(a_ready, n - 1)
                    nc.vector.reciprocal(rec[:, i % 2, :], lsum[:, i % 2, :]).then_inc(ratio_ready, 1)
                    dve.wait_ge(ratio_ready, 2 * n + 1)
                    nc.vector.scalar_tensor_tensor(ratio[:, i % 2:i % 2 + 1], lsum[:, i % 2, 0:1], rec[:, i % 2, 1:2],
                                                   lams[:, 5:6], ALU.mult, ALU.mult).then_inc(ratio_ready, 1)
                    dve.wait_ge(ratio_ready, 2 * n + 2)
                    w = (i + 1) * P
                    nc.vector.scalar_tensor_tensor(sc_b[i % 2][0][:, 0:w], sc_b[i % 2][1][:, 0:w],
                                                   ratio[:, i % 2:i % 2 + 1], sc_b[i % 2][0][:, 0:w],
                                                   ALU.mult, ALU.add).then_inc(comb_ready, 1)

                def low_a(hd, i):
                    for cc in range(i // 4 + 1):
                        n = chunk_at["T", hd, i, cc]
                        w = width(i, cc)
                        dve.wait_ge(athi_ready, n + 1)
                        low_part(at_lo[n % 2][:, 0:w], ps[1 + ring_at["T", hd, i, cc] % 2][:, 0:w],
                                 at_hi[n % 2][:, 0:w], atlo_ready)

                def gate_r(hd, hf):
                    dve.wait_ge(r_ready, 2 * hd + hf + 1)
                    nc.vector.scalar_tensor_tensor(ya[:, hd, half(hf)], ya[:, hd, half(hf)], gains[:, 0:1], r_b,
                                                   ALU.mult, ALU.mult).then_inc(rt_ready, 1)

                def out_b(hd, i):
                    n = TT * hd + i
                    dve.wait_ge(pv_done, chunk_at["T", hd, i, i // 4] + 1)
                    if i % 4 == 0 and n >= 4:
                        dve.wait_ge(on_ready, n // 4)
                    nc.vector.tensor_copy(og[:, tile(i % 4)], ps[3][:, 0:P]).then_inc(oh_ready, 1)
                    dve.wait_ge(oh_ready, n + 1)
                    nc.vector.tensor_tensor(og[:, tile(i % 4)], og[:, tile(i % 4)], ps[3][:, P:2 * P],
                                            ALU.add).then_inc(ob_ready, 1)

                def norm_b(hd, hf):
                    n = 2 * hd + hf
                    dve.wait_ge(brs_ready, n + 1)
                    if n >= 1:
                        dve.wait_ge(on_t, n)
                    nc.vector.tensor_tensor(on.rearrange("p (t d) -> p t d", t=4), og.rearrange("p (t d) -> p t d", t=4),
                                            ssq[:].rearrange("p (t o) -> p t o", o=1).broadcast_to([P, 4, P]),
                                            ALU.mult).then_inc(on_ready, 1)

                def keep_b(hd, hf):
                    dve.wait_ge(on_t, 2 * hd + hf + 1)
                    nc.vector.tensor_scalar(yb[:, hd, half(hf)], ps[1 + ring_at["out", hd, hf] % 2][:], gains[:, 1:2],
                                            None, ALU.mult).then_inc(yb_ready, 1)

                def fill_out(hd, i):
                    what, hf = fill_of(hd, i)
                    if what == "r":
                        gate_r(hd, hf)
                    elif what in ("q", "k") and hf == 1:
                        dve.wait_ge(dqhi, 4 * (hd + 1) + (3 if what == "q" else 4))
                        if what == "q":
                            low_scaled(dq_lo[:, half(1)], ps[0][:], q_scale(hd + 1), dq_hi[:, half(1)], dqlo)
                        else:
                            low_part(dk_lo[:, half(1)], ps[0][:], dk_hi[:, half(1)], dqlo)

                def low_y(br, j):
                    dve.wait_ge(yhi_ready, 4 * br + j + 1)
                    low_part(y_lo[j], (ya if br == 0 else yb)[:, j, :], y_hi[j], ylo_ready)

                dve.wait_ge(lam_ready, 2)
                dve.wait_ge(bias_ready, 3)
                for i in range(2):
                    maxima(0, i)
                    combine(0, i)
                for hd in range(DIFF_H):
                    for i in range(TT):
                        if hd + i > 0:
                            out_b(*((hd, i - 1) if i > 0 else (hd - 1, TT - 1)))
                        low_a(hd, i)
                        if i < 2:
                            dve.wait_ge(dvhi, 2 * hd + i + 1)
                            low_part(dv[:, 4 * i:4 * i + 4, 1, :], ps[0][:].rearrange("p (t d) -> p t d", t=4),
                                     dv[:, 4 * i:4 * i + 4, 0, :], dvlo)
                        if i == 5:
                            keep_b(hd, 0)
                        if i == 1 and hd > 0:
                            keep_b(hd - 1, 1)
                        if i == 6:
                            fill_out(hd, i)
                        ahead = (hd, i + 2) if i + 2 < TT else (hd + 1, i + 2 - TT)
                        if ahead[0] < DIFF_H:
                            maxima(*ahead)
                            combine(*ahead)
                        if i == 4:
                            norm_b(hd, 0)
                        if i == 0 and hd > 0:
                            norm_b(hd - 1, 1)
                        if i != 6:
                            fill_out(hd, i)
                        if hd == DIFF_H - 1 and i >= 6:
                            low_y(0, i - 6)
                        if i == 5 and hd + 1 < DIFF_H:
                            dve.wait_ge(dqhi, 4 * (hd + 1) + 1)
                            low_scaled(dq_lo[:, half(0)], raw_b[0], q_scale(hd + 1), dq_hi[:, half(0)], dqlo)
                            dve.wait_ge(dqhi, 4 * (hd + 1) + 2)
                            low_part(dk_lo[:, half(0)], raw_b[1], dk_hi[:, half(0)], dqlo)
                out_b(DIFF_H - 1, TT - 1)
                norm_b(DIFF_H - 1, 1)
                for j in (2, 3):
                    low_y(0, j)
                keep_b(DIFF_H - 1, 1)

                def low_z(ks):
                    for k in ks:
                        for hf in range(2):
                            dve.wait_ge(zhi_ready, 2 * k + hf + 1)
                            low_part(u_lo[:, k, half(hf)], z[k][:, half(hf)], u_hi[:, k, half(hf)], zlo_ready)

                for br in range(2):
                    if br == 1:
                        for j in range(4):
                            low_y(1, j)
                    for m in range(KT):
                        if (br, m) == (1, 6):
                            low_z(range(6))
                        if m % 2 == 0:
                            dve.wait_ge(pa_done, 4 * br + m // 2 + 1)
                        else:
                            dve.wait_ge(unit_done, MB + BRANCH_UNIT["w", br, m // 2] + 1)
                        for hf in range(2):
                            n = 2 * KT * br + 2 * m + hf
                            dve.wait_ge(sig_ready, n + 1)
                            product = ps[4 - 4 * (m % 2) + hf][:]
                            if br == 0:
                                sig = z[m][:, half(hf)] if m < EARLY else sig_b[hf]
                                nc.vector.tensor_tensor(z[m][:, half(hf)], sig, product,
                                                        ALU.mult).then_inc(zz_ready, 1)
                            else:
                                nc.vector.tensor_tensor(sig_b[hf], sig_b[hf], product, ALU.mult).then_inc(gz_ready, 1)
                                dve.wait_ge(gz_ready, 2 * m + hf + 1)
                                nc.vector.tensor_tensor(z[m][:, half(hf)], z[m][:, half(hf)], sig_b[hf],
                                                        ALU.add).then_inc(zz_ready, 1)
                low_z((6, 7))
                dve.wait_ge(h_back, 16)
                for m, hf in [(m, hf) for m in range(LATE) for hf in range(2)] + [(m, 0) for m in range(LATE, KT)]:
                    out_residual(m, hf)
                out_residual(LATE, 1)

            dve.wait_ge(lam_in, 64)
            for j in range(2):
                nc.vector.tensor_tensor_reduce(out=lamj[:], in0=lamv[0:1, 2 * j, :], in1=lamv[0:1, 2 * j + 1, :],
                                               scale=1.0, scalar=0.0, op0=ALU.mult, op1=ALU.add,
                                               accum_out=lams[0:1, j:j + 1]).then_inc(lam_s, 1)
                dve.wait_ge(lam_s, j + 1)
            dve.wait_ge(lam_e, 1)
            nc.vector.tensor_tensor(lams[:, 4:5], lams[:, 3:4], lams[:, 2:3], ALU.subtract).then_inc(lam_ready, 1)
            dve.wait_ge(lam_ready, 1)
            nc.vector.tensor_scalar(lams[:, 5:6], lams[:, 4:5], -LAM_INIT, None, ALU.add).then_inc(lam_ready, 1)
            dve.wait_ge(vec_t, 1)
            nc.vector.tensor_copy(vecT[:, 0:N_ROWS], ps[7][:, 0:N_ROWS]).then_inc(vecT_ready, 1)
            dve.wait_ge(vecT_ready, 1)
            nc.vector.tensor_copy(gains[:, 0:1], fm("gla_head_norm")).then_inc(gains_ready, 1)
            nc.vector.tensor_scalar(gains[:, 1:2], fm("diff_head_norm"), 1.0 - LAM_INIT, None,
                                    ALU.mult).then_inc(gains_ready, 1)
            dve.wait_ge(gains_ready, 2)
            dve.wait_ge(c_ready, 1)
            chunk(0)
            dve.wait_ge(x_t, 2 * TT)
            chunk(1)
            chunk_out(0)
            chunk_out(1)
            scale(0, "ffn1_norm")
            norm(0)
            ffn(0)
            norm(1)
            mixer()
            norm(2)
            ffn(1)
            for hf in range(2):
                dve.wait_ge(rstd_ready, 6 + hf + 1)
                for k in range(KT):
                    s = slice(hf * HALF, (hf + 1) * HALF)
                    g0 = ROWS["final_norm"][0] + k
                    nc.vector.scalar_tensor_tensor(h[:, k, s], h[:, k, s], vecT[:, g0:g0 + 1], rstd[hf],
                                                   ALU.mult, ALU.mult).then_inc(y_ready, 1)

        @block.tensor
        def _(pe):
            def three(out_, w, x, start, stop):
                for q, (i, j) in enumerate(((0, 0), (0, 1), (1, 0))):
                    mm = nc.tensor.matmul(out_, w[i], x[j], start=(start and q == 0), stop=(stop and q == 2))
                return mm

            def mean_square(n, hf):
                pe.wait_ge(sq_used, half_added(n, hf))
                nc.tensor.matmul(ps[2 + hf][:], ones[:], rstd[hf], start=True, stop=True).then_inc(ms_done, 1)

            def first_units(norm, n):
                for hf in range(2):
                    for i in range(2):
                        pe.wait_ge(w_split, n + i + 1)
                        slot = (n + i) % SLOTS
                        for k in range(KT):
                            if i == 0:
                                j = piece(norm, hf, k)
                                pe.wait_ge(ulo_pool if k % 2 else ulo_dve, j // 2 + 1)
                            mm = three(ps[2 * i + hf][:], (w_hi[:, slot, tile(k)], w_lo[:, slot, tile(k)]),
                                       (u_hi[:, k, half(hf)], u_lo[:, k, half(hf)]), k == 0, k == KT - 1)
                            if (hf, i, k) == (0, 0, 3 * (norm - 1)):
                                mean_square(norm, 1)
                        if hf == 1:
                            mm.then_inc(unit_done, 1)

            def column_sums(m):
                pe.wait_ge(ada_used, (m + 1) * KT)
                acc, bank = sum_place(m)
                for j in range(KT):
                    mm = nc.tensor.matmul(bank[:, j:j + 1], acc[:, tile(j)], ones[:, 0:1], start=True, stop=True)
                mm.then_inc(ada_sum, 1)

            def project(n, slot, bank, first=None, made=None, midway=None):
                pe.wait_ge(w_split, n + 1)
                for k in range(KT):
                    if first is not None:
                        pe.wait_ge(made, first + 2 * k + 2)
                    if midway is not None and k == KT // 2:
                        midway()
                    c = slice(k * P, (k + 1) * P)
                    for w, u in ((w_hi, u_hi), (w_hi, u_lo), (w_lo, u_hi)):
                        for hf in range(2):
                            mm = nc.tensor.matmul(ps[bank + hf][:], w[:, slot, c], u[:, k, hf * HALF:(hf + 1) * HALF],
                                                  start=(k == 0 and u is u_hi and w is w_hi),
                                                  stop=(k == KT - 1 and w is w_lo))
                return mm

            def hidden_in(f, j, jj, n, slot, first=None):
                mm = project(n, slot % SLOTS, 4 * jj, first)
                mm.then_inc(unit_done, 1)
                if f == 0 and isinstance(j, int) and j == 1:
                    pe.wait_ge(mod_ready, 3)
                mm = project(n + 1, (slot + 1) % SLOTS, 4 * jj + 2)
                mm.then_inc(unit_done, 1)

            def down(f, g, n, slot, norm=None):
                pe.wait_ge(w_split, n + 2)
                if norm is None:
                    pe.wait_ge(hlo_ready, 2 * (f * FT + 2 * g + 2))

                def part(i, j):
                    hf, m = i // KT, i % KT
                    for q, (w, x) in enumerate(((w_hi, hid_hi), (w_hi, hid_lo), (w_lo, hid_hi))):
                        mm = nc.tensor.matmul(ps[4 + i % 4][:], w[:, (slot + j) % SLOTS, tile(m)], x[:, j, half(hf)],
                                              start=(j == 0 and q == 0), stop=(j == 1 and q == 2))
                    return mm
                if norm is not None:
                    pe.wait_ge(prod_ready, 2 * (f * FT + 2 * g + 2))
                    pe.wait_ge(hlo_ready, 2 * (f * FT + 2 * g + 1))
                    for i in range(4):
                        part(i, 0)
                    pe.wait_ge(hlo_ready, 2 * (f * FT + 2 * g + 2))
                for i in range(2 * KT):
                    if norm is not None and i == 12:
                        mean_square(norm, 0)
                    if i >= 4:
                        pe.wait_ge(acc_done, 2 * KT * (f * GROUPS + g) + i - 3)
                    for j in range(1 if norm is not None and i < 4 else 0, 2):
                        mm = part(i, j)
                    if i < DOWN - 1:
                        mm.then_inc(out_done, 1)
                mm.then_inc(unit_done, 2)

            def ffn(f):
                t0 = f * FT
                first_units(2 * f, BASE[f])
                if f == 0:
                    pe.wait_ge(mod_ready, 2)
                    column_sums(2)
                hidden_in(f, 1, 1, BASE[f] + 2, 2)

                def body(g, with_ada):
                    n = unit0(f, g)
                    pe.wait_ge(prod_ready, 2 * (t0 + 2 * g - 1))
                    hidden_in(f, 2 * g, 0, n, 1)
                    down(f, g - 1, n + 2, 0)
                    pe.wait_ge(acc_done, DOWN * (f * GROUPS + g) - 2)

                    def midway():
                        pe.wait_ge(acc_done, DOWN * (f * GROUPS + g))
                        if with_ada:
                            column_sums(g + ADA_FIRST - 1)
                    project(n + 4, 2, 4, midway=midway).then_inc(unit_done, 1)
                    if with_ada:
                        pe.wait_ge(mod_ready, g + ADA_FIRST)
                    mm = project(n + 5, 0, 6)
                    mm.then_inc(unit_done, 1)
                first = 1
                if f == 0:
                    first = 1 + N_MOD - ADA_FIRST
                    with pe.Fori(1, first) as g:
                        body(g, True)
                with pe.Fori(first, GROUPS) as g:
                    body(g, False)
                down(f, GROUPS - 1, unit0(f, GROUPS), 1, 2 * f + 1)

            def mixer():
                first_units(1, MB)
                free = [None, (low_ready, 2), (gqk_act, 2), (gqk_act, 4), (gqk_dve, 2), (gqk_dve, 4)]

                def unit(u):
                    if 2 <= u <= 6:
                        pe.wait_ge(*free[u - 1])
                    elif u > 6:
                        pe.wait_ge(vt_act, u - 6)
                        pe.wait_ge(vt_dve, u - 6)
                    project(MB + u, u % SLOTS, 2 * (u % 2)).then_inc(unit_done, 1)

                def turn_v(src, bank, gate):
                    for t in range(TT):
                        mm = nc.tensor.transpose(ps[bank + t // 4][:, tile(t % 4)], src[:, tile(t)], ident[:])
                        if gate and t % 4 == 3:
                            mm.then_inc(v_tr, 1)
                    if not gate:
                        mm.then_inc(v_tr, 1)

                pe.wait_ge(low_ready, 2)
                pe.wait_ge(w2_in, 32)
                for t in range(TT):
                    mm = nc.tensor.matmul(ps[4 + t // 2][:, (t % 2) * KW:(t % 2 + 1) * KW], low[:, tile(t)], w2b[:],
                                          start=True, stop=True)
                    if t % 2:
                        mm.then_inc(z_done, 1)
                for u in range(2, U_GV + 1):
                    unit(u)
                pe.wait_ge(la_ready, 4)
                for hd in range(GLA_H):
                    if hd + 1 < GLA_H:
                        unit(U_GV + hd + 1)
                    pe.wait_ge(vt_act, hd + 1)
                    pe.wait_ge(vt_dve, hd + 1)
                    if hd >= 2:
                        pe.wait_ge(gv_act, hd - 1)
                        pe.wait_ge(gv_dve, hd - 1)
                    turn_v(v_t[hd % 2], 4 + 2 * (hd % 2), False)
                pe.wait_ge(gv_act, GLA_H)
                pe.wait_ge(gv_dve, GLA_H)

                def free_piece(n):
                    if n >= 2:
                        pe.wait_ge(piece_used, n - 1)

                def decays(t, c):
                    for p in range(3):
                        n = piece_at["E", t, c, p]
                        free_piece(n)
                        lo, hi = p * HALF, min((p + 1) * HALF, EC)
                        for q, la in enumerate((la_hi, la_lo)):
                            mm = nc.tensor.matmul(ps[4 + n % 2][:, 0:hi - lo], la[:, t, tile(c)], cum[:, lo:hi],
                                                  start=(q == 0), stop=(q == 1))
                        mm.then_inc(piece_ready, 1)

                def scores(t, c):
                    pe.wait_ge(mult_dve, CT * t + c + 1)
                    pe.wait_ge(mult_pool, CT * t + c + 1)
                    pe.wait_ge(qk_ready, CT * t + c + 1)
                    if t + c > 0:
                        pe.wait_ge(pred_ready, CT * t + c)
                    nc.tensor.matmul(ps[6][:, 448:450], qk[c], heads2[:], start=True, stop=True)
                    for l in range(LEVELS):
                        for hh in range(2):
                            ch = slice(hh * GLA_DK, (hh + 1) * GLA_DK)
                            e = ed[c][ch, l * P:(l + 1) * P]
                            mm = nc.tensor.matmul(blocks(ps[6 + hh][:, l * P // 2:(l + 1) * P // 2], l), e,
                                                  second_halves(e, l), start=True, stop=True)
                    mm.then_inc(score_done, 1)
                    if t > 0:
                        pe.wait_ge(state_ready, CT * (t - 1) + c + 1)
                        if c == 0:
                            pe.wait_ge(og_ready, 2 * t)
                        for hh in range(2):
                            ch = slice(hh * GLA_DK, (hh + 1) * GLA_DK)
                            nc.tensor.matmul(ps[2 + hh][:, tile(c)], state[ch, c, :], ed[c][ch, LEVELS * P:(LEVELS + 1) * P],
                                             start=(c == 0), stop=False, skip_group_check=True)
                    if t < TT - 1:
                        n = piece_at["T", t, c]
                        free_piece(n)
                        nc.tensor.transpose(ps[4 + n % 2][:, 0:P], ed[c][:, (LEVELS + 1) * P:EC],
                                            ident[:]).then_inc(piece_ready, 1)

                def first_part(t, j):
                    n, part = t // 2, 2 * (t % 2) + j
                    hf = FIRST[n][1]
                    if part == 0 and n > 0:
                        pe.wait_ge(dqlo, n)
                    u = U_HEAD + n // 2
                    if part == 0:
                        pe.wait_ge(w_split, MB + u + 1)
                    for k in (2 * part, 2 * part + 1):
                        mm = three(ps[1][:], (w_hi[:, u % SLOTS, tile(k)], w_lo[:, u % SLOTS, tile(k)]),
                                   (u_hi[:, k, half(hf)], u_lo[:, k, half(hf)]), k == 0, k == KT - 1)
                    if part == 3:
                        mm.then_inc(unit_done if hf else first_done, 1)

                def sum_squares(t):
                    n = piece_at["ms", t]
                    free_piece(n)
                    pe.wait_ge(ogsq_ready, t + 1)
                    nc.tensor.matmul(ps[4 + n % 2][:], ones[:], og_sq, start=True, stop=True).then_inc(piece_ready, 1)

                pe.wait_ge(lalo_ready, 4)
                pe.wait_ge(const_ready, 6 + 6 * LEVELS + 4)
                for c in range(CT):
                    decays(0, c)
                for t in range(TT):
                    for c in range(CT):
                        scores(t, c)
                        if t < TT - 1:
                            decays(t + 1, c)
                        first_part(t, c)
                    if t < TT - 1:
                        pe.wait_ge(piece_used, piece_at["T", t, 1] + 1)
                        for c in range(CT):
                            for hh in range(2):
                                ch = slice(hh * GLA_DK, (hh + 1) * GLA_DK)
                                mm = nc.tensor.matmul(ps[0][ch, tile(c)], kd[:, c * P + hh * GLA_DK:c * P + (hh + 1) * GLA_DK],
                                                      gv[:, t, tile(2 * c + hh)], start=True, stop=True)
                        mm.then_inc(kv_done, 1)
                    if t > 0:
                        sum_squares(t - 1)
                    pe.wait_ge(pred_ready, CT * (t + 1))
                    for c in range(CT):
                        for hh in range(2):
                            mm = nc.tensor.matmul(ps[2 + hh][:, tile(c)], gv[:, t, tile(2 * c + hh)], st[:, tile(2 * c + hh)],
                                                  start=(t == 0), stop=True, skip_group_check=True)
                    mm.then_inc(o_done, 1)

                def key_scores(hd, i):
                    for cc in range(i // 4 + 1):
                        n = pair_at[hd, i, cc]
                        if n >= 2:
                            pe.wait_ge(max_ready, 2 * (n - 1))
                        wide = max(width(i, cc), 2 * P)
                        for q, (x, y) in enumerate(((dq_hi, dk_hi), (dq_hi, dk_lo), (dq_lo, dk_hi))):
                            for m in range(2):
                                ch = slice(m * DIFF_DH, (m + 1) * DIFF_DH)
                                mm = nc.tensor.matmul(ps[4 + 2 * (n % 2) + m][:, 0:wide], x[ch, tile(i)],
                                                      y[ch, cc * HALF:cc * HALF + wide], start=(q == 0), stop=(q == 2))
                        mm.then_inc(s_done, 1)

                def free_ring(n):
                    if n >= 2:
                        what = ring[n - 2]
                        if what[0] == "T":
                            pe.wait_ge(atlo_ready, chunk_at[what] + 1)
                        else:
                            pe.wait_ge(yb_ready, 2 * what[1] + what[2] + 1)

                def turn_a(hd, i):
                    pe.wait_ge(a_ready, TT * hd + i + 1)
                    for cc in range(i // 4 + 1):
                        n = ring_at["T", hd, i, cc]
                        free_ring(n)
                        for j in range(width(i, cc) // P):
                            mm = nc.tensor.transpose(ps[1 + n % 2][:, tile(j)], sc_b[i % 2][0][:, tile(4 * cc + j)], ident[:])
                        mm.then_inc(at_done, 1)

                def values(hd, i):
                    if hd + i > 0:
                        pe.wait_ge(ob_ready, TT * hd + i)
                    if i in (0, 4):
                        pe.wait_ge(dvlo, 2 * hd + i // 4 + 1)
                    for cc in range(i // 4 + 1):
                        n = chunk_at["T", hd, i, cc]
                        pe.wait_ge(atlo_ready, n + 1)
                        for j in range(width(i, cc) // P):
                            kb = 4 * cc + j
                            for q, at in enumerate((at_hi, at_lo)):
                                mm = nc.tensor.matmul(ps[3][:, 0:2 * P], at[n % 2][:, tile(j)],
                                                      dv[:, kb].rearrange("p two d -> p (two d)"),
                                                      start=(kb == 0 and q == 0), stop=(kb == i and q == 1))
                        mm.then_inc(pv_done, 1)

                def turn_out(hd, hf):
                    n = ring_at["out", hd, hf]
                    free_ring(n)
                    pe.wait_ge(on_ready, 2 * hd + hf + 1)
                    for t in range(4):
                        mm = nc.tensor.transpose(ps[1 + n % 2][:, tile(t)], on[:, tile(t)], ident[:])
                    mm.then_inc(on_t, 1)

                def turn_v_half(hd, hf):
                    if hf == 1:
                        pe.wait_ge(r_ready, 2 * hd + 1)
                    elif hd == 0:
                        pe.wait_ge(vt_act, GLA_H + 2)
                    else:
                        pe.wait_ge(dqlo, 4 * hd + 4)
                    for t in range(4):
                        mm = nc.tensor.transpose(ps[0][:, tile(t)], v_t[1][:, tile(4 * hf + t)], ident[:])
                    mm.then_inc(v_tr, 1)

                def fill(hd, i):
                    what, hf = fill_of(hd, i)
                    if i < 2:
                        pe.wait_ge(dvlo, 2 * hd + i + 1)
                    elif i == 2:
                        pe.wait_ge(r_ready, 2 * hd + 2)
                    elif what == "gate":
                        pe.wait_ge(gate_kept, i - 2)
                    elif i in (3, 4):
                        pe.wait_ge(raw_ready, 2 * hd + i - 2)
                    elif i in (5, 6):
                        pe.wait_ge(vt_act, GLA_H + 2 * (hd + 1) + i - 4)
                    else:
                        pe.wait_ge(dqlo, 4 * (hd + 1) + 3)
                    u = BRANCH_UNIT["gate", 0, i // 2 - 1] if what == "gate" else r_unit(hd) + FILL_UNIT[what]
                    if hf == 0:
                        pe.wait_ge(w_split, MB + u + 1)
                    for k in range(KT):
                        mm = three(ps[0][:], (w_hi[:, u % SLOTS, tile(k)], w_lo[:, u % SLOTS, tile(k)]),
                                   (u_hi[:, k, half(hf)], u_lo[:, k, half(hf)]), k == 0, k == KT - 1)
                    if what == "k" and hf == 1:
                        mm.then_inc(unit_done, 2)
                    elif completes(hd, i):
                        mm.then_inc(unit_done, 1)
                    else:
                        mm.then_inc(fill_done, 1)

                u = U_HEAD + 2
                pe.wait_ge(w_split, MB + u + 1)
                pe.wait_ge(state_ready, CT * (TT - 1))
                for hf in range(2):
                    for k in range(KT):
                        mm = three(ps[3 * hf][:], (w_hi[:, u % SLOTS, tile(k)], w_lo[:, u % SLOTS, tile(k)]),
                                   (u_hi[:, k, half(hf)], u_lo[:, k, half(hf)]), k == 0, k == KT - 1)
                        if (hf, k) == (1, 3):
                            pe.wait_ge(piece_used, len(pieces))
                            pe.wait_ge(dqlo, 4)
                            key_scores(0, 0)
                            key_scores(0, 1)
                    if hf == 0:
                        mm.then_inc(first_done, 1)
                        sum_squares(TT - 1)
                        pe.wait_ge(og_ready, 2 * TT)
                mm.then_inc(unit_done, 1)
                turn_v_half(0, 0)
                for hd in range(DIFF_H):
                    for i in range(TT):
                        turn_a(hd, i)
                        if i == 1 or (i == 0 and hd > 0):
                            turn_v_half(hd, i)
                        if i == 5:
                            turn_out(hd, 0)
                        if i == 1 and hd > 0:
                            turn_out(hd - 1, 1)
                        if i == 6:
                            fill(hd, i)
                        if i == 6 and hd + 1 < DIFF_H:
                            pe.wait_ge(dqlo, 4 * (hd + 1) + 2)
                        if i == 2 and hd > 0:
                            pe.wait_ge(dqlo, 4 * hd + 4)
                        ahead = (hd, i + 2) if i + 2 < TT else (hd + 1, i + 2 - TT)
                        if ahead[0] < DIFF_H:
                            key_scores(*ahead)
                        if i != 6:
                            fill(hd, i)
                        values(hd, i)
                def branch_product(br, m):
                    n = 2 * KT * br + 2 * m
                    if n >= 4:
                        pe.wait_ge(zz_ready, n - 2)
                    u = BRANCH_UNIT["w", br, m // 2]
                    if m % 2 == 0:
                        pe.wait_ge(w_split, MB + u + 1)
                    for k in range(4):
                        if m == 0:
                            pe.wait_ge(ylo_ready, 4 * br + k + 1)
                        c = slice((2 * k + m % 2) * P, (2 * k + m % 2 + 1) * P)
                        for hf in range(2):
                            mm = three(ps[4 - 4 * (m % 2) + hf][:], (w_hi[:, u % SLOTS, c], w_lo[:, u % SLOTS, c]),
                                       (y_hi[k][:, half(hf)], y_lo[k][:, half(hf)]), k == 0, k == 3)
                    mm.then_inc(pa_done if m % 2 == 0 else unit_done, 1)

                branch_product(0, 0)
                turn_out(DIFF_H - 1, 1)
                pe.wait_ge(gate_kept, 2 * EARLY)
                pe.wait_ge(yb_ready, 2 * DIFF_H)
                pe.wait_ge(ob_ready, TT * DIFF_H)
                branch_product(0, 1)
                for br in range(2):
                    for m in range(KT):
                        if (br, m) >= (0, EARLY):
                            n = 2 * KT * br + 2 * m
                            pe.wait_ge(sig_ready, n - 2)
                            u = BRANCH_UNIT["gate", br, m]
                            project(MB + u, u % SLOTS, 2 + 4 * (m % 2)).then_inc(unit_done, 1)
                        if m % 2 == 1 and (br, m) > (0, 1):
                            branch_product(br, m - 1)
                            branch_product(br, m)
                for m in range(LATE):
                    if m == 1:
                        pe.wait_ge(zz_ready, 4 * KT - 2)
                    if m == 3:
                        pe.wait_ge(zz_ready, 4 * KT)
                    if m >= 4:
                        pe.wait_ge(res_ready, 2 * (m - 3))
                    project(MB + U_OUT + m, (U_OUT + m) % SLOTS, 2 * ((m + 1) % 4), 0 if m == 0 else None,
                            zlo_ready).then_inc(unit_done, 1)
                for hf in range(2):
                    for m in range(LATE, KT):
                        slot = (U_OUT + m) % SLOTS
                        if hf == 0:
                            pe.wait_ge(res_ready, 2 * (m - 3))
                            pe.wait_ge(w_split, MB + U_OUT + m + 1)
                        for k in range(KT):
                            mm = three(ps[2 * ((m + 1) % 4) + hf][:], (w_hi[:, slot, tile(k)], w_lo[:, slot, tile(k)]),
                                       (u_hi[:, k, half(hf)], u_lo[:, k, half(hf)]), k == 0, k == KT - 1)
                        mm.then_inc(unit_done if hf else out_half, 1)
                        if (hf, m) == (1, LATE):
                            mean_square(2, 0)

            pe.wait_ge(const_ready, 4)
            pe.wait_ge(lam_s, 2)
            nc.tensor.matmul(ps[6][:, 0:2], ones[0:1, :], lams[0:1, 0:2], start=True, stop=True).then_inc(lam_ps, 1)
            pe.wait_ge(vec_in, 16 * len(ROWS))
            nc.tensor.transpose(ps[7][:, 0:N_ROWS], vec[0:N_ROWS, :], ident[0:N_ROWS, 0:N_ROWS]).then_inc(vec_t, 1)
            for i in range(2 * TT):
                t, k0 = i // 2, 4 * (i % 2)
                if i % 2 == 0:
                    pe.wait_ge(x_in[t % 3], 16 * (t // 3 + 1))
                if i >= 4:
                    pe.wait_ge(h_act, i - 3)
                for k in range(k0, k0 + 4):
                    mm = nc.tensor.transpose(ps[X_BANK[i % 4]][:, (k - k0) * P:(k - k0 + 1) * P],
                                             x_tile[t % 3][:, k * P:(k + 1) * P], ident[:])
                mm.then_inc(x_t, 1)
            mean_square(0, 0)
            column_sums(0)
            mean_square(0, 1)
            column_sums(1)
            ffn(0)
            mixer()
            ffn(1)
            mean_square(3, 1)
            for i in range(2 * TT):
                hf, kg, t = i // 8, i // 4 % 2, 4 * (i // 8) + i % 4
                if i % 4 == 0:
                    pe.wait_ge(y_ready, 8 * hf + 4 * kg + 4)
                if i >= 4:
                    pe.wait_ge(o_ready, i - 3)
                for k in range(4 * kg, 4 * kg + 4):
                    mm = nc.tensor.transpose(ps[i % 4 + 4][:, tile(k - 4 * kg)], h[:, k, tile(t)], ident[:])
                mm.then_inc(y_t, 1)


NAMES = ["x", "c", "w_ada", "b_ada", "ffn1_norm", "ffn1_w_in", "ffn1_w_out", "mix_norm", "w_in",
         "gla_alpha_w2", "gla_alpha_b", "gla_head_norm", "diff_lq1", "diff_lk1", "diff_lq2", "diff_lk2",
         "diff_head_norm", "w_branch_a", "w_branch_b", "w_out", "ffn2_norm", "ffn2_w_in", "ffn2_w_out",
         "final_norm"]


def kernel(**inputs):
    import concourse.bacc as bacc
    from concourse.bass_utils import run_bass_kernel_spmd

    nc = bacc.Bacc("TRN2", target_bir_lowering=False, num_devices=1)
    arrays, args = {}, {}
    for name in NAMES:
        arr = np.ascontiguousarray(inputs[name])
        arrays[f"in_{name}"] = arr
        args[name] = nc.dram_tensor(f"in_{name}", arr.shape, mybir.dt.from_np(arr.dtype), kind="ExternalInput").ap()
    out = nc.dram_tensor("out_h", (1, S, D), F32, kind="ExternalOutput").ap()
    build_program(nc, args, out)
    result = run_bass_kernel_spmd(nc, [arrays], core_ids=[0])
    return result.results[0]["out_h"]
```
